# Optimizing a Trainium2 kernel written in Bass

```python
import jax, jax.numpy as jnp
from jax import lax
import numpy as np
import math

D_MODEL = 1024
BATCH = 1
SEQ = 512
DEPTH = 1

D_MIX = D_MODEL
CONV_CH = D_MIX // 2
CONV_WIDTH = 31
FOX_HEADS = 8
FOX_HEAD_DIM = 64
FOX_WIDTH = FOX_HEADS * FOX_HEAD_DIM
Q_BLOCK = 128
N_MEM = 256
MEM_HEADS = 4
MEM_HEAD_DIM = 128
MEM_INNER = MEM_HEADS * MEM_HEAD_DIM
D_FF = 4 * D_MODEL
EPS = 1e-6
NEG_INF = -1e30
IN_COLS = 2 * CONV_CH + 3 * FOX_WIDTH + FOX_HEADS


def rms_norm(x, g):
    xf = x.astype(jnp.float32)
    y = xf * lax.rsqrt(jnp.mean(xf * xf, axis=-1, keepdims=True) + EPS)
    return (y * g.astype(jnp.float32)).astype(x.dtype)

def layer_norm(x, g, b):
    xf = x.astype(jnp.float32)
    mu = jnp.mean(xf, axis=-1, keepdims=True)
    xc = xf - mu
    y = xc * lax.rsqrt(jnp.mean(xc * xc, axis=-1, keepdims=True) + EPS)
    return (y * g.astype(jnp.float32) + b.astype(jnp.float32)).astype(x.dtype)

def causal_depthwise_conv(u, w, b):
    out = lax.conv_general_dilated(
        u, w[:, None, :], window_strides=(1,), padding=[(CONV_WIDTH - 1, 0)],
        dimension_numbers=("NWC", "WIO", "NWC"), feature_group_count=u.shape[-1])
    return out + b

def forgetting_attention(q, k, v, log_f):
    S = q.shape[1]
    dh = q.shape[-1]
    scale = dh ** -0.5
    cum = jnp.cumsum(log_f, axis=1).transpose(0, 2, 1)
    outs = []
    for i in range(S // Q_BLOCK):
        q0 = i * Q_BLOCK
        kl = q0 + Q_BLOCK
        qb = q[:, q0:kl]
        kb = k[:, :kl]
        vb = v[:, :kl]
        logits = jnp.einsum("bqhd,bkhd->bhqk", qb, kb,
                            preferred_element_type=jnp.float32) * scale
        logits = logits + cum[:, :, q0:kl, None] - cum[:, :, None, :kl]
        q_pos = q0 + jnp.arange(Q_BLOCK)
        k_pos = jnp.arange(kl)
        mask = k_pos[None, :] <= q_pos[:, None]
        p = jax.nn.softmax(jnp.where(mask, logits, NEG_INF), axis=-1)
        outs.append(jnp.einsum("bhqk,bkhd->bqhd", p.astype(vb.dtype), vb))
    return jnp.concatenate(outs, axis=1)

def hybrid_mixer(h, w_in, b_forget, conv_w, conv_b, conv_ln_g, conv_ln_b, w_out):
    B, S, _ = h.shape
    z = h @ w_in
    o = 0
    a = z[..., o:o + CONV_CH]; o += CONV_CH
    g = z[..., o:o + CONV_CH]; o += CONV_CH
    q = z[..., o:o + FOX_WIDTH]; o += FOX_WIDTH
    k = z[..., o:o + FOX_WIDTH]; o += FOX_WIDTH
    v = z[..., o:o + FOX_WIDTH]; o += FOX_WIDTH
    f_logit = z[..., o:o + FOX_HEADS]

    u = a * jax.nn.sigmoid(g)
    u = causal_depthwise_conv(u, conv_w, conv_b)
    u = jax.nn.silu(layer_norm(u, conv_ln_g, conv_ln_b))

    log_f = jax.nn.log_sigmoid((f_logit + b_forget).astype(jnp.float32))
    shp = (B, S, FOX_HEADS, FOX_HEAD_DIM)
    att = forgetting_attention(q.reshape(shp), k.reshape(shp), v.reshape(shp), log_f)
    att = att.reshape(B, S, FOX_WIDTH)

    return jnp.concatenate([u, att], axis=-1) @ w_out

def memory_cross_attention(h, mem_n, w_mq, w_mk, w_mv, w_mo):
    B, S, _ = h.shape
    q = (h @ w_mq).reshape(B, S, MEM_HEADS, MEM_HEAD_DIM)
    k = (mem_n @ w_mk).reshape(B, N_MEM, MEM_HEADS, MEM_HEAD_DIM)
    v = (mem_n @ w_mv).reshape(B, N_MEM, MEM_HEADS, MEM_HEAD_DIM)
    logits = jnp.einsum("bqhd,bmhd->bhqm", q, k,
                        preferred_element_type=jnp.float32) * (MEM_HEAD_DIM ** -0.5)
    p = jax.nn.softmax(logits, axis=-1)
    out = jnp.einsum("bhqm,bmhd->bqhd", p.astype(v.dtype), v).reshape(B, S, MEM_INNER)
    return out @ w_mo

def squared_relu_mlp(h, w_up, w_down):
    return jnp.square(jax.nn.relu(h @ w_up)) @ w_down

def first_inputs(seed: int = 0) -> dict:
    key = jax.random.key(seed)
    ks = jax.random.split(key, 24)
    nrm = lambda k, shape, fan_in: jax.random.normal(k, shape, jnp.float32) * (fan_in ** -0.5)
    gain = lambda k, shape: 1.0 + 0.05 * jax.random.normal(k, shape, jnp.float32)
    small = lambda k, shape: 0.02 * jax.random.normal(k, shape, jnp.float32)
    L = DEPTH
    return {
        "x": jax.random.normal(ks[0], (BATCH, SEQ, D_MODEL), jnp.float32),
        "mem": jax.random.normal(ks[1], (BATCH, N_MEM, D_MODEL), jnp.float32),
        "norm_mix_pre": gain(ks[2], (L, D_MODEL)),
        "norm_mix_post": gain(ks[3], (L, D_MODEL)),
        "w_in": nrm(ks[4], (L, D_MODEL, IN_COLS), D_MODEL),
        "b_forget": jax.random.uniform(ks[5], (L, FOX_HEADS), jnp.float32, 1.0, 5.0),
        "conv_w": nrm(ks[6], (L, CONV_WIDTH, CONV_CH), CONV_WIDTH),
        "conv_b": small(ks[7], (L, CONV_CH)),
        "conv_ln_g": gain(ks[8], (L, CONV_CH)),
        "conv_ln_b": small(ks[9], (L, CONV_CH)),
        "w_out": nrm(ks[10], (L, D_MIX, D_MODEL), D_MIX),
        "norm_mem_pre": gain(ks[11], (L, D_MODEL)),
        "norm_mem_post": gain(ks[12], (L, D_MODEL)),
        "norm_memkv": gain(ks[13], (L, D_MODEL)),
        "w_mq": nrm(ks[14], (L, D_MODEL, MEM_INNER), D_MODEL),
        "w_mk": nrm(ks[15], (L, D_MODEL, MEM_INNER), D_MODEL),
        "w_mv": nrm(ks[16], (L, D_MODEL, MEM_INNER), D_MODEL),
        "w_mo": nrm(ks[17], (L, MEM_INNER, D_MODEL), MEM_INNER),
        "norm_mlp_pre": gain(ks[18], (L, D_MODEL)),
        "norm_mlp_post": gain(ks[19], (L, D_MODEL)),
        "w_up": nrm(ks[20], (L, D_MODEL, D_FF), D_MODEL),
        "w_down": nrm(ks[21], (L, D_FF, D_MODEL), D_FF),
    }

def first_block(x, mem, norm_mix_pre, norm_mix_post, w_in, b_forget, conv_w, conv_b,
              conv_ln_g, conv_ln_b, w_out, norm_mem_pre, norm_mem_post, norm_memkv,
              w_mq, w_mk, w_mv, w_mo, norm_mlp_pre, norm_mlp_post, w_up, w_down):
    for l in range(DEPTH):
        h = rms_norm(x, norm_mix_pre[l])
        y = hybrid_mixer(h, w_in[l], b_forget[l], conv_w[l], conv_b[l],
                         conv_ln_g[l], conv_ln_b[l], w_out[l])
        x = x + rms_norm(y, norm_mix_post[l])
        h = rms_norm(x, norm_mem_pre[l])
        mem_n = rms_norm(mem, norm_memkv[l])
        y = memory_cross_attention(h, mem_n, w_mq[l], w_mk[l], w_mv[l], w_mo[l])
        x = x + rms_norm(y, norm_mem_post[l])
        h = rms_norm(x, norm_mlp_pre[l])
        y = squared_relu_mlp(h, w_up[l], w_down[l])
        x = x + rms_norm(y, norm_mlp_post[l])
    return x


DEPTH_2 = 2

N_MIXERS = 2
N_MLA_LAYERS = (DEPTH_2 + 1) // N_MIXERS
N_HYENA_LAYERS = DEPTH_2 // N_MIXERS

MLA_HEADS = 8
QK_NOPE_DIM = 128
QK_ROPE_DIM = 64
V_HEAD_DIM = 128
Q_LORA_RANK = 384
KV_LORA_RANK = 256
MLA_IN_DIM = Q_LORA_RANK + KV_LORA_RANK + QK_ROPE_DIM
ROPE_THETA = 10000.0

HYENA_ORDER = 2
HYENA_EMB_DIM = 33
HYENA_FILTER_WIDTH = 64
HYENA_FAST_DECAY = 0.3
HYENA_SLOW_DECAY = 1.5
HYENA_TARGET = 1e-2
SHORT_CONV_WIDTH = 3

D_FF_2 = 2816
FFN_CONV_WIDTH = 3

NORM_EPS = 1e-5
RMS_EPS = 1e-6
DEEPNORM_ALPHA = (2.0 * DEPTH_2) ** 0.25
DEEPNORM_BETA = (8.0 * DEPTH_2) ** -0.25


def layer_norm_2(x, g, b):
    xf = x.astype(jnp.float32)
    mu = jnp.mean(xf, -1, keepdims=True)
    var = jnp.mean(jnp.square(xf - mu), -1, keepdims=True)
    return ((xf - mu) * lax.rsqrt(var + NORM_EPS) * g.astype(jnp.float32) + b.astype(jnp.float32)).astype(x.dtype)

def rms_norm_2(x, g):
    xf = x.astype(jnp.float32)
    ms = jnp.mean(jnp.square(xf), -1, keepdims=True)
    return (xf * lax.rsqrt(ms + RMS_EPS) * g.astype(jnp.float32)).astype(x.dtype)

def dwconv_centred(x, w):
    k_width = w.shape[0]
    pad = k_width // 2
    s = x.shape[1]
    xp = jnp.pad(x, ((0, 0), (pad, pad), (0, 0)))
    return sum(xp[:, k:k + s] * w[k] for k in range(k_width))

def rope_tables(positions):
    inv = 1.0 / (ROPE_THETA ** (jnp.arange(0, QK_ROPE_DIM, 2, dtype=jnp.float32) / QK_ROPE_DIM))
    ang = positions.astype(jnp.float32)[..., None] * inv
    return jnp.cos(ang), jnp.sin(ang)

def apply_rope(x, cos, sin):
    x1, x2 = jnp.split(x.astype(jnp.float32), 2, axis=-1)
    return jnp.concatenate([x1 * cos - x2 * sin, x1 * sin + x2 * cos], -1).astype(x.dtype)

def mla_mixer(x, cos, sin, w_in, g_q, w_uq, g_kv, w_ukv, w_o):
    b, s, _ = x.shape
    h = x @ w_in
    c_q, c_kv, k_rope = jnp.split(h, [Q_LORA_RANK, Q_LORA_RANK + KV_LORA_RANK], axis=-1)
    q = (rms_norm_2(c_q, g_q) @ w_uq).reshape(b, s, MLA_HEADS, QK_NOPE_DIM + QK_ROPE_DIM)
    q_nope = q[..., :QK_NOPE_DIM]
    q_rope = apply_rope(q[..., QK_NOPE_DIM:], cos[:, :, None], sin[:, :, None])
    k_rope = apply_rope(k_rope, cos, sin)
    kv = (rms_norm_2(c_kv, g_kv) @ w_ukv).reshape(b, s, MLA_HEADS, QK_NOPE_DIM + V_HEAD_DIM)
    k_nope, v = kv[..., :QK_NOPE_DIM], kv[..., QK_NOPE_DIM:]
    scale = (QK_NOPE_DIM + QK_ROPE_DIM) ** -0.5
    nb = s // Q_BLOCK
    qn_blocks = q_nope.reshape(b, nb, Q_BLOCK, MLA_HEADS, QK_NOPE_DIM).transpose(1, 0, 2, 3, 4)
    qr_blocks = q_rope.reshape(b, nb, Q_BLOCK, MLA_HEADS, QK_ROPE_DIM).transpose(1, 0, 2, 3, 4)

    def attend(blk):
        qn, qr = blk
        sc = (jnp.einsum('bqhd,bkhd->bhqk', qn, k_nope)
              + jnp.einsum('bqhr,bkr->bhqk', qr, k_rope))
        p = jax.nn.softmax(sc.astype(jnp.float32) * scale, axis=-1).astype(v.dtype)
        return jnp.einsum('bhqk,bkhd->bqhd', p, v)

    o = lax.map(attend, (qn_blocks, qr_blocks))
    o = o.transpose(1, 0, 2, 3, 4).reshape(b, s, MLA_HEADS * V_HEAD_DIM)
    return o @ w_o

def hyena_positional_features(length):
    t = jnp.linspace(0.0, 1.0, length, dtype=jnp.float32)[:, None]
    bands = (HYENA_EMB_DIM - 1) // 2
    w = 2.0 * math.pi * jnp.arange(length, dtype=jnp.float32)[:, None] / length
    f = jnp.linspace(1e-4, bands - 1, bands, dtype=jnp.float32)[None, :]
    z = jnp.concatenate([t, jnp.cos(f * w), -jnp.sin(f * w)], axis=-1)
    return t, z

def hyena_filters(length, fw1, fb1, fw2, fb2, fw3, fb3, freq, fw_out):
    t, z = hyena_positional_features(length)
    freq = freq.astype(jnp.float32)
    h = jnp.sin(freq * (z @ fw1.astype(jnp.float32) + fb1.astype(jnp.float32)))
    h = jnp.sin(freq * (h @ fw2.astype(jnp.float32) + fb2.astype(jnp.float32)))
    h = jnp.sin(freq * (h @ fw3.astype(jnp.float32) + fb3.astype(jnp.float32)))
    h = h @ fw_out.astype(jnp.float32)
    deltas = jnp.abs(jnp.linspace(math.log(HYENA_FAST_DECAY) / HYENA_TARGET,
                                  math.log(HYENA_SLOW_DECAY) / HYENA_TARGET,
                                  D_MODEL, dtype=jnp.float32))
    decay = jnp.exp(-t * deltas)
    return h.reshape(length, HYENA_ORDER, 2, D_MODEL) * decay[:, None, None, :]

def two_sided_kernel(h_fwd, h_bwd):
    zero = jnp.zeros_like(h_fwd[:1])
    return jnp.concatenate([h_fwd.at[0].add(h_bwd[0]), zero, h_bwd[:0:-1]], axis=0)

def hyena_mixer(x, w_in, w_short, fw1, fb1, fw2, fb2, fw3, fb3, freq, fw_out, d_bias, w_o):
    b, length, _ = x.shape
    u = dwconv_centred(x @ w_in, w_short)
    v, g1, g2 = jnp.split(u, 3, axis=-1)
    filt = hyena_filters(length, fw1, fb1, fw2, fb2, fw3, fb3, freq, fw_out)
    n = 2 * length
    z = v.astype(jnp.float32)
    for o, gate in enumerate((g1, g2)):
        k_f = jnp.fft.rfft(two_sided_kernel(filt[:, o, 0], filt[:, o, 1]), n=n, axis=0)
        z_f = jnp.fft.rfft(z, n=n, axis=1)
        y = jnp.fft.irfft(z_f * k_f, n=n, axis=1)[:, :length]
        z = gate.astype(jnp.float32) * (y + d_bias[o].astype(jnp.float32) * z)
    return z.astype(x.dtype) @ w_o

def conv_ffn(x, w_up, w_conv, w_down):
    h = dwconv_centred(x @ w_up, w_conv)
    a, g = jnp.split(h, 2, axis=-1)
    return (jax.nn.silu(g) * a) @ w_down

def second_inputs(seed: int = 0) -> dict:
    key = jax.random.key(seed)
    ks = iter(jax.random.split(key, 40))

    def nrm(shape, scale):
        return jax.random.normal(next(ks), shape, jnp.float32) * scale

    def gain(shape):
        return 1.0 + nrm(shape, 0.01)

    nm, nh = N_MLA_LAYERS, N_HYENA_LAYERS
    hf = HYENA_FILTER_WIDTH
    return {
        "x": nrm((BATCH, SEQ, D_MODEL), 1.0),
        "positions": jnp.broadcast_to(jnp.arange(SEQ, dtype=jnp.int32), (BATCH, SEQ)),
        "mla_w_in": nrm((nm, D_MODEL, MLA_IN_DIM), D_MODEL ** -0.5),
        "mla_g_q": gain((nm, Q_LORA_RANK)),
        "mla_w_uq": nrm((nm, Q_LORA_RANK, MLA_HEADS * (QK_NOPE_DIM + QK_ROPE_DIM)), Q_LORA_RANK ** -0.5),
        "mla_g_kv": gain((nm, KV_LORA_RANK)),
        "mla_w_ukv": nrm((nm, KV_LORA_RANK, MLA_HEADS * (QK_NOPE_DIM + V_HEAD_DIM)), KV_LORA_RANK ** -0.5),
        "mla_w_o": nrm((nm, MLA_HEADS * V_HEAD_DIM, D_MODEL), (MLA_HEADS * V_HEAD_DIM) ** -0.5 * DEEPNORM_BETA),
        "hy_w_in": nrm((nh, D_MODEL, 3 * D_MODEL), D_MODEL ** -0.5),
        "hy_w_short": nrm((nh, SHORT_CONV_WIDTH, 3 * D_MODEL), SHORT_CONV_WIDTH ** -0.5),
        "hy_fw1": nrm((nh, HYENA_EMB_DIM, hf), HYENA_EMB_DIM ** -0.5),
        "hy_fb1": nrm((nh, hf), 0.02),
        "hy_fw2": nrm((nh, hf, hf), hf ** -0.5),
        "hy_fb2": nrm((nh, hf), 0.02),
        "hy_fw3": nrm((nh, hf, hf), hf ** -0.5),
        "hy_fb3": nrm((nh, hf), 0.02),
        "hy_freq": gain((nh, hf)),
        "hy_fw_out": nrm((nh, hf, HYENA_ORDER * 2 * D_MODEL), hf ** -0.5),
        "hy_d_bias": nrm((nh, HYENA_ORDER, D_MODEL), 0.1),
        "hy_w_o": nrm((nh, D_MODEL, D_MODEL), D_MODEL ** -0.5 * DEEPNORM_BETA),
        "ffn_w_up": nrm((DEPTH_2, D_MODEL, 2 * D_FF_2), D_MODEL ** -0.5),
        "ffn_w_conv": nrm((DEPTH_2, FFN_CONV_WIDTH, 2 * D_FF_2), FFN_CONV_WIDTH ** -0.5),
        "ffn_w_down": nrm((DEPTH_2, D_FF_2, D_MODEL), D_FF_2 ** -0.5 * DEEPNORM_BETA),
        "ln1_g": gain((DEPTH_2, D_MODEL)),
        "ln1_b": nrm((DEPTH_2, D_MODEL), 0.01),
        "ln2_g": gain((DEPTH_2, D_MODEL)),
        "ln2_b": nrm((DEPTH_2, D_MODEL), 0.01),
    }

def second_block(x, positions, mla_w_in, mla_g_q, mla_w_uq, mla_g_kv, mla_w_ukv, mla_w_o,
              hy_w_in, hy_w_short, hy_fw1, hy_fb1, hy_fw2, hy_fb2, hy_fw3, hy_fb3, hy_freq,
              hy_fw_out, hy_d_bias, hy_w_o, ffn_w_up, ffn_w_conv, ffn_w_down,
              ln1_g, ln1_b, ln2_g, ln2_b):
    cos, sin = rope_tables(positions)
    for i in range(DEPTH_2):
        j = i // N_MIXERS
        if i % N_MIXERS == 0:
            m = mla_mixer(x, cos, sin, mla_w_in[j], mla_g_q[j], mla_w_uq[j],
                          mla_g_kv[j], mla_w_ukv[j], mla_w_o[j])
        else:
            m = hyena_mixer(x, hy_w_in[j], hy_w_short[j], hy_fw1[j], hy_fb1[j], hy_fw2[j],
                            hy_fb2[j], hy_fw3[j], hy_fb3[j], hy_freq[j], hy_fw_out[j],
                            hy_d_bias[j], hy_w_o[j])
        x = layer_norm_2(DEEPNORM_ALPHA * x + m, ln1_g[i], ln1_b[i])
        x = layer_norm_2(DEEPNORM_ALPHA * x + conv_ffn(x, ffn_w_up[i], ffn_w_conv[i], ffn_w_down[i]),
                       ln2_g[i], ln2_b[i])
    return x


def setup_inputs(seed=0):
    out = dict(first_inputs(seed))
    for name, value in second_inputs(seed + 1).items():
        if name != "x":
            out[name + "_2"] = value
    return out


def reference(
    x, mem, norm_mix_pre, norm_mix_post, w_in, b_forget, conv_w, conv_b, conv_ln_g, conv_ln_b,
    w_out, norm_mem_pre, norm_mem_post, norm_memkv, w_mq, w_mk, w_mv, w_mo, norm_mlp_pre,
    norm_mlp_post, w_up, w_down, positions_2, mla_w_in_2, mla_g_q_2, mla_w_uq_2, mla_g_kv_2,
    mla_w_ukv_2, mla_w_o_2, hy_w_in_2, hy_w_short_2, hy_fw1_2, hy_fb1_2, hy_fw2_2, hy_fb2_2,
    hy_fw3_2, hy_fb3_2, hy_freq_2, hy_fw_out_2, hy_d_bias_2, hy_w_o_2, ffn_w_up_2, ffn_w_conv_2,
    ffn_w_down_2, ln1_g_2, ln1_b_2, ln2_g_2, ln2_b_2,
):
    x = first_block(
        x, mem, norm_mix_pre, norm_mix_post, w_in, b_forget, conv_w, conv_b, conv_ln_g,
        conv_ln_b, w_out, norm_mem_pre, norm_mem_post, norm_memkv, w_mq, w_mk, w_mv, w_mo,
        norm_mlp_pre, norm_mlp_post, w_up, w_down,
    )
    return second_block(
        x, positions_2, mla_w_in_2, mla_g_q_2, mla_w_uq_2, mla_g_kv_2, mla_w_ukv_2, mla_w_o_2,
        hy_w_in_2, hy_w_short_2, hy_fw1_2, hy_fb1_2, hy_fw2_2, hy_fb2_2, hy_fw3_2, hy_fb3_2,
        hy_freq_2, hy_fw_out_2, hy_d_bias_2, hy_w_o_2, ffn_w_up_2, ffn_w_conv_2, ffn_w_down_2,
        ln1_g_2, ln1_b_2, ln2_g_2, ln2_b_2,
    )


_drawn_inputs = setup_inputs


def setup_inputs(seed=0):
    import zlib

    import numpy as np

    out = dict(_drawn_inputs(seed))
    spreads = {}
    factors = {'mla_g_q_2': 8.0,
     'mla_g_kv_2': 8.0,
     'hy_freq_2': 4.566,
     'hy_d_bias_2': 4.884,
     'ln1_b_2': 2.675}
    for name, (base, spread) in spreads.items():
        noise = np.random.default_rng([zlib.crc32(name.encode()), seed]).standard_normal(out[name].shape)
        drawn = base * np.exp(spread * noise) if base else spread * noise
        out[name] = __import__('jax').numpy.asarray(drawn.astype(out[name].dtype))
    for name, factor in factors.items():
        out[name] = (out[name] * factor).astype(out[name].dtype)
    return out
```

```python
from contextlib import ExitStack

import numpy as np

import concourse.bass as bass
from concourse import mybir

F = mybir.dt.float32
R = mybir.dt.float32r
I32 = mybir.dt.int32
ALU = mybir.AluOpType
ACT = mybir.ActivationFunctionType
AX = mybir.AxisListType.X

S = 512
D = 1024
ALPHA = float(np.float32((2.0 * 2) ** 0.25))
MAGIC = 12582912.0
TWO_PI = 6.283185307179586
C1 = 6.28125
C2 = 0.0019350051879882812
C3 = TWO_PI - C1 - C2
PI_IN = 3.1415925
HALF_PI = 1.5707963267948966


def tokens(waits):
    out = []
    for w in waits:
        if isinstance(w, list) or (isinstance(w, tuple) and not isinstance(w[-1], int)):
            out += tokens(w)
        elif w is not None:
            out.append(w)
    return out


class Engine:

    def __init__(self, sem):
        self.sem, self.count, self.ops = sem, 0, []

    def do(self, make, *waits, inc=True):
        self.ops.append([make, tokens(waits), False])
        return self.mark() if inc else None

    def mark(self):
        if not self.ops[-1][2]:
            self.ops[-1][2] = True
            self.count += 1
        return (self.sem, self.count)

    def issue(self, eng):
        seen = {}

        for make, waits, inc in self.ops:
            for sem, value in waits:
                if seen.get(id(sem), 0) < value:
                    eng.wait_ge(sem, value)
                    seen[id(sem)] = value
            ins = make(eng)
            if inc is True:
                ins.then_inc(self.sem, 1)


class Channel:

    def __init__(self, sem):
        self.sem, self.count = sem, 0


PCOLS = [("g_mix_pre", 8), ("g_mix_post", 8), ("g_mem_pre", 8), ("g_mem_post", 8), ("g_memkv", 8),
         ("g_mlp_pre", 8), ("g_mlp_post", 8), ("conv_w", 124), ("conv_b", 4), ("cln_g", 4), ("cln_b", 4),
         ("g_q", 3), ("g_kv", 2), ("w_short", 72), ("d_bias", 16), ("ffn_conv0", 132), ("ffn_conv1", 132),
         ("ln1_g0", 8), ("ln1_b0", 8), ("ln2_g0", 8), ("ln2_b0", 8),
         ("ln1_g1", 8), ("ln1_b1", 8), ("ln2_g1", 8), ("ln2_b1", 8), ("b_forget", 8),
         ("inv", 1), ("sgn", 1), ("one", 1), ("eps6", 1), ("eps5", 1), ("halfpi", 1)]
POFF, _at = {}, 0
for _n, _w in PCOLS:
    POFF[_n] = _at
    _at += _w
NPC = _at

CHUNKS = [
    ("dft_k", 0, 1024), ("dft_kx", 0, 512), ("dft_k", 1, 1024), ("dft_k", 2, 1024), ("dft_k", 3, 1024),
    ("dft_k", 0, 1024), ("dft_kx", 0, 512), ("dft_k", 1, 1024), ("dft_k", 2, 1024), ("dft_k", 3, 1024),
    *[("win_ag", i, 2048) for i in range(4)], ("win_f", 0, 64), *[("win_v", i, 2048) for i in range(2)],
    *[("win_qk", i, 2048) for i in range(4)],
    *[("w_out", i, 2048) for i in range(4)],
    *[("w_mk", i, 2048) for i in range(2)], *[("w_mv", i, 2048) for i in range(2)],
    *[("w_mq", i, 2048) for i in range(2)], *[("w_mo", i, 2048) for i in range(2)],
    *[("w_up", i, 2048) for i in range(16)], *[("w_down", i, 2048) for i in range(16)],
    *[("mla_in", i, 2048) for i in range(3)], ("mla_inx", 0, 1024),
]
for _p in range(4):
    CHUNKS += [("uq", _p, 1536), ("ukv", _p, 1024)]
CHUNKS += [("mla_o", i, 2048) for i in range(4)]
CHUNKS += [("up2_0", i, 2048) for i in range(22)] + [("down2_0", i, 2048) for i in range(11)]
CHUNKS += [("hy_in", i, 2048) for i in range(12)]
for _o in range(2):
    CHUNKS += [("dft_z", i, 1024) for i in range(4)] + [("dft_i", i, 2048) for i in range(2)]
CHUNKS += [("hy_o", i, 2048) for i in range(4)]
CHUNKS += [("up2_1", i, 2048) for i in range(22)] + [("down2_1", i, 2048) for i in range(11)]


def build(nc, t):
    es = ExitStack()
    BASE = 16512

    def sb(name, kb, shape, dt=F):
        return nc.alloc_sbuf_tensor_at(name, shape, dt, offset=BASE + int(kb * 1024))

    def sem(name):
        return es.enter_context(nc.semaphore(name))

    def chan(name):
        return Channel(sem(name))

    with es:
        psum = [es.enter_context(nc.psum_tensor(f"ps{i}", [128, 512], F)) for i in range(8)]
        pe, act, dve, pool, sp = (Engine(sem(n)) for n in ("s_pe", "s_act", "s_dve", "s_pool", "s_sp"))

        def dma(q, ch, dst, src, *waits):
            ch.count += 16
            sm = ch.sem
            q.ops.append([lambda e: e.dma_start(dst, src).then_inc(sm, 16), tokens(waits), None])
            return (ch.sem, ch.count)

        X = sb("X", 0, [128, 8, 512])
        W32 = [sb(f"W32_{i}", 16 + 8 * i, [128, 2048]) for i in range(3)]
        WH = [sb(f"WH{i}", 40 + 8 * i, [128, 2048], R) for i in range(2)]
        WL = [sb(f"WL{i}", 56 + 8 * i, [128, 2048], R) for i in range(2)]
        PAR = sb("PAR", 72, [128, NPC])
        IDT = sb("IDT", 75, [128, 128])
        ONE = sb("ONE", 75.5, [128, 128])
        IDR = sb("IDR", 76, [128, 128], R)
        MKR = sb("MKR", 76.5, [128, 128], R)
        SM = sb("SM", 77, [128, 256])
        TMP = [sb(f"TMP{i}", 78 + 2 * i, [128, 512]) for i in range(6)]
        A = 90

        ch_w = [chan(f"c_w{i}") for i in range(3)]
        ch_t = [chan(f"c_t{i}") for i in range(6)]
        ch_m = {}

        def once(name):
            ch_m[name] = chan("c_" + name)
            return ch_m[name]

        stores = []

        free = [[] for _ in range(8)]
        turn = [0]

        def bank():
            i = turn[0] % 8
            turn[0] += 1
            return i, psum[i], free[i]

        wst = {"dma": 0, "split": 0, "get": 0}
        w_split = []
        w_used = []

        def w_dma():
            n = wst["dma"]
            if n >= len(CHUNKS):
                return
            name, i, cols = CHUNKS[n]
            s = n % 3
            wst["dma"] += 1
            w_split.append([dma(sp, ch_w[s], W32[s][:, 0:cols], t[name][i], w_split[n - 3] if n >= 3 else None)])

        def w_do_split():
            n = wst["split"]
            if n >= len(CHUNKS):
                return
            cols = CHUNKS[n][2]
            s, r = n % 3, n % 2
            landed = w_split[n][0]
            used = w_used[n - 2] if n >= 2 else None
            src, hi, lo = W32[s][:, 0:cols], WH[r][:, 0:cols], WL[r][:, 0:cols]
            a = act.do(lambda e: e.activation(hi, src, ACT.Copy), landed, used)
            b = pool.do(lambda e: e.tensor_tensor(lo, src, hi.bitcast(F), ALU.subtract), landed, used, a)
            w_split[n] = [a, b]
            wst["split"] += 1
            w_dma()

        def w_get(name):
            n = wst["get"]
            assert CHUNKS[n][0] == name, (CHUNKS[n], name)
            if wst["split"] <= n:
                w_do_split()
            if wst["split"] <= n + 1:
                w_do_split()
            wst["get"] += 1
            r = n % 2
            return WH[r], WL[r], w_split[n]

        def w_release():
            w_used.append(pe.mark())

        def mm(out, l, r, start, stop, *waits):
            pe.do(lambda e: e.matmul(out, l, r, start=start, stop=stop), *waits, inc=False)

        def mm3(out, lh, ll, rh, rl, first, last, *waits):
            mm(out, ll, rh, first, False, *waits)
            mm(out, lh, rl, False, False)
            mm(out, lh, rh, False, last)

        def cp(out, src, *w, scale=1.0):
            return act.do(lambda e: e.activation(out, src, ACT.Copy, scale=scale), *w)

        def tt(out, a, b, op, *w):
            return dve.do(lambda e: e.tensor_tensor(out, a, b, op), *w)

        def ts(out, a, s1, s2, o1, o2, *w):
            if s2 is None:
                return dve.do(lambda e: e.tensor_scalar(out, a, s1, None, o1), *w)
            return dve.do(lambda e: e.tensor_scalar(out, a, s1, s2, o1, o2), *w)

        def stt(out, a, s, b, o1, o2, *w):
            return dve.do(lambda e: e.scalar_tensor_tensor(out=out, in0=a, scalar=s, in1=b, op0=o1, op1=o2), *w)

        def af(out, src, fn, *w, scale=1.0, bias=0.0):
            return act.do(lambda e: e.activation(out, src, fn, scale=scale, bias=bias), *w)

        def split(src, hi, lo, *w, scale=None):
            a = cp(hi, src, *w, scale=1.0 if scale is None else scale)
            if scale is None:
                b = tt(lo, src, hi.bitcast(F), ALU.subtract, *w, a)
            else:
                b = stt(lo, src, scale, hi.bitcast(F), ALU.mult, ALU.subtract, *w, a)
            return [a, b]

        def par(name, i=0, p=slice(0, 128)):
            c = POFF[name] + i
            return PAR[p, c:c + 1]

        k_par = dma(sp, once("par"), PAR[:], t["par"])
        k_id = dma(sp, once("idt"), IDT[:], t["consts"][:, 0:128])
        k_mk = dma(sp, once("mk"), TMP[0][:, 0:128], t["consts"][:, 128:256])
        k_one = dve.do(lambda e: e.memset(ONE[:], 1.0))
        c_idr = cp(IDR[:], IDT[:], k_id)
        c_mkr = cp(MKR[:], TMP[0][:, 0:128], k_mk)
        consts = [k_par, k_id, k_one, c_idr, c_mkr]
        for e in (pe, act, dve, pool):
            e.ops.append([lambda g: None, tokens(consts), None])
        w_dma()
        w_dma()
        w_dma()

        FW = sb("FW", A, [64, 4096])
        WPH = sb("WPH", A + 16, [64, 2048], R)
        WPL = sb("WPL", A + 24, [64, 2048], R)
        HPH = sb("HPH", A + 32, [128, 2, 4, 1024], R)
        HPL = sb("HPL", A + 64, [128, 2, 4, 1024], R)
        DEC = sb("DEC", A + 96, [128, 4, 1024])
        H3H = sb("H3H", A + 112, [64, 512], R)
        H3L = sb("H3L", A + 114, [64, 512], R)
        ZF = TMP[1]
        k_fw = dma(sp, once("fw"), FW[:], t["fw_out"])
        k_dec = dma(sp, once("dec"), DEC[:], t["decay"])
        k_zf = dma(sp, once("zf"), ZF[0:33, :], t["zfeat"])
        k_f1 = dma(sp, once("f1"), SM[0:64, 0:128], t["fsmall"][:, 0:128])
        k_f2 = dma(sp, once("f2"), SM[0:64, 128:256], t["fsmall"][:, 128:256])

        def sin_of(dst, arg, P, *w):
            kq = TMP[4][0:P, :]
            a = ts(kq, arg, 1.0 / TWO_PI, MAGIC, ALU.mult, ALU.add, *w)
            a = ts(kq, kq, MAGIC, None, ALU.subtract, None, a)
            for c in (C1, C2, C3):
                a = stt(arg, kq, -c, arg, ALU.mult, ALU.add, a)
            a = ts(arg, arg, PI_IN, -PI_IN, ALU.min, ALU.max, a)
            return af(dst, arg, ACT.Sin, a), a

        hin, hw = ZF[0:33, :], [k_zf]
        for layer in range(3):
            i, ps, fr = bank()
            lhs = SM[0:33, 0:64] if layer == 0 else SM[0:64, 64 * layer:64 * layer + 64]
            mm(ps[0:64, :], lhs, hin, True, True, fr, k_f1, k_f2, *hw)
            m = pe.mark()
            arg = TMP[2 + layer % 2][0:64, :]
            a = ts(arg, ps[0:64, :], SM[0:64, 192 + layer:193 + layer], SM[0:64, 195:196], ALU.add, ALU.mult, m)
            free[i] = [a]
            s, _ = sin_of(arg, arg, 64, a)
            hin, hw = arg, [s]
        h3 = split(hin, H3H[:], H3L[:], *hw)
        hp_used = []
        kst = [None] * 6
        KD = t["kd"]
        for o in range(2):
            c0 = 2048 * o
            wp = []
            for sgn in range(2):
                for c in range(2):
                    f_ = FW[:, c0 + 512 * c:c0 + 512 * c + 512]
                    b_ = FW[:, c0 + 1024 + 512 * c:c0 + 1024 + 512 * c + 512]
                    q = 1024 * sgn + 512 * c
                    tmp = TMP[c][0:64, :]
                    a = tt(tmp, f_, b_, ALU.subtract if sgn else ALU.add, k_fw, hp_used, c_mkr, *hw,
                           wp[-2] if len(wp) > 1 else None, kst)
                    wp.append(split(tmp, WPH[:, q:q + 512], WPL[:, q:q + 512], a))
            hp = []
            for sgn in range(2):
                for tb in range(4):
                    toks = []
                    for c in range(2):
                        i, ps, fr = bank()
                        q = 1024 * sgn + 512 * c
                        tsl = slice(128 * tb, 128 * tb + 128)
                        mm3(ps[:], H3H[:, tsl], H3L[:, tsl], WPH[:, q:q + 512], WPL[:, q:q + 512], True, True,
                            fr, h3, wp)
                        m = pe.mark()
                        k = (2 * tb + c) % 4
                        csl = slice(512 * c, 512 * c + 512)
                        a = tt(TMP[k][:], ps[:], DEC[:, tb, csl], ALU.mult, m, k_dec, hp_used,
                               hp[-4] if len(hp) >= 4 else wp)
                        free[i] = [a]
                        x = split(TMP[k][:], HPH[:, sgn, tb, csl], HPL[:, sgn, tb, csl], a)
                        hp.append(x)
            for m_ in range(4):
                for extra in range(2 if m_ == 0 else 1):
                    wh, wl, wt = w_get("dft_kx" if extra else "dft_k")
                    for part in range(1 if extra else 2):
                        for c in range(2):
                            i, ps, fr = bank()
                            for kt in range(4):
                                col = kt * (128 if extra else 256) + 128 * part
                                csl = slice(512 * c, 512 * c + 512)
                                mm3(ps[:], wh[:, col:col + 128], wl[:, col:col + 128], HPH[:, part, kt, csl],
                                    HPL[:, part, kt, csl], kt == 0, kt == 3, fr, wt, hp)
                            m = pe.mark()
                            k = 2 * part + c
                            a = cp(TMP[k][:], ps[:], m, hp, kst[k])
                            free[i] = [a]
                            row = (8 if extra else 2 * m_ + part)
                            kst[k] = dma(sp, ch_t[k], KD[o, row, :, 512 * c:512 * c + 512], TMP[k][:], a)
                    w_release()
            hp_used = [pe.mark()]
        stores += list(kst)
        kd_done = list(kst)

        def gemm_t(name, nchunk, KT, MT, acts, atoks, evac, N=512):
            ah, al = acts
            for c in range(nchunk):
                wh, wl, wt = w_get(name)
                for m_ in range(MT):
                    i, ps, fr = bank()
                    for k in range(KT):
                        col = (k * MT + m_) * 128
                        mm3(ps[:, 0:N], wh[:, col:col + 128], wl[:, col:col + 128], ah[:, k, 0:N], al[:, k, 0:N],
                            k == 0, k == KT - 1, fr, wt, atoks[k])
                    free[i] = evac(c * MT + m_, ps, pe.mark())
                w_release()

        def colstat(tiles, toks, N, scale, eps, rstd, out, slot):
            nb = N // 128
            i, ps, fr = bank()
            for b in range(nb):
                for k, ap in enumerate(tiles):
                    mm(ps[:, b:b + 1], ap[:, 128 * b:128 * b + 128], ONE[:, 0:1], k == 0, k == len(tiles) - 1,
                       fr, toks[k])
            m = pe.mark()
            v, r = SM[:, slot:slot + nb], SM[:, slot + 4:slot + 4 + nb]
            if rstd:
                a = af(v, ps[:, 0:nb], ACT.Sqrt, m, scale=scale, bias=eps)
                a2 = dve.do(lambda e: e.reciprocal(r, v), a)
            else:
                a = a2 = ts(r, ps[:, 0:nb], scale, None, ALU.mult, None, m)
            dg = TMP[5]
            d = []
            for b in range(nb):
                d.append(ts(dg[:, 128 * b:128 * b + 128], IDT[:], SM[:, slot + 4 + b:slot + 5 + b], None,
                            ALU.mult, None, a2, colstat.last))
            free[i] = [a]
            i2, ps2, fr2 = bank()
            mm(ps2[:, 0:N], ONE[:], dg[:, 0:N], True, True, fr2, *d)
            m2 = pe.mark()
            o = cp(out, ps2[:, 0:N], m2)
            free[i2] = [o]
            colstat.last = m2
            return o, m

        colstat.last = None

        def rms_stat(tiles, toks, N, eps, out, *w):
            n = len(tiles)
            nb = N // 128
            i, ps, fr = bank()
            used = [None] * 3
            SQ = [TMP[0], TMP[1], TMP[2]]
            ACC = TMP[3]
            prev = None
            for k in range(n):
                q = SQ[k % 3][:, 0:N]
                if k == 0:
                    prev = af(ACC[:, 0:N], tiles[k], ACT.Square, toks[k], *w)
                    continue
                a = af(q, tiles[k], ACT.Square, toks[k], used[k % 3], *w)
                prev = used[k % 3] = tt(ACC[:, 0:N], ACC[:, 0:N], q, ALU.add, a, prev)
            turn[0] -= 1
            return colstat([ACC[:, 0:N]], [prev], N, 1.0 / (128 * n), par(eps), True, out, 0)

        RS = TMP[4]

        k_x = dma(sp, once("x"), X[:], t["xt"])

        HH = sb("HH", A, [128, 8, 512], R)
        HL = sb("HL", A + 16, [128, 8, 512], R)

        def norm_split(gain, stat, xt, HHs, HLs, N, *w, src=X, n=8):
            toks, prev = [], [None] * 3
            for k in range(n):
                q = TMP[k % 3][:, 0:N]
                a = stt(q, src[:, k, 0:N], par(gain, k), RS[:, 0:N], ALU.mult, ALU.mult, stat, xt[k], prev[k % 3], *w)
                prev[k % 3] = split(q, HHs[:, k, 0:N], HLs[:, k, 0:N], a)
                toks.append(prev[k % 3])
            return toks

        xt = [[k_x]] * 8
        st, _ = rms_stat([X[:, k, :] for k in range(8)], xt, S, "eps6", RS[:], kst)
        ht = norm_split("g_mix_pre", st, xt, HH, HL, S, hp_used)

        QH = sb("QH", A + 32, [128, 4, 512], R)
        QL = sb("QL", A + 40, [128, 4, 512], R)
        KH = sb("KH", A + 48, [128, 4, 512], R)
        KL = sb("KL", A + 56, [128, 4, 512], R)
        VH = sb("VH", A + 64, [128, 4, 512], R)
        VL = sb("VL", A + 72, [128, 4, 512], R)
        U = sb("U", A + 80, [128, 4, 542])
        CO = sb("CO", A + 89, [128, 4, 512])
        PP = sb("PP", A + 97, [128, 4, 512])
        ATP = sb("ATP", A + 105, [128, 4, 256])
        QA = sb("QA", A + 109, [128, 2, 512], R)
        KA = sb("KA", A + 113, [128, 2, 512], R)
        z_u = dve.do(lambda e: e.memset(U[:, :, 0:30], 0.0), hp_used)
        conv_t = []
        sg = {}

        def ev_ag(n, ps, m):
            j = n // 2
            if n % 2 == 0:
                sg["t"] = af(TMP[j % 2][:], ps[:], ACT.Sigmoid, m, sg.get(j % 2), ht[7])
                return [sg["t"]]
            a = tt(U[:, j, 30:542], ps[:], TMP[j % 2][:], ALU.mult, m, sg["t"], hp_used)
            sg[j % 2] = a
            c = ts(CO[:, j, :], U[:, j, 0:512], par("conv_w", 31 * j), par("conv_b", j), ALU.mult, ALU.add, a, z_u)
            for w_ in range(1, 31):
                c = stt(CO[:, j, :], U[:, j, w_:w_ + 512], par("conv_w", 31 * j + w_), CO[:, j, :],
                        ALU.mult, ALU.add, c)
            conv_t.append(c)
            return [a]

        ag_free = []

        def ev_ag_defer(n, ps, m):
            return ev_ag(n, ps, m)

        gemm_t("win_ag", 4, 8, 2, (HH, HL), ht, ev_ag_defer)
        wh, wl, wt = w_get("win_f")
        i, ps, fr = bank()
        for b in range(4):
            for k in range(8):
                bs = slice(128 * b, 128 * b + 128)
                mm3(ps[:, 8 * b:8 * b + 8], HH[:, k, bs], HL[:, k, bs], wh[:, 8 * k:8 * k + 8], wl[:, 8 * k:8 * k + 8],
                    k == 0, k == 7, fr, wt, ht)
        w_release()
        m = pe.mark()
        z, e1, e2, lf = (SM[:, 32 * q:32 * q + 32] for q in range(1, 5))
        bf = PAR[:, POFF["b_forget"]:POFF["b_forget"] + 8]
        zt = [tt(SM[:, 32 + 8 * b:40 + 8 * b], ps[:, 8 * b:8 * b + 8], bf, ALU.add, m) for b in range(4)]
        free[i] = zt
        a = af(e1, z, ACT.Abs, *zt)
        a = af(e1, e1, ACT.Exp, a, scale=-1.0)
        a = af(e1, e1, ACT.Ln, a, bias=par("one"))
        b_ = ts(e2, z, 0.0, None, ALU.min, None, *zt)
        lft = tt(lf, e2, e1, ALU.subtract, a, b_)
        vb = [bank() for _ in range(4)]
        for c in range(2):
            wh, wl, wt = w_get("win_v")
            for b in range(4):
                for k in range(4):
                    kk = 4 * c + k
                    bs = slice(128 * b, 128 * b + 128)
                    mm3(vb[b][1][:], HH[:, kk, bs], HL[:, kk, bs], wh[:, 512 * k:512 * k + 512],
                        wl[:, 512 * k:512 * k + 512], kk == 0, kk == 7, vb[b][2], wt, ht)
                if c == 1:
                    vm = pe.mark()
                    free[vb[b][0]] = split(vb[b][1][:], VH[:, b, :], VL[:, b, :], vm, hp_used)
            w_release()
        vt = [free[vb[b][0]] for b in range(4)]
        qkt = []

        def ev_qk(n, ps, m):
            j = n // 2
            if n % 2 == 0:
                r = split(ps[:], QH[:, j, :], QL[:, j, :], m, hp_used, scale=0.125)
            else:
                r = split(ps[:], KH[:, j, :], KL[:, j, :], m, hp_used)
            qkt.append(r)
            return r

        gemm_t("win_qk", 4, 8, 2, (HH, HL), ht, ev_qk)
        h_dead = [pe.mark()]
        TRI = TMP[5]
        k_tri = dma(sp, once("tri"), TRI[:], t["consts"][:, 256:768], colstat.last)
        i, ps, fr = bank()
        for k in range(4):
            mm(ps[0:8, 128 * k:512], SM[:, 128 + 8 * k:136 + 8 * k], TRI[:, 0:512 - 128 * k], k == 0, k == 3,
               fr, lft, k_tri)
        m = pe.mark()
        colstat.last = m
        CH = sb("CH", A + 105, [8, 512], R)
        CL = sb("CL", A + 107, [8, 512], R)
        NH = sb("NH", 78, [8, 512], R)
        NL = sb("NL", 80, [8, 512], R)
        c_ = split(ps[0:8, :], CH[:], CL[:], m, hp_used)
        free[i] = c_
        n1 = cp(NH[:], CH[:].bitcast(F), *c_, sg[0], sg[1], scale=-1.0)
        n2 = cp(NL[:], CL[:].bitcast(F), *c_, sg[0], sg[1], scale=-1.0)
        o1 = pool.do(lambda e: e.memset(QA[:].bitcast(F), 1.0), hp_used)
        o2 = pool.do(lambda e: e.memset(KA[:].bitcast(F), 1.0), hp_used)
        augt = []
        for q, (dst, src, row) in enumerate([(QA, CH, 0), (QA, CL, 1), (KA, NH, 2), (KA, NL, 3)]):
            for g in range(2):
                augt.append(dma(sp, once(f"aug{q}{g}"), dst[row:row + 97:32, g, :].bitcast(F),
                                src[4 * g:4 * g + 4, :].bitcast(F), *c_, n1, n2, o1, o2))
        MN = TMP[3]
        cm, _ = colstat([CO[:, j, :] for j in range(4)], conv_t, S, 1.0 / 512, None, False, MN[:], 0)
        xc = [tt(CO[:, j, :], CO[:, j, :], MN[:], ALU.subtract, cm) for j in range(4)]
        st, _ = rms_stat([CO[:, j, :] for j in range(4)], [[x_] for x_ in xc], S, "eps6", RS[:], augt, xc[3])
        cat = []
        for j in range(4):
            a = tt(CO[:, j, :], CO[:, j, :], RS[:], ALU.mult, st)
            a = af(CO[:, j, :], CO[:, j, :], ACT.Silu, a, scale=par("cln_g", j), bias=par("cln_b", j))
            cat.append(split(CO[:, j, :], HH[:, j, :], HL[:, j, :], a, h_dead))
        co_dead = cat

        PTH = sb("PTH", A + 80, [128, 4, 512], R)
        PTL = sb("PTL", A + 88, [128, 4, 512], R)

        def logits_softmax(i_, ps, nk, m, scale, Pt, slot, pfree):
            mx = SM[:, slot + i_:slot + i_ + 1]
            sm_ = SM[:, slot + 4 + i_:slot + 5 + i_]
            rc = SM[:, slot + 8 + i_:slot + 9 + i_]
            a = dve.do(lambda e: e.reduce_max(mx, ps[:, 0:nk], AX), m, pfree)
            b = ts(mx, mx, -scale, None, ALU.mult, None, a)
            c = act.do(lambda e: e.activation(Pt, ps[:, 0:nk], ACT.Exp, bias=mx, scale=scale, accum_out=sm_), b, pfree)
            d = dve.do(lambda e: e.reciprocal(rc, sm_), c)
            return c, d

        fx = {"p": [], "pv": []}

        def fox_s(h):
            pb, j = 64 * (h % 2), h // 2
            ab, g = 32 * (h % 4), h // 4
            out = []
            for i_ in range(4):
                nk = 128 * (i_ + 1)
                bi, ps, fr = bank()
                qs = slice(128 * i_, 128 * i_ + 128)
                mm3(ps[:, 0:nk], QH[pb:pb + 64, j, qs], QL[pb:pb + 64, j, qs], KH[pb:pb + 64, j, 0:nk],
                    KL[pb:pb + 64, j, 0:nk], True, False, fr, qkt[2 * j], qkt[2 * j + 1])
                mm(ps[:, 0:nk], QA[ab:ab + 4, g, qs], KA[ab:ab + 4, g, 0:nk], False, False, augt)
                mm(ps[:, nk - 128:nk], IDR[:], MKR[:], False, True)
                c, d = logits_softmax(i_, ps, nk, pe.mark(), 1.0, PP[:, i_, 0:nk], 32 * (h % 2) + 64, fx["p"])
                free[bi] = [c]
                out.append((c, d))
            return out

        atd = [None] * 4

        def fox_t(h, sm_):
            bl = []
            for j in range(4):
                bi, ps, fr = bank()
                for i_ in range(j, 4):
                    o = ps[:, 128 * i_:128 * i_ + 128]
                    src = PP[:, i_, 128 * j:128 * j + 128]
                    pe.do(lambda e, o=o, src=src: e.transpose(o, src, IDT[:]), fr, sm_[i_][0], inc=False)
                m = pe.mark()
                sp_ = split(ps[:, 128 * j:512], PTH[:, j, 128 * j:512], PTL[:, j, 128 * j:512], m, fx["pv"], co_dead)
                free[bi] = sp_
                bl.append(sp_)
            fx["p"] = [pe.mark()]
            return bl

        def fox_pv(h, bl, sm_):
            bi, ps, fr = bank()
            hs = slice(64 * h, 64 * h + 64)
            for i_ in range(4):
                for j in range(i_ + 1):
                    q = slice(128 * i_, 128 * i_ + 128)
                    mm3(ps[:, 64 * i_:64 * i_ + 64], PTH[:, j, q], PTL[:, j, q], VH[:, j, hs], VL[:, j, hs],
                        j == 0, j == i_, fr, bl, vt)
            m = pe.mark()
            fx["pv"] = [m]
            slot = 32 * (h % 2) + 64 + 8
            o = []
            for i_ in range(4):
                dst = ATP[:, i_, 64 * (h % 2):64 * (h % 2) + 64]
                o.append(ts(dst, ps[:, 64 * i_:64 * i_ + 64], SM[:, slot + i_:slot + i_ + 1], None, ALU.mult, None,
                            m, sm_[i_][1], atd[0], augt))
            free[bi] = o
            if h % 2 == 0:
                fx["o"] = o
                return
            bi, ps, fr = bank()
            for i_ in range(4):
                dst, src = ps[:, 128 * i_:128 * i_ + 128], ATP[:, i_, 0:128]
                pe.do(lambda e, dst=dst, src=src: e.transpose(dst, src, IDT[:]), fr, fx["o"], o, inc=False)
            atd[0] = pe.mark()
            j = 4 + h // 2
            sp_ = split(ps[:], HH[:, j, :], HL[:, j, :], atd[0], h_dead)
            free[bi] = sp_
            cat.append(sp_)

        smx = fox_s(0)
        for h in range(8):
            bl = fox_t(h, smx)
            nxt = fox_s(h + 1) if h < 7 else None
            fox_pv(h, bl, smx)
            smx = nxt

        def res_gemm(name, nchunk, KT, MT, acts, atoks, Y, g, *w):
            yt = []

            def ev(n, ps, m):
                a = cp(Y[:, n, :], ps[:], m, *w)
                yt.append([a])
                return [a]

            gemm_t(name, nchunk, KT, MT, acts, atoks, ev)
            return finish_res(Y, yt, g)

        def finish_res(Y, yt, g):
            st, _ = rms_stat([Y[:, k, :] for k in range(8)], yt, S, "eps6", RS[:], xt[7])
            out = []
            for k in range(8):
                a = stt(Y[:, k, :], Y[:, k, :], par(g, k), RS[:], ALU.mult, ALU.mult, st)
                out.append([tt(X[:, k, :], X[:, k, :], Y[:, k, :], ALU.add, a, xt[k])])
            return out

        Y1 = sb("Y1", A + 32, [128, 8, 512])
        xt = res_gemm("w_out", 4, 8, 2, (HH, HL), cat, Y1, "g_mix_post", fx["pv"])

        MX = sb("MX", A + 32, [128, 8, 256])
        HMH = sb("HMH", A + 40, [128, 8, 256], R)
        HML = sb("HML", A + 48, [128, 8, 256], R)
        KMH = sb("KMH", A + 56, [128, 4, 256], R)
        KML = sb("KML", A + 60, [128, 4, 256], R)
        VMH = sb("VMH", A + 64, [128, 2, 512], R)
        VML = sb("VML", A + 68, [128, 2, 512], R)
        QMH = sb("QMH", A + 72, [128, 4, 512], R)
        QML = sb("QML", A + 80, [128, 4, 512], R)
        PM = sb("PM", A + 88, [128, 4, 256])
        PMH = sb("PMH", A + 92, [128, 2, 512], R)
        PML = sb("PML", A + 96, [128, 2, 512], R)
        OMH = sb("OMH", A + 100, [128, 4, 512], R)
        OML = sb("OML", A + 108, [128, 4, 512], R)
        k_m = dma(sp, once("mem"), MX[:], t["memt"], xt)
        mt = [[k_m]] * 8
        st, _ = rms_stat([MX[:, k, :] for k in range(8)], mt, 256, "eps6", RS[:, 0:256], xt[7])
        hmt = norm_split("g_memkv", st, mt, HMH, HML, 256, src=MX)
        kmt = []

        def ev_km(n, ps, m):
            r = split(ps[:, 0:256], KMH[:, n, :], KML[:, n, :], m)
            kmt.append(r)
            return r

        gemm_t("w_mk", 2, 8, 2, (HMH, HML), hmt, ev_km, N=256)
        vb = [bank() for _ in range(2)]
        for c in range(2):
            wh, wl, wt = w_get("w_mv")
            for b in range(2):
                for k in range(4):
                    kk = 4 * c + k
                    bs = slice(128 * b, 128 * b + 128)
                    mm3(vb[b][1][:], HMH[:, kk, bs], HML[:, kk, bs], wh[:, 512 * k:512 * k + 512],
                        wl[:, 512 * k:512 * k + 512], kk == 0, kk == 7, vb[b][2], wt, hmt)
                if c == 1:
                    free[vb[b][0]] = split(vb[b][1][:], VMH[:, b, :], VML[:, b, :], pe.mark())
            w_release()
        vmt = [free[vb[b][0]] for b in range(2)]
        st, _ = rms_stat([X[:, k, :] for k in range(8)], xt, S, "eps6", RS[:], hmt[6], hmt[7], hmt[5])
        ht = norm_split("g_mem_pre", st, xt, HH, HL, S, hmt)
        qmt = []

        def ev_qm(n, ps, m):
            r = split(ps[:], QMH[:, n, :], QML[:, n, :], m)
            qmt.append(r)
            return r

        gemm_t("w_mq", 2, 8, 2, (HH, HL), ht, ev_qm)
        MS = float(128.0 ** -0.5)
        mfx = {"p": [], "pv": []}

        def mem_s(h):
            out = []
            for i_ in range(4):
                bi, ps, fr = bank()
                qs = slice(128 * i_, 128 * i_ + 128)
                mm3(ps[:, 0:256], QMH[:, h, qs], QML[:, h, qs], KMH[:, h, :], KML[:, h, :], True, True, fr,
                    qmt[h], kmt[h])
                slot = 32 * (h % 2) + 64
                c, d = logits_softmax(i_, ps, 256, pe.mark(), MS, PM[:, i_, :], slot, mfx["p"])
                free[bi] = [c]
                out.append([ts(PM[:, i_, :], PM[:, i_, :], SM[:, slot + 8 + i_:slot + 9 + i_], None, ALU.mult, None,
                               c, d)])
            return out

        def mem_t(h, sm_):
            bl = []
            for j in range(2):
                bi, ps, fr = bank()
                for i_ in range(4):
                    o, src = ps[:, 128 * i_:128 * i_ + 128], PM[:, i_, 128 * j:128 * j + 128]
                    pe.do(lambda e, o=o, src=src: e.transpose(o, src, IDT[:]), fr, sm_[i_], inc=False)
                sp_ = split(ps[:], PMH[:, j, :], PML[:, j, :], pe.mark(), mfx["pv"])
                free[bi] = sp_
                bl.append(sp_)
            mfx["p"] = [pe.mark()]
            return bl

        omt = []

        def mem_pv(h, bl):
            bi, ps, fr = bank()
            hs = slice(128 * h, 128 * h + 128)
            for j in range(2):
                mm3(ps[:], VMH[:, j, hs], VML[:, j, hs], PMH[:, j, :], PML[:, j, :], j == 0, j == 1, fr, bl, vmt)
            mfx["pv"] = [pe.mark()]
            free[bi] = split(ps[:], OMH[:, h, :], OML[:, h, :], mfx["pv"])
            omt.append(free[bi])

        smx = mem_s(0)
        for h in range(4):
            bl = mem_t(h, smx)
            nxt = mem_s(h + 1) if h < 3 else None
            mem_pv(h, bl)
            smx = nxt
        Y2 = sb("Y2", A + 0, [128, 8, 512])
        xt = res_gemm("w_mo", 2, 4, 4, (OMH, OML), omt, Y2, "g_mem_post", qmt)

        st, _ = rms_stat([X[:, k, :] for k in range(8)], xt, S, "eps6", RS[:], xt[7])
        ht = norm_split("g_mlp_pre", st, xt, HH, HL, S)
        mo_dead = [pe.mark()]
        MID = sb("MID", A + 32, [128, 32, 512])
        MRH = [sb(f"MRH{i}", A + 96 + 2 * i, [128, 512], R) for i in range(2)]
        MRL = [sb(f"MRL{i}", A + 100 + 2 * i, [128, 512], R) for i in range(2)]
        mid = []
        md = [None, None, None]

        def ev_up(n, ps, m):
            q = TMP[n % 3][:]
            a = af(q, ps[:], ACT.Relu, m, md[n % 3], mo_dead, ht[7], ht[6], ht[5])
            md[n % 3] = tt(MID[:, n, :], q, q, ALU.mult, a)
            mid.append([md[n % 3]])
            return [a]

        gemm_t("w_up", 16, 8, 2, (HH, HL), ht, ev_up)

        def down(name, nchunk, src, toks, Y, evac):
            bs = [bank() for _ in range(8)]
            used = [None, None]
            last = 2 * nchunk - 1
            for c in range(nchunk):
                wh, wl, wt = w_get(name)
                for kk in range(2):
                    k = 2 * c + kk
                    sp_ = split(src[:, k, :], MRH[k % 2][:], MRL[k % 2][:], toks[k], used[k % 2])
                    for m_ in range(8):
                        col = kk * 1024 + 128 * m_
                        mm3(bs[m_][1][:], wh[:, col:col + 128], wl[:, col:col + 128], MRH[k % 2][:], MRL[k % 2][:],
                            k == 0, k == last, bs[m_][2], wt, sp_)
                        if k == last:
                            free[bs[m_][0]] = evac(m_, bs[m_][1], pe.mark())
                    used[k % 2] = [pe.mark()]
                w_release()

        yt = []
        h_dead = [pe.mark()]

        def ev_y(n, ps, m):
            a = cp(Y2[:, n, :], ps[:], m, h_dead)
            yt.append([a])
            return [a]

        down("w_down", 16, MID, mid, Y2, ev_y)
        xt = finish_res(Y2, yt, "g_mlp_post")
        y_dead = [xt]

        def x_split(*w):
            return [split(X[:, k, :], HH[:, k, :], HL[:, k, :], xt[k], *w) for k in range(8)]

        def deep_norm(g, b):
            nonlocal xt
            MN = TMP[3]
            cm, _ = colstat([X[:, j, :] for j in range(8)], xt, S, 1.0 / 1024, None, False, MN[:], 0)
            xc = [[tt(X[:, j, :], X[:, j, :], MN[:], ALU.subtract, cm)] for j in range(8)]
            st, _ = rms_stat([X[:, j, :] for j in range(8)], xc, S, "eps5", RS[:], xc[7])
            out = []
            for k in range(8):
                a = tt(X[:, k, :], X[:, k, :], RS[:], ALU.mult, st)
                out.append([af(X[:, k, :], X[:, k, :], ACT.Identity, a, scale=par(g, k), bias=par(b, k))])
            xt = out

        def ev_deep(n, ps, m):
            a = stt(X[:, n, :], X[:, n, :], ALPHA, ps[:], ALU.mult, ALU.add, m, xt[n])
            xt[n] = [a]
            return [a]

        def ffn(l):
            nonlocal xt
            ht = x_split([pe.mark()], y_dead)
            cw = f"ffn_conv{l}"
            PADB = [sb(f"PAD{l}{i}", A + 84 + 2.25 * i, [128, 514]) for i in range(4)]
            zp = [pool.do(lambda e, q=q: e.memset(q[:, 0:1], 0.0), ht[0]) for q in PADB]
            zp += [pool.do(lambda e, q=q: e.memset(q[:, 513:514], 0.0), ht[0]) for q in PADB]
            stt_ = {"u": [None] * 4, "o": [None, None, None, None]}
            mid = []

            def ev(n, ps, m):
                b = n % 4
                q = PADB[b]
                o = TMP[b]
                j = n // 2 + (22 if n % 2 else 0)
                a = cp(q[:, 1:513], ps[:], m, stt_["u"][b], zp)
                c = ts(o[:], q[:, 0:512], par(cw, 3 * j), None, ALU.mult, None, a, stt_["o"][b])
                c = stt(o[:], q[:, 1:513], par(cw, 3 * j + 1), o[:], ALU.mult, ALU.add, c)
                c = stt(o[:], q[:, 2:514], par(cw, 3 * j + 2), o[:], ALU.mult, ALU.add, c)
                stt_["u"][b] = c
                if n % 2 == 0:
                    stt_["a"] = c
                else:
                    s_ = af(o[:], o[:], ACT.Silu, c)
                    r = tt(MID[:, n // 2, :], TMP[b - 1][:], o[:], ALU.mult, s_, stt_["a"])
                    mid.append([r])
                    stt_["o"][b] = stt_["o"][b - 1] = r
                return [a]

            gemm_t(f"up2_{l}", 22, 8, 2, (HH, HL), ht, ev)
            down(f"down2_{l}", 11, MID, mid, None, ev_deep)

        ht = x_split(h_dead, y_dead)
        CQF = sb("CQF", A + 60, [128, 6, 512])
        CQH = sb("CQH", A + 32, [128, 3, 512], R)
        CQL = sb("CQL", A + 38, [128, 3, 512], R)
        CVH = sb("CVH", A + 44, [128, 2, 512], R)
        CVL = sb("CVL", A + 48, [128, 2, 512], R)
        KRH = sb("KRH", A + 52, [128, 512], R)
        KRL = sb("KRL", A + 54, [128, 512], R)
        CS = sb("CS", A + 56, [128, 512])
        SN = sb("SN", A + 58, [128, 512])
        POSI = sb("POSI", 78, [128, 512], I32)
        k_pos = dma(sp, once("pos"), POSI[:], t["pos"], ht[7])
        ANG = TMP[1]
        a = dve.do(lambda e: e.tensor_copy(ANG[:], POSI[:]), k_pos)
        a = ts(ANG[:], ANG[:], par("inv"), None, ALU.mult, None, a)
        s_, rd = sin_of(SN[:], ANG[:], 128, a, h_dead)
        a = af(TMP[2][:], ANG[:], ACT.Abs, rd)
        c_ = af(CS[:], TMP[2][:], ACT.Sin, a, h_dead, scale=-1.0, bias=par("halfpi"))
        s_ = ts(SN[:], SN[:], par("sgn"), None, ALU.mult, None, s_)
        tab = [s_, c_]
        cqt = []

        def rope(psA, psB, mA, mB, hi, lo, q, *w):
            t1, t2 = TMP[q], TMP[q + 1]
            a = tt(t1[:], psA[:], CS[:], ALU.mult, mA, tab, *w)
            b = tt(t2[:], psB[:], SN[:], ALU.mult, mB, tab, *w)
            c = tt(t1[:], t1[:], t2[:], ALU.add, a, b)
            return a, b, split(t1[:], hi, lo, c, *w)

        krs = {}

        def ev_in(n, ps, m):
            if n < 5:
                a = cp(CQF[:, n, :], ps[:], m, y_dead, mid)
                cqt.append([a])
                return [a]
            a = cp(TMP[3][:], ps[:], m, tab)
            krs["a"] = a
            return [a]

        mid = [h_dead]
        gemm_t("mla_in", 3, 8, 2, (HH, HL), ht, ev_in)

        def ev_inx(n, ps, m):
            a, b, krs["t"] = rope(TMP[3], ps, krs["a"], m, KRH[:], KRL[:], 1)
            return [b]

        gemm_t("mla_inx", 1, 8, 1, (HH, HL), ht, ev_inx)
        x_dead = [pe.mark()]
        st, _ = rms_stat([CQF[:, k, :] for k in range(3)], cqt[0:3], S, "eps6", RS[:], krs["t"])
        cq = norm_split("g_q", st, cqt, CQH, CQL, S, y_dead, src=CQF, n=3)
        st2, _ = rms_stat([CQF[:, 3 + k, :] for k in range(2)], cqt[3:5], S, "eps6", RS[:], cq)
        cv = norm_split("g_kv", st2, cqt[3:5], CVH, CVL, S, y_dead, src=CQF[:, 3:5, :], n=2)
        QNH = sb("QNH", A + 60, [128, 2, 512], R)
        QNL = sb("QNL", A + 64, [128, 2, 512], R)
        QRH = sb("QRH", A + 68, [128, 512], R)
        QRL = sb("QRL", A + 70, [128, 512], R)
        KNH = sb("KNH", A + 72, [128, 2, 512], R)
        KNL = sb("KNL", A + 76, [128, 2, 512], R)
        V2H = sb("V2H", A + 80, [128, 4, 256], R)
        V2L = sb("V2L", A + 84, [128, 4, 256], R)
        PA = sb("PA", A + 88, [128, 4, 512])
        PAH = sb("PAH", A + 96, [128, 4, 512], R)
        PAL = sb("PAL", A + 104, [128, 4, 512], R)
        MLS = float(192.0 ** -0.5)
        lfx = {"p": [], "pv": [], "pair": [cq, cv]}
        omt = []

        def mla_s(h, pt):
            hh = h % 2
            pb = 64 * hh
            out = []
            for i_ in range(4):
                bi, ps, fr = bank()
                qs = slice(128 * i_, 128 * i_ + 128)
                mm3(ps[:], QNH[:, hh, qs], QNL[:, hh, qs], KNH[:, hh, :], KNL[:, hh, :], True, False, fr, pt)
                mm3(ps[:], QRH[pb:pb + 64, qs], QRL[pb:pb + 64, qs], KRH[pb:pb + 64, :], KRL[pb:pb + 64, :],
                    False, True, krs["t"])
                slot = 32 * hh + 64
                c, d = logits_softmax(i_, ps, 512, pe.mark(), MLS, PA[:, i_, :], slot, lfx["p"])
                free[bi] = [c]
                out.append([ts(PA[:, i_, :], PA[:, i_, :], SM[:, slot + 8 + i_:slot + 9 + i_], None, ALU.mult, None,
                               c, d)])
            return out

        def mla_t(h, sm_):
            bl = []
            for j in range(4):
                bi, ps, fr = bank()
                for i_ in range(4):
                    o, src = ps[:, 128 * i_:128 * i_ + 128], PA[:, i_, 128 * j:128 * j + 128]
                    pe.do(lambda e, o=o, src=src: e.transpose(o, src, IDT[:]), fr, sm_[i_], inc=False)
                sp_ = split(ps[:], PAH[:, j, :], PAL[:, j, :], pe.mark(), lfx["pv"])
                free[bi] = sp_
                bl.append(sp_)
            lfx["p"] = [pe.mark()]
            return bl

        def mla_pv(h, bl, pt):
            bi, ps, fr = bank()
            hs = slice(128 * (h % 2), 128 * (h % 2) + 128)
            for j in range(4):
                mm3(ps[:], V2H[:, j, hs], V2L[:, j, hs], PAH[:, j, :], PAL[:, j, :], j == 0, j == 3, fr, bl, pt)
            lfx["pv"] = [pe.mark()]
            free[bi] = split(ps[:], HH[:, h, :], HL[:, h, :], lfx["pv"], x_dead)
            omt.append(free[bi])

        for p in range(4):
            wh, wl, wt = w_get("uq")
            pw = lfx["pair"]
            pt = []
            rb = []
            for m_ in range(4):
                bi, ps, fr = bank()
                for k in range(3):
                    col = (k * 4 + m_) * 128
                    mm3(ps[:], wh[:, col:col + 128], wl[:, col:col + 128], CQH[:, k, :], CQL[:, k, :], k == 0, k == 2,
                        fr, wt, cq)
                m = pe.mark()
                if m_ < 2:
                    free[bi] = split(ps[:], QNH[:, m_, :], QNL[:, m_, :], m, pw)
                    pt.append(free[bi])
                else:
                    rb.append((bi, ps, m))
            cpa = cp(TMP[3][:], rb[0][1][:], rb[0][2], lfx.get("rope"), cq, cv)
            free[rb[0][0]] = [cpa]
            a, b, r = rope(TMP[3], rb[1][1], cpa, rb[1][2], QRH[:], QRL[:], 1, pw)
            free[rb[1][0]] = [b]
            lfx["rope"] = r
            pt.append(r)
            w_release()
            wh, wl, wt = w_get("ukv")
            for m_ in range(2):
                bi, ps, fr = bank()
                for k in range(2):
                    col = k * 512 + m_ * 128
                    mm3(ps[:], wh[:, col:col + 128], wl[:, col:col + 128], CVH[:, k, :], CVL[:, k, :], k == 0, k == 1,
                        fr, wt, cv)
                free[bi] = split(ps[:], KNH[:, m_, :], KNL[:, m_, :], pe.mark(), pw)
                pt.append(free[bi])
            for b in range(4):
                bi, ps, fr = bank()
                bs = slice(128 * b, 128 * b + 128)
                for k in range(2):
                    col = k * 512 + 256
                    mm3(ps[:, 0:256], CVH[:, k, bs], CVL[:, k, bs], wh[:, col:col + 256], wl[:, col:col + 256],
                        k == 0, k == 1, fr, wt, cv)
                free[bi] = split(ps[:, 0:256], V2H[:, b, :], V2L[:, b, :], pe.mark(), pw)
                pt.append(free[bi])
            w_release()
            smx = mla_s(2 * p, pt)
            for hh in range(2):
                h = 2 * p + hh
                bl = mla_t(h, smx)
                nxt = mla_s(h + 1, pt) if hh == 0 else None
                mla_pv(h, bl, pt)
                smx = nxt
            lfx["pair"] = [pe.mark()]
        gemm_t("mla_o", 4, 8, 2, (HH, HL), omt, ev_deep)
        h_dead = [pe.mark()]
        deep_norm("ln1_g0", "ln1_b0")
        ffn(0)
        deep_norm("ln2_g0", "ln2_b0")

        h_dead = [pe.mark()]
        ht = x_split(h_dead)
        XD = t["xd"]
        s_x = dma(sp, once("xs"), XD, X[:], xt)
        stores.append(s_x)
        VG = [sb(f"VG{i}", A + 32 + 16 * i, [128, 8, 512]) for i in range(3)]
        PADH = [sb(f"PADH{i}", A + 96 + 2.25 * i, [128, 514]) for i in range(4)]
        zp = [pool.do(lambda e, q=q: e.memset(q[:, 0:1], 0.0), h_dead) for q in PADH]
        zp += [pool.do(lambda e, q=q: e.memset(q[:, 513:514], 0.0), h_dead) for q in PADH]
        hyu = [None] * 4
        vg = [[None] * 8 for _ in range(3)]

        def ev_hy(n, ps, m):
            b = n % 4
            q = PADH[b]
            g, j = n // 8, n % 8
            o = VG[g][:, j, :]
            a = cp(q[:, 1:513], ps[:], m, hyu[b], zp)
            c = ts(o, q[:, 0:512], par("w_short", 3 * n), None, ALU.mult, None, a, h_dead)
            c = stt(o, q[:, 1:513], par("w_short", 3 * n + 1), o, ALU.mult, ALU.add, c)
            c = stt(o, q[:, 2:514], par("w_short", 3 * n + 2), o, ALU.mult, ALU.add, c)
            hyu[b] = c
            vg[g][j] = [c]
            return [a]

        gemm_t("hy_in", 12, 8, 2, (HH, HL), ht, ev_hy)
        x_dead = [pe.mark()]
        ZH = sb("ZH", A, [128, 4, 1024], R)
        ZL = sb("ZL", A + 16, [128, 4, 1024], R)
        YF = sb("YF", A + 80, [128, 8, 1024])
        KB = [sb(f"KB{i}", 8 * i, [128, 2048]) for i in range(2)]
        YH = [sb(f"YH{i}", 8 * i, [128, 1024], R) for i in range(2)]
        YL = [sb(f"YL{i}", 8 * i + 4, [128, 1024], R) for i in range(2)]
        ch_k = [chan("c_k0"), chan("c_k1")]
        ch_kx = chan("c_kx")
        z_src, z_tok = VG[0], vg[0]
        inv_done = [s_x]
        kx_done = []
        for o in range(2):
            zt = []
            for tb in range(4):
                for c in range(2):
                    bi, ps, fr = bank()
                    for j in range(4):
                        dst = ps[:, 128 * j:128 * j + 128]
                        src = z_src[:, 4 * c + j, 128 * tb:128 * tb + 128]
                        pe.do(lambda e, dst=dst, src=src: e.transpose(dst, src, IDT[:]), fr, z_tok[4 * c + j],
                              inc=False)
                    csl = slice(512 * c, 512 * c + 512)
                    free[bi] = split(ps[:], ZH[:, tb, csl], ZL[:, tb, csl], pe.mark(), x_dead)
                    zt.append(free[bi])
            yft = [None] * 8
            kbu = [inv_done, inv_done]
            pt_ = [None, None]
            for m_ in range(4):
                kl = dma(sp, ch_k[m_ % 2], KB[m_ % 2][:].rearrange("p (a c) -> p a c", a=2),
                         KD[o, 2 * m_:2 * m_ + 2].rearrange("a p c -> p a c"), kbu[m_ % 2], kd_done, s_x)
                wh, wl, wt = w_get("dft_z")
                bk = []
                for part in range(2):
                    for c in range(2):
                        bi, ps, fr = bank()
                        for kt in range(4):
                            col = kt * 256 + 128 * part
                            csl = slice(512 * c, 512 * c + 512)
                            mm3(ps[:], wh[:, col:col + 128], wl[:, col:col + 128], ZH[:, kt, csl], ZL[:, kt, csl],
                                kt == 0, kt == 3, fr, wt, zt)
                        bk.append((bi, ps, pe.mark()))
                w_release()
                ku = []
                for c in range(2):
                    csl = slice(512 * c, 512 * c + 512)
                    (br, pr, mr), (bi_, pi, mi) = bk[c], bk[2 + c]
                    kr = KB[m_ % 2][:, 512 * c:512 * c + 512]
                    ki = KB[m_ % 2][:, 1024 + 512 * c:1536 + 512 * c]
                    kr2, kr2t = kr, None
                    if m_ == 0:
                        kr2 = TMP[5][:]
                        kr2t = dma(sp, ch_kx, kr2, KD[o, 8, :, 512 * c:512 * c + 512], kd_done, colstat.last, kx_done)
                    t1, t2 = TMP[2 * c][:], TMP[2 * c + 1][:]
                    a1 = tt(t1, pr[:], kr, ALU.mult, mr, kl, pt_[c])
                    a2 = tt(t2, pi[:], ki, ALU.mult, mi, kl, pt_[c])
                    a3 = tt(YF[:, 2 * m_, csl], t1, t2, ALU.subtract, a1, a2, inv_done, x_dead, hyu)
                    b1 = tt(t1, pr[:], ki, ALU.mult, a3)
                    b2 = tt(t2, pi[:], kr2, ALU.mult, a3, kr2t)
                    b3 = tt(YF[:, 2 * m_ + 1, csl], t1, t2, ALU.add, b1, b2, inv_done, x_dead, hyu)
                    if m_ == 0:
                        kx_done = [b2]
                    pt_[c] = b3
                    free[br], free[bi_] = [b1], [b2]
                    ku.append(b3)
                    yft[2 * m_] = (yft[2 * m_] or []) + [a3]
                    yft[2 * m_ + 1] = (yft[2 * m_ + 1] or []) + [b3]
                kbu[m_ % 2] = ku
            bs = [bank() for _ in range(8)]
            order = [0, 2, 4, 6, 1, 3, 5, 7]
            used = [kbu, kbu]
            gate = VG[1 + o]
            res = []
            for c in range(2):
                wh, wl, wt = w_get("dft_i")
                for kk in range(4):
                    k = 4 * c + kk
                    f_ = order[k]
                    sp_ = split(YF[:, f_, :], YH[k % 2][:], YL[k % 2][:], yft[f_], used[k % 2])
                    for m_ in range(8):
                        cs_ = slice(128 * m_, 128 * m_ + 128)
                        ws_ = slice(512 * kk, 512 * kk + 512)
                        mm3(bs[m_][1][:], YH[k % 2][:, cs_], YL[k % 2][:, cs_], wh[:, ws_], wl[:, ws_],
                            k == 0, k == 7, bs[m_][2], wt, sp_)
                        if k == 7:
                            m = pe.mark()
                            a = stt(VG[0][:, m_, :], VG[0][:, m_, :], par("d_bias", 8 * o + m_), bs[m_][1][:],
                                    ALU.mult, ALU.add, m, z_tok[m_], zt)
                            b = tt(VG[0][:, m_, :], VG[0][:, m_, :], gate[:, m_, :], ALU.mult, a, vg[1 + o][m_])
                            free[bs[m_][0]] = [a]
                            res.append([b])
                    used[k % 2] = [pe.mark()]
                w_release()
            z_tok = res
            inv_done = [pe.mark()]
            x_dead = inv_done
        k_x = dma(sp, once("xl"), X[:], XD, inv_done)
        xt = [[k_x] for _ in range(8)]
        ht = [split(VG[0][:, k, :], HH[:, k, :], HL[:, k, :], z_tok[k], inv_done) for k in range(8)]
        gemm_t("hy_o", 4, 8, 2, (HH, HL), ht, ev_deep)
        deep_norm("ln1_g1", "ln1_b1")
        ffn(1)
        deep_norm("ln2_g1", "ln2_b1")
        for k in range(8):
            stores.append(dma(sp, once(f"out{k}"), t["out"][:, k, :], X[:, k, :], xt[k]))
        assert wst["get"] == len(CHUNKS)
        sp.ops.append([lambda e: None, tokens(stores), None])

        block = es.enter_context(nc.Block())

        @block.sync
        def _(e):
            sp.issue(e)

        @block.gpsimd
        def _(e):
            pool.issue(e)

        @block.scalar
        def _(e):
            act.issue(e)

        @block.vector
        def _(e):
            dve.issue(e)

        @block.tensor
        def _(e):
            pe.issue(e)


def layout(v):
    f32 = np.float32
    o = {}

    def cut(w, kt, mt):
        K, M = w.shape
        n = M // (128 * mt)
        return np.ascontiguousarray(w.reshape(kt, 128, n, mt * 128).transpose(2, 1, 0, 3).reshape(n, 128, -1))

    def rows(w, kk):
        K, N = w.shape
        return np.ascontiguousarray(w.reshape(K // (128 * kk), kk, 128, N).transpose(0, 2, 1, 3).reshape(-1, 128, kk * N))

    def pairs(a, b):
        K = a.shape[0]
        return np.stack([a.reshape(K, -1, 128), b.reshape(K, -1, 128)], 2).reshape(K, -1)

    w_in = v["w_in"][0]
    o["win_ag"] = cut(pairs(w_in[:, 512:1024], w_in[:, 0:512]), 8, 2)
    o["win_qk"] = cut(pairs(w_in[:, 1024:1536], w_in[:, 1536:2048]), 8, 2)
    o["win_v"] = rows(w_in[:, 2048:2560], 4)
    o["win_f"] = rows(w_in[:, 2560:2568], 8)
    o["w_out"] = cut(v["w_out"][0], 8, 2)
    o["w_mk"] = cut(v["w_mk"][0], 8, 2)
    o["w_mv"] = rows(v["w_mv"][0], 4)
    o["w_mq"] = cut(v["w_mq"][0], 8, 2)
    o["w_mo"] = cut(v["w_mo"][0], 4, 4)
    o["w_up"] = cut(v["w_up"][0], 8, 2)
    o["w_down"] = rows(v["w_down"][0], 2)
    mi = v["mla_w_in_2"][0]
    kr = mi[:, 640:704]
    sw = np.concatenate([kr[:, 32:64], kr[:, 0:32]], 1)
    o["mla_in"] = cut(np.concatenate([mi[:, 0:640], kr, kr], 1), 8, 2)
    o["mla_inx"] = cut(np.concatenate([sw, sw], 1), 8, 1)
    uq = v["mla_w_uq_2"][0].reshape(384, 8, 192)
    qn, q1, q2 = uq[:, :, 0:128], uq[:, :, 128:160], uq[:, :, 160:192]
    qr = np.concatenate([q1, q2], 2)
    qs = np.concatenate([q2, q1], 2)
    uqp = np.concatenate([qn.reshape(384, 4, 256), qr.reshape(384, 4, 128), qs.reshape(384, 4, 128)], 2)
    o["uq"] = cut(uqp.reshape(384, 2048), 3, 4)
    ukv = v["mla_w_ukv_2"][0].reshape(256, 4, 2, 256)
    ukp = np.concatenate([ukv[..., 0:128].reshape(256, 4, 256), ukv[..., 128:256].reshape(256, 4, 256)], 2)
    o["ukv"] = cut(ukp.reshape(256, 2048), 2, 4)
    o["mla_o"] = cut(v["mla_w_o_2"][0], 8, 2)
    o["hy_in"] = cut(v["hy_w_in_2"][0], 8, 2)
    o["hy_o"] = cut(v["hy_w_o_2"][0], 8, 2)
    for l in range(2):
        up = v["ffn_w_up_2"][l]
        o[f"up2_{l}"] = cut(pairs(up[:, 0:2816], up[:, 2816:5632]), 8, 2)
        o[f"down2_{l}"] = rows(v["ffn_w_down_2"][l], 2)
    tt_ = np.arange(512)
    ph = (np.outer(tt_, tt_) % 1024) * (2 * np.pi / 1024)
    cr, si = np.cos(ph), -np.sin(ph)
    alt = (-1.0) ** tt_
    sn = si.copy()
    sn[:, 0] = alt
    crx = cr[:, 0:128].copy()
    crx[:, 0] = alt
    o["dft_k"] = cut(pairs(cr, si).astype(f32), 4, 2)
    o["dft_kx"] = cut(crx.astype(f32), 4, 1)
    o["dft_z"] = cut(pairs(cr, sn).astype(f32), 4, 2)
    wgt = np.full((512, 1), 2.0 / 1024)
    wgt[0] = 1.0 / 1024
    ir, ii = cr.T * wgt, si.T * wgt
    ii[0] = alt / 1024
    o["dft_i"] = rows(np.concatenate([ir, ii], 0).astype(f32), 4)
    ln = np.linspace(0.0, 1.0, 512, dtype=f32)[:, None]
    w = (2.0 * np.pi * np.arange(512)[:, None] / 512).astype(f32)
    fr = np.linspace(1e-4, 15, 16, dtype=f32)[None]
    o["zfeat"] = np.ascontiguousarray(np.concatenate([ln, np.cos(fr * w), -np.sin(fr * w)], 1).T.astype(f32))
    dl = np.abs(np.linspace(np.log(0.3) / 1e-2, np.log(1.5) / 1e-2, 1024, dtype=f32))
    o["decay"] = np.ascontiguousarray(np.exp(-ln * dl).astype(f32).reshape(4, 128, 1024).transpose(1, 0, 2))
    o["fw_out"] = np.ascontiguousarray(v["hy_fw_out_2"][0])
    fs = np.zeros((64, 256), f32)
    fs[0:33, 0:64] = v["hy_fw1_2"][0]
    fs[:, 64:128] = v["hy_fw2_2"][0]
    fs[:, 128:192] = v["hy_fw3_2"][0]
    for i, n in enumerate(("hy_fb1_2", "hy_fb2_2", "hy_fb3_2", "hy_freq_2")):
        fs[:, 192 + i] = v[n][0]
    o["fsmall"] = fs

    def feat(x):
        return np.ascontiguousarray(x.T.reshape(8, 128, -1).transpose(1, 0, 2))

    o["xt"] = feat(v["x"][0])
    o["memt"] = feat(v["mem"][0])
    o["pos"] = np.ascontiguousarray(np.broadcast_to(v["positions_2"], (128, 512)))
    i_, j_ = np.arange(128)[:, None], np.arange(128)[None]
    o["consts"] = np.concatenate([np.eye(128), np.where(j_ <= i_, 0.0, -1e30), (i_ <= j_) * 1.0,
                                  np.ones((128, 384))], 1).astype(f32)
    p = np.zeros((128, NPC), f32)

    def put(name, x):
        c = x.reshape(-1, 128).T
        p[:, POFF[name]:POFF[name] + c.shape[1]] = c

    for n, k in (("g_mix_pre", "norm_mix_pre"), ("g_mix_post", "norm_mix_post"), ("g_mem_pre", "norm_mem_pre"),
                 ("g_mem_post", "norm_mem_post"), ("g_memkv", "norm_memkv"), ("g_mlp_pre", "norm_mlp_pre"),
                 ("g_mlp_post", "norm_mlp_post"), ("conv_b", "conv_b"), ("cln_g", "conv_ln_g"),
                 ("cln_b", "conv_ln_b"), ("g_q", "mla_g_q_2"), ("g_kv", "mla_g_kv_2"), ("d_bias", "hy_d_bias_2")):
        put(n, v[k])
    put("conv_w", np.ascontiguousarray(v["conv_w"][0].reshape(31, 4, 128).transpose(1, 0, 2)))
    put("w_short", np.ascontiguousarray(v["hy_w_short_2"][0].reshape(3, 24, 128).transpose(1, 0, 2)))
    for l in range(2):
        put(f"ffn_conv{l}", np.ascontiguousarray(v["ffn_w_conv_2"][l].reshape(3, 44, 128).transpose(1, 0, 2)))
        for n in ("ln1_g", "ln1_b", "ln2_g", "ln2_b"):
            put(f"{n}{l}", v[f"{n}_2"][l])
    p[:, POFF["b_forget"]:POFF["b_forget"] + 8] = v["b_forget"]
    inv = (1.0 / (np.float32(10000.0) ** (np.arange(0, 64, 2, dtype=f32) / np.float32(64)))).astype(f32)
    p[:, POFF["inv"]] = np.tile(inv, 4)
    p[:, POFF["sgn"]] = np.where(np.arange(128) % 64 < 32, -1.0, 1.0)
    p[:, POFF["one"]] = 1.0
    p[:, POFF["eps6"]] = 1e-6
    p[:, POFF["eps5"]] = 1e-5
    p[:, POFF["halfpi"]] = HALF_PI
    o["par"] = p
    return o


def kernel(**inputs):
    import concourse.bacc as _bacc
    from concourse.bass_utils import run_bass_kernel_spmd as _run

    arrays = layout({k: np.asarray(a) for k, a in inputs.items()})
    nc = _bacc.Bacc("TRN2", target_bir_lowering=False, num_devices=1)
    t = {}
    for name, a in arrays.items():
        t[name] = nc.dram_tensor(f"in_{name}", a.shape, mybir.dt.from_np(a.dtype), kind="ExternalInput").ap()
    t["out"] = nc.dram_tensor("out_0", (128, 8, 512), F, kind="ExternalOutput").ap()
    t["kd"] = nc.dram_tensor("kd", (2, 9, 128, 1024), F, kind="Internal").ap()
    t["xd"] = nc.dram_tensor("xd", (128, 8, 512), F, kind="Internal").ap()
    build(nc, t)
    r = _run(nc, [{f"in_{n}": a for n, a in arrays.items()}], core_ids=[0])
    got = np.asarray(r.results[0]["out_0"])
    return np.ascontiguousarray(got.transpose(1, 0, 2).reshape(1024, 512).T)[None]
```

```python
from contextlib import ExitStack

import numpy as np

import concourse.bass as bass
from concourse import mybir

F = mybir.dt.float32
R = mybir.dt.float32r
I32 = mybir.dt.int32
ALU = mybir.AluOpType
ACT = mybir.ActivationFunctionType
AX = mybir.AxisListType.X

S = 512
D = 1024
ALPHA = float(np.float32((2.0 * 2) ** 0.25))
MAGIC = 12582912.0
TWO_PI = 6.283185307179586
C1 = 6.28125
C2 = 0.0019350051879882812
C3 = TWO_PI - C1 - C2
PI_IN = 3.1415925
HALF_PI = 1.5707963267948966


def tokens(waits):
    out = []
    for w in waits:
        if isinstance(w, list) or (isinstance(w, tuple) and not isinstance(w[-1], int)):
            out += tokens(w)
        elif w is not None:
            out.append(w)
    return out


class Engine:

    def __init__(self, sem):
        self.sem, self.count, self.ops = sem, 0, []

    def do(self, make, *waits, inc=True):
        self.ops.append([make, tokens(waits), False])
        return self.mark() if inc else None

    def mark(self):
        if not self.ops[-1][2]:
            self.ops[-1][2] = True
            self.count += 1
        return (self.sem, self.count)

    def issue(self, eng):
        seen = {}

        for make, waits, inc in self.ops:
            for sem, value in waits:
                if seen.get(id(sem), 0) < value:
                    eng.wait_ge(sem, value)
                    seen[id(sem)] = value
            ins = make(eng)
            if inc is True:
                ins.then_inc(self.sem, 1)


class Channel:

    def __init__(self, sem):
        self.sem, self.count = sem, 0


PCOLS = [("g_mix_pre", 8), ("g_mix_post", 8), ("g_mem_pre", 8), ("g_mem_post", 8), ("g_memkv", 8),
         ("g_mlp_pre", 8), ("g_mlp_post", 8), ("conv_w", 124), ("conv_b", 4), ("cln_g", 4), ("cln_b", 4),
         ("g_q", 3), ("g_kv", 2), ("w_short", 72), ("d_bias", 16), ("ffn_conv0", 132), ("ffn_conv1", 132),
         ("ln1_g0", 8), ("ln1_b0", 8), ("ln2_g0", 8), ("ln2_b0", 8),
         ("ln1_g1", 8), ("ln1_b1", 8), ("ln2_g1", 8), ("ln2_b1", 8), ("b_forget", 8),
         ("inv", 1), ("sgn", 1), ("one", 1), ("eps6", 1), ("eps5", 1), ("halfpi", 1)]
POFF, _at = {}, 0
for _n, _w in PCOLS:
    POFF[_n] = _at
    _at += _w
NPC = _at

CHUNKS = [
    ("dft_c", 0, 2048), ("dft_kx", 0, 512), ("dft_s", 0, 2048),
    ("dft_c", 0, 2048), ("dft_kx", 0, 512), ("dft_s", 0, 2048),
    *[("win_ag", i, 2048) for i in range(4)], ("win_f", 0, 64), *[("win_v", i, 2048) for i in range(2)],
    *[("win_qk", i, 2048) for i in range(4)],
    *[("w_out", i, 2048) for i in range(4)],
    *[("w_mk", i, 2048) for i in range(2)], *[("w_mv", i, 2048) for i in range(2)],
    *[("w_mq", i, 2048) for i in range(2)], *[("w_mo", i, 2048) for i in range(2)],
    *[("w_up", i, 2048) for i in range(16)], *[("w_down", i, 2048) for i in range(16)],
    *[("mla_in", i, 2048) for i in range(3)], ("mla_inx", 0, 1024),
]
for _p in range(4):
    CHUNKS += [("uq", _p, 1536), ("ukv", _p, 1024)]
CHUNKS += [("mla_o", i, 2048) for i in range(4)]
CHUNKS += [("up2_0", i, 2048) for i in range(22)] + [("down2_0", i, 2048) for i in range(11)]
CHUNKS += [("hy_in", i, 2048) for i in range(12)]
for _o in range(2):
    CHUNKS += [("dft_z", i, 1024) for i in range(4)] + [("dft_i", i, 2048) for i in range(2)]
CHUNKS += [("hy_o", i, 2048) for i in range(4)]
CHUNKS += [("up2_1", i, 2048) for i in range(22)] + [("down2_1", i, 2048) for i in range(11)]


def build(nc, t):
    es = ExitStack()
    BASE = 16512

    def sb(name, kb, shape, dt=F):
        return nc.alloc_sbuf_tensor_at(name, shape, dt, offset=BASE + int(kb * 1024))

    def sem(name):
        return es.enter_context(nc.semaphore(name))

    def chan(name):
        return Channel(sem(name))

    with es:
        psum = [es.enter_context(nc.psum_tensor(f"ps{i}", [128, 512], F)) for i in range(8)]
        pe, act, dve, pool, sp = (Engine(sem(n)) for n in ("s_pe", "s_act", "s_dve", "s_pool", "s_sp"))

        def dma(q, ch, dst, src, *waits):
            ch.count += 16
            sm = ch.sem
            q.ops.append([lambda e: e.dma_start(dst, src).then_inc(sm, 16), tokens(waits), None])
            return (ch.sem, ch.count)

        X = sb("X", 0, [128, 8, 512])
        W32 = [sb(f"W32_{i}", 16 + 8 * i, [128, 2048]) for i in range(3)]
        WH = [sb(f"WH{i}", 40 + 8 * i, [128, 2048], R) for i in range(2)]
        WL = [sb(f"WL{i}", 56 + 8 * i, [128, 2048], R) for i in range(2)]
        PAR = sb("PAR", 72, [128, NPC])
        IDT = sb("IDT", 75, [128, 128])
        ONE = sb("ONE", 75.5, [128, 128])
        IDR = sb("IDR", 76, [128, 128], R)
        MKR = sb("MKR", 76.5, [128, 128], R)
        SM = sb("SM", 77, [128, 256])
        TMP = [sb(f"TMP{i}", 78 + 2 * i, [128, 512]) for i in range(6)]
        A = 90

        ch_w = [chan(f"c_w{i}") for i in range(3)]
        ch_s = [chan(f"c_s{i}") for i in range(8)]
        ch_m = {}

        def once(name):
            ch_m[name] = chan("c_" + name)
            return ch_m[name]

        stores = []

        free = [[] for _ in range(8)]
        turn = [0]

        held = set()

        def bank(hold=False):
            while turn[0] % 8 in held:
                turn[0] += 1
            i = turn[0] % 8
            turn[0] += 1
            if hold:
                held.add(i)
            return i, psum[i], free[i]

        def give(i, toks):
            free[i] = toks
            held.discard(i)

        later = []

        def run_later(keep=0):
            while len(later) > keep:
                later.pop(0)()

        tfree = [[] for _ in range(4)]
        tturn = [0]
        tpend = set()

        def tmp():
            if len(tpend) == 4:
                run_later()
            while tturn[0] % 4 in tpend:
                tturn[0] += 1
            k = tturn[0] % 4
            tturn[0] += 1
            return k, TMP[k], tfree[k]

        taps = []

        def run_taps(n):
            for _ in range(min(n, len(taps))):
                taps.pop(0)()

        wst = {"dma": 0, "split": 0, "get": 0}
        w_split = []
        w_used = []

        def w_dma():
            n = wst["dma"]
            if n >= len(CHUNKS):
                return
            name, i, cols = CHUNKS[n]
            s = n % 3
            wst["dma"] += 1
            w_split.append([dma(sp, ch_w[s], W32[s][:, 0:cols], t[name][i], w_split[n - 3] if n >= 3 else None)])

        def w_do_split():
            n = wst["split"]
            if n >= len(CHUNKS):
                return
            cols = CHUNKS[n][2]
            s, r = n % 3, n % 2
            landed = w_split[n][0]
            used = w_used[n - 2] if n >= 2 else None
            src, hi, lo = W32[s][:, 0:cols], WH[r][:, 0:cols], WL[r][:, 0:cols]
            a = act.do(lambda e: e.activation(hi, src, ACT.Copy), landed, used)
            b = pool.do(lambda e: e.tensor_tensor(lo, src, hi.bitcast(F), ALU.subtract), landed, used, a)
            w_split[n] = [a, b]
            wst["split"] += 1
            w_dma()

        def w_get(name):
            n = wst["get"]
            assert CHUNKS[n][0] == name, (CHUNKS[n], name)
            if wst["split"] <= n:
                w_do_split()
            if wst["split"] <= n + 1:
                w_do_split()
            wst["get"] += 1
            r = n % 2
            return WH[r], WL[r], w_split[n]

        def w_release():
            w_used.append(pe.mark())

        def mm(out, l, r, start, stop, *waits):
            pe.do(lambda e: e.matmul(out, l, r, start=start, stop=stop), *waits, inc=False)

        def mm3(out, lh, ll, rh, rl, first, last, *waits):
            mm(out, ll, rh, first, False, *waits)
            mm(out, lh, rl, False, False)
            mm(out, lh, rh, False, last)

        def cp(out, src, *w, scale=1.0):
            return act.do(lambda e: e.activation(out, src, ACT.Copy, scale=scale), *w)

        def tt(out, a, b, op, *w):
            return dve.do(lambda e: e.tensor_tensor(out, a, b, op), *w)

        def ts(out, a, s1, s2, o1, o2, *w):
            if s2 is None:
                return dve.do(lambda e: e.tensor_scalar(out, a, s1, None, o1), *w)
            return dve.do(lambda e: e.tensor_scalar(out, a, s1, s2, o1, o2), *w)

        def stt(out, a, s, b, o1, o2, *w):
            return dve.do(lambda e: e.scalar_tensor_tensor(out=out, in0=a, scalar=s, in1=b, op0=o1, op1=o2), *w)

        def af(out, src, fn, *w, scale=1.0, bias=0.0):
            return act.do(lambda e: e.activation(out, src, fn, scale=scale, bias=bias), *w)

        def split(src, hi, lo, *w, scale=None):
            a = cp(hi, src, *w, scale=1.0 if scale is None else scale)
            if scale is None:
                b = tt(lo, src, hi.bitcast(F), ALU.subtract, *w, a)
            else:
                b = stt(lo, src, scale, hi.bitcast(F), ALU.mult, ALU.subtract, *w, a)
            return [a, b]

        def par(name, i=0, p=slice(0, 128)):
            c = POFF[name] + i
            return PAR[p, c:c + 1]

        k_par = dma(sp, once("par"), PAR[:], t["par"])
        k_id = dma(sp, once("idt"), IDT[:], t["consts"][:, 0:128])
        k_mk = dma(sp, once("mk"), TMP[0][:, 0:128], t["consts"][:, 128:256])
        k_one = dve.do(lambda e: e.memset(ONE[:], 1.0))
        c_idr = cp(IDR[:], IDT[:], k_id)
        c_mkr = cp(MKR[:], TMP[0][:, 0:128], k_mk)
        consts = [k_par, k_id, k_one, c_idr, c_mkr]
        for e in (pe, act, dve, pool):
            e.ops.append([lambda g: None, tokens(consts), None])

        FW = sb("FW", A, [64, 4096])
        WPH = sb("WPH", A + 16, [64, 2048], R)
        WPL = sb("WPL", A + 24, [64, 2048], R)
        HPH = sb("HPH", A + 32, [128, 2, 4, 1024], R)
        HPL = sb("HPL", A + 64, [128, 2, 4, 1024], R)
        DEC = sb("DEC", A + 96, [128, 4, 1024])
        H3H = sb("H3H", A + 112, [64, 512], R)
        H3L = sb("H3L", A + 114, [64, 512], R)
        ZF = TMP[1]
        k_zf = dma(sp, once("zf"), ZF[0:33, :], t["zfeat"])
        k_f1 = dma(sp, once("f1"), SM[0:64, :], t["fsmall"])
        k_fw = dma(sp, once("fw"), FW[:], t["fw_out"])
        w_dma()
        k_dec = dma(sp, once("dec"), DEC[:], t["decay"])
        w_dma()
        w_dma()

        def sin_of(dst, arg, P, *w):
            kq = TMP[4][0:P, :]
            a = ts(kq, arg, 1.0 / TWO_PI, MAGIC, ALU.mult, ALU.add, *w)
            a = ts(kq, kq, MAGIC, None, ALU.subtract, None, a)
            for c in (C1, C2, C3):
                a = stt(arg, kq, -c, arg, ALU.mult, ALU.add, a)
            a = ts(arg, arg, PI_IN, -PI_IN, ALU.min, ALU.max, a)
            return af(dst, arg, ACT.Sin, a), a

        hin, hw = ZF[0:33, :], [k_zf]
        for layer in range(3):
            i, ps, fr = bank()
            lhs = SM[0:33, 0:64] if layer == 0 else SM[0:64, 64 * layer:64 * layer + 64]
            mm(ps[0:64, :], lhs, hin, True, True, fr, k_f1, *hw)
            m = pe.mark()
            arg = TMP[2 + layer % 2][0:64, :]
            a = ts(arg, ps[0:64, :], SM[0:64, 192 + layer:193 + layer], SM[0:64, 195:196], ALU.add, ALU.mult, m)
            free[i] = [a]
            s, _ = sin_of(arg, arg, 64, a)
            hin, hw = arg, [s]
        h3 = split(hin, H3H[:], H3L[:], *hw)
        for k in range(4):
            tfree[k] = [h3, c_mkr]
        KD = t["kd"]
        stage = [None] * 8
        sturn = [0]
        wp = [[], []]
        hp_used = [[], []]
        hpt = [[], []]

        def make_w(sgn, o):
            c0 = 2048 * o
            new = []
            for c in range(2):
                f_ = FW[:, c0 + 512 * c:c0 + 512 * c + 512]
                b_ = FW[:, c0 + 1024 + 512 * c:c0 + 1024 + 512 * c + 512]
                q = 1024 * sgn + 512 * c
                k, tm, tf = tmp()
                a = tt(tm[0:64, :], f_, b_, ALU.subtract if sgn else ALU.add, k_fw, tf)
                x = split(tm[0:64, :], WPH[:, q:q + 512], WPL[:, q:q + 512], a, hpt[sgn])
                tfree[k] = [x]
                new.append(x)
            wp[sgn] = new

        def make_h(sgn, tb):
            for c in range(2):
                i, ps, fr = bank()
                q = 1024 * sgn + 512 * c
                tsl = slice(128 * tb, 128 * tb + 128)
                csl = slice(512 * c, 512 * c + 512)
                mm3(ps[:], H3H[:, tsl], H3L[:, tsl], WPH[:, q:q + 512], WPL[:, q:q + 512], True, True,
                    fr, h3, wp[sgn])
                k, tm, tf = tmp()
                a = tt(tm[:], ps[:], DEC[:, tb, csl], ALU.mult, pe.mark(), k_dec, tf)
                free[i] = [a]
                x = split(tm[:], HPH[:, sgn, tb, csl], HPL[:, sgn, tb, csl], a, hp_used[sgn])
                tfree[k] = [x]
                hpt[sgn].append(x)

        def spectrum(o, part, nm, wh, wl, wt, row0, between):
            for m_ in range(nm):
                for c in range(2):
                    i, ps, fr = bank()
                    csl = slice(512 * c, 512 * c + 512)
                    for kt in range(4):
                        col = kt * 128 * nm + 128 * m_
                        mm3(ps[:], wh[:, col:col + 128], wl[:, col:col + 128], HPH[:, part, kt, csl],
                            HPL[:, part, kt, csl], kt == 0, kt == 3, fr, wt, hpt[part])
                    k = sturn[0] % 8
                    sturn[0] += 1
                    a = cp(X[:, k, :], ps[:], pe.mark(), stage[k])
                    free[i] = [a]
                    stage[k] = dma(sp, ch_s[k], KD[o, row0 + 2 * m_, :, csl], X[:, k, :], a)
                if between is not None:
                    between(m_)

        make_w(0, 0)
        make_w(1, 0)
        for tb in range(4):
            make_h(0, tb)
        for o in range(2):
            wh, wl, wt = w_get("dft_c")
            if o == 0:
                spectrum(o, 0, 4, wh, wl, wt, 0, lambda m_: make_h(1, m_))
            else:
                make_w(1, 1)
                hpt[1] = []
                spectrum(o, 0, 4, wh, wl, wt, 0, lambda m_: make_h(1, m_))
            w_release()
            wh, wl, wt = w_get("dft_kx")
            spectrum(o, 0, 1, wh, wl, wt, 8, None)
            w_release()
            hp_used[0] = [pe.mark()]
            wh, wl, wt = w_get("dft_s")
            if o == 0:
                make_w(0, 1)
                hpt[0] = []
            spectrum(o, 1, 4, wh, wl, wt, 1, (lambda m_: make_h(0, m_)) if o == 0 else None)
            w_release()
            hp_used[1] = [pe.mark()]
        kd_done = list(stage)
        stores += kd_done
        hp_used = [pe.mark()]

        def gemm_t(name, nchunk, KT, MT, acts, atoks, evac, N=512, korder=None, base=0, lag=0, head=True):
            ah, al = acts
            ko = korder or list(range(KT))

            def step(ps, fr, m_, k, wh, wl, wt):
                col = (k * MT + m_) * 128
                mm3(ps[:, 0:N], wh[:, col:col + 128], wl[:, col:col + 128], ah[:, k, 0:N], al[:, k, 0:N],
                    k == ko[0], k == ko[-1], fr, wt, atoks[k])

            for c in range(nchunk):
                wh, wl, wt = w_get(name)
                if c == 0 and head:
                    bs = [bank(hold=True) for _ in range(MT)]
                    for k in ko:
                        for m_ in range(MT):
                            step(bs[m_][1], bs[m_][2], m_, k, wh, wl, wt)
                            if k == ko[-1]:
                                give(bs[m_][0], evac(base + m_, bs[m_][1], pe.mark()))
                        if k != ko[-1] and later:
                            later.pop(0)()
                else:
                    for m_ in range(MT):
                        i, ps, fr = bank()
                        for k in ko:
                            step(ps, fr, m_, k, wh, wl, wt)
                        free[i] = evac(base + c * MT + m_, ps, pe.mark())
                        run_later(lag)
                w_release()
            run_later()

        dg_used = [None]

        class ColSum:

            def __init__(self, n, N=S):
                self.n, self.nb, self.k = n, N // 128, 0
                self.bank = None

            def add(self, ap, *w):
                if self.bank is None:
                    self.bank = bank(hold=True)
                i, ps, fr = self.bank
                last = self.k == self.n - 1
                for b in range(self.nb):
                    st, l, o = self.k == 0 and b == 0, ap[:, 128 * b:128 * b + 128], ps[:, b:b + 1]
                    pe.do(lambda e, o=o, l=l, st=st: e.matmul(o, l, ONE[:, 0:1], start=st, stop=last,
                                                              skip_group_check=True), fr, *w, inc=False)
                self.k += 1
                return pe.mark()

            def finish(self, scale, eps, slot):
                i, ps, _ = self.bank
                m = pe.mark()
                v, r = SM[:, slot:slot + self.nb], SM[:, slot + 4:slot + 4 + self.nb]
                if eps is None:
                    a = a2 = ts(r, ps[:, 0:self.nb], scale, None, ALU.mult, None, m)
                else:
                    a = af(v, ps[:, 0:self.nb], ACT.Sqrt, m, scale=scale, bias=par(eps))
                    a2 = dve.do(lambda e: e.reciprocal(r, v), a)
                give(i, [a])
                return a2

        def spread(slot, N, tok, out=None):
            nb = N // 128
            dg = TMP[5]
            d = [ts(dg[:, 128 * b:128 * b + 128], IDT[:], SM[:, slot + 4 + b:slot + 5 + b], None,
                    ALU.mult, None, tok, dg_used[0]) for b in range(nb)]
            i, ps, fr = bank(hold=True)
            mm(ps[:, 0:N], ONE[:], dg[:, 0:N], True, True, fr, *d)
            m = dg_used[0] = pe.mark()
            if out is None:
                return i, ps, m
            o = cp(out, ps[:, 0:N], m, d)
            give(i, [o])
            return o

        RS = TMP[4]
        HH = sb("HH", A, [128, 8, 512], R)
        HL = sb("HL", A + 16, [128, 8, 512], R)

        def gain_split(src, g, hi, lo, *w):
            a = act.do(lambda e: e.activation(hi, src, ACT.Identity, scale=g), *w)
            b = stt(lo, src, g, hi.bitcast(F), ALU.mult, ALU.subtract, *w, a)
            return [a, b]

        xt = []
        xs = ColSum(8)
        ht = []
        for k in range(8):
            kx = dma(sp, ch_s[k], X[:, k, :], t["xt"][:, k, :], stage[k])
            xt.append([kx])
            ht.append(gain_split(X[:, k, :], par("g_mix_pre", k), HH[:, k, :], HL[:, k, :], kx, hp_used))
            q, tm, tf = tmp()
            a = af(tm[:], X[:, k, :], ACT.Square, kx, tf)

            def add(tm=tm, a=a, q=q):
                tfree[q] = [xs.add(tm, a)]

            add()
        rr = xs.finish(1.0 / D, "eps6", 0)
        rs = spread(0, S, rr, RS[:])

        QH = sb("QH", A + 32, [128, 4, 512], R)
        QL = sb("QL", A + 40, [128, 4, 512], R)
        KH = sb("KH", A + 48, [128, 4, 512], R)
        KL = sb("KL", A + 56, [128, 4, 512], R)
        VH = sb("VH", A + 64, [128, 4, 512], R)
        VL = sb("VL", A + 72, [128, 4, 512], R)
        U = sb("U", A + 80, [128, 4, 542])
        CO = sb("CO", A + 89, [128, 4, 512])
        PP = sb("PP", A + 97, [128, 4, 512])
        ATP = sb("ATP", A + 105, [128, 4, 256])
        QA = sb("QA", A + 109, [128, 2, 512], R)
        KA = sb("KA", A + 113, [128, 2, 512], R)
        z_u = dve.do(lambda e: e.memset(U[:, :, 0:30], 0.0), hp_used)
        conv_t = [None] * 4
        sg = {}

        def tap(j, w_):
            if w_ == 0:
                conv_t[j] = ts(CO[:, j, :], U[:, j, 0:512], par("conv_w", 31 * j), par("conv_b", j),
                               ALU.mult, ALU.add, z_u, conv_t[j])
            else:
                conv_t[j] = stt(CO[:, j, :], U[:, j, w_:w_ + 512], par("conv_w", 31 * j + w_), CO[:, j, :],
                                ALU.mult, ALU.add, conv_t[j])

        def ev_ag(n, ps, m):
            j = n // 2
            if n % 2 == 0:
                k, tm, tf = tmp()
                a = tt(tm[:], ps[:], RS[:], ALU.mult, m, rs, tf)
                b = af(tm[:], tm[:], ACT.Sigmoid, a)
                c = pool.do(lambda e: e.tensor_tensor(tm[:], tm[:], RS[:], ALU.mult), b, rs)
                sg["k"], sg["tm"], sg["c"] = k, tm, c
                run_taps(6)
                return [a]
            a = tt(U[:, j, 30:542], ps[:], sg["tm"][:], ALU.mult, m, sg["c"], hp_used)
            tfree[sg["k"]] = [a]
            conv_t[j] = a
            for w_ in range(31):
                taps.append(lambda w_=w_: tap(j, w_))
            run_taps(6)
            return [a]

        gemm_t("win_ag", 4, 8, 2, (HH, HL), ht, ev_ag)
        wh, wl, wt = w_get("win_f")
        i, ps, fr = bank()
        for b in range(4):
            for k in range(8):
                bs = slice(128 * b, 128 * b + 128)
                mm3(ps[:, 8 * b:8 * b + 8], HH[:, k, bs], HL[:, k, bs], wh[:, 8 * k:8 * k + 8], wl[:, 8 * k:8 * k + 8],
                    k == 0, k == 7, fr, wt, ht)
        w_release()
        m = pe.mark()
        z, e1, e2, lf = (SM[:, 32 * q:32 * q + 32] for q in range(1, 5))
        bf = PAR[:, POFF["b_forget"]:POFF["b_forget"] + 8]
        zt = [stt(SM[:, 32 + 8 * b:40 + 8 * b], ps[:, 8 * b:8 * b + 8], SM[:, 4 + b:5 + b], bf, ALU.mult, ALU.add,
                  m, rr) for b in range(4)]
        free[i] = zt
        a = af(e1, z, ACT.Abs, *zt)
        a = af(e1, e1, ACT.Exp, a, scale=-1.0)
        a = af(e1, e1, ACT.Ln, a, bias=par("one"))
        b_ = ts(e2, z, 0.0, None, ALU.min, None, *zt)
        lft = tt(lf, e2, e1, ALU.subtract, a, b_)
        vb = [bank() for _ in range(4)]
        vt = []
        for c in range(2):
            wh, wl, wt = w_get("win_v")
            for b in range(4):
                for k in range(4):
                    kk = 4 * c + k
                    bs = slice(128 * b, 128 * b + 128)
                    mm3(vb[b][1][:], HH[:, kk, bs], HL[:, kk, bs], wh[:, 512 * k:512 * k + 512],
                        wl[:, 512 * k:512 * k + 512], kk == 0, kk == 7, vb[b][2], wt, ht)
                if c == 1:
                    free[vb[b][0]] = gain_split(vb[b][1][:], SM[:, 4 + b:5 + b], VH[:, b, :], VL[:, b, :], pe.mark(),
                                                hp_used, rr)
                    vt.append(free[vb[b][0]])
                run_taps(5)
            w_release()
        TRI = TMP[5]
        k_tri = dma(sp, once("tri"), TRI[:], t["consts"][:, 256:768], dg_used[0])
        i, ps, fr = bank()
        for k in range(4):
            mm(ps[0:8, 128 * k:512], SM[:, 128 + 8 * k:136 + 8 * k], TRI[:, 0:512 - 128 * k], k == 0, k == 3,
               fr, lft, k_tri)
        m = pe.mark()
        dg_used[0] = m
        CH = sb("CH", A + 97, [8, 512], R)
        CL = sb("CL", A + 99, [8, 512], R)
        NH = sb("NH", A + 101, [8, 512], R)
        NL = sb("NL", A + 103, [8, 512], R)
        c_ = split(ps[0:8, :], CH[:], CL[:], m, hp_used)
        free[i] = c_
        n1 = cp(NH[:], CH[:].bitcast(F), *c_, scale=-1.0)
        n2 = cp(NL[:], CL[:].bitcast(F), *c_, scale=-1.0)
        o1 = pool.do(lambda e: e.memset(QA[:].bitcast(F), 1.0), hp_used)
        o2 = pool.do(lambda e: e.memset(KA[:].bitcast(F), 1.0), hp_used)
        augt = []
        for q, (dst, src, row) in enumerate([(QA, CH, 0), (QA, CL, 1), (KA, NH, 2), (KA, NL, 3)]):
            for g in range(2):
                augt.append(dma(sp, once(f"aug{q}{g}"), dst[row:row + 97:32, g, :].bitcast(F),
                                src[4 * g:4 * g + 4, :].bitcast(F), *c_, n1, n2, o1, o2))
        qkt = []

        def ev_qk(n, ps, m):
            j = n // 2
            k, tm, tf = tmp()
            a = stt(tm[:], ps[:], 1.0 if n % 2 else 0.125, RS[:], ALU.mult, ALU.mult, m, rs, tf)
            hi, lo = (KH, KL) if n % 2 else (QH, QL)
            r = split(tm[:], hi[:, j, :], lo[:, j, :], a, hp_used)
            tfree[k] = r
            qkt.append(r)
            run_taps(5)
            return [a]

        def qk_pair(j):
            gemm_t("win_qk", 1, 8, 2, (HH, HL), ht, ev_qk, base=2 * j, head=False)

        PTH = sb("PTH", A, [128, 4, 512], R)
        PTL = sb("PTL", A + 16, [128, 4, 512], R)

        def logits_softmax(i_, ps, nk, m, scale, Pt, slot, pfree):
            mx = SM[:, slot + i_:slot + i_ + 1]
            sm_ = SM[:, slot + 4 + i_:slot + 5 + i_]
            rc = SM[:, slot + 8 + i_:slot + 9 + i_]
            a = dve.do(lambda e: e.reduce_max(mx, ps[:, 0:nk], AX), m, pfree)
            b = ts(mx, mx, -scale, None, ALU.mult, None, a)
            c = act.do(lambda e: e.activation(Pt, ps[:, 0:nk], ACT.Exp, bias=mx, scale=scale, accum_out=sm_), b, pfree)
            d = dve.do(lambda e: e.reciprocal(rc, sm_), c)
            return c, d

        fx = {"p": [], "pv": []}
        cat = [None] * 8
        h_dead = []

        def fox_s(h):
            pb, j = 64 * (h % 2), h // 2
            ab, g = 32 * (h % 4), h // 4
            out = []
            for i_ in range(4):
                nk = 128 * (i_ + 1)
                bi, ps, fr = bank()
                qs = slice(128 * i_, 128 * i_ + 128)
                mm3(ps[:, 0:nk], QH[pb:pb + 64, j, qs], QL[pb:pb + 64, j, qs], KH[pb:pb + 64, j, 0:nk],
                    KL[pb:pb + 64, j, 0:nk], True, False, fr, qkt[2 * j], qkt[2 * j + 1])
                mm(ps[:, 0:nk], QA[ab:ab + 4, g, qs], KA[ab:ab + 4, g, 0:nk], False, False, augt)
                mm(ps[:, nk - 128:nk], IDR[:], MKR[:], False, True)
                c, d = logits_softmax(i_, ps, nk, pe.mark(), 1.0, PP[:, i_, 0:nk], 32 * (h % 2) + 160, fx["p"] + augt)
                free[bi] = [c]
                out.append((c, d))
            return out

        atd = [None]

        def fox_t(h, sm_):
            bl = []
            for j in range(4):
                bi, ps, fr = bank()
                for i_ in range(j, 4):
                    o = ps[:, 128 * i_:128 * i_ + 128]
                    src = PP[:, i_, 128 * j:128 * j + 128]
                    pe.do(lambda e, o=o, src=src: e.transpose(o, src, IDT[:]), fr, sm_[i_][0], inc=False)
                m = pe.mark()
                sp_ = split(ps[:, 128 * j:512], PTH[:, j, 128 * j:512], PTL[:, j, 128 * j:512], m, fx["pv"], h_dead)
                free[bi] = sp_
                bl.append(sp_)
            fx["p"] = [pe.mark()]
            return bl

        def fox_pv(h, bl, sm_):
            bi, ps, fr = bank()
            hs = slice(64 * h, 64 * h + 64)
            for i_ in range(4):
                for j in range(i_ + 1):
                    q = slice(128 * i_, 128 * i_ + 128)
                    mm3(ps[:, 64 * i_:64 * i_ + 64], PTH[:, j, q], PTL[:, j, q], VH[:, j, hs], VL[:, j, hs],
                        j == 0, j == i_, fr, bl, vt)
            m = pe.mark()
            fx["pv"] = [m]
            slot = 32 * (h % 2) + 160 + 8
            o = []
            for i_ in range(4):
                dst = ATP[:, i_, 64 * (h % 2):64 * (h % 2) + 64]
                o.append(ts(dst, ps[:, 64 * i_:64 * i_ + 64], SM[:, slot + i_:slot + i_ + 1], None, ALU.mult, None,
                            m, sm_[i_][1], atd[0]))
            free[bi] = o
            if h % 2 == 0:
                fx["o"] = o
                return
            oo = fx["o"] + o

            def turn_pair():
                bi, ps, fr = bank()
                for i_ in range(4):
                    dst, src = ps[:, 128 * i_:128 * i_ + 128], ATP[:, i_, 0:128]
                    pe.do(lambda e, dst=dst, src=src: e.transpose(dst, src, IDT[:]), fr, oo, inc=False)
                atd[0] = pe.mark()
                j = 4 + h // 2
                sp_ = split(ps[:], HH[:, j, :], HL[:, j, :], atd[0], h_dead)
                free[bi] = sp_
                cat[j] = sp_

            later.append(turn_pair)

        for j in range(4):
            qk_pair(j)
        h_dead = [pe.mark()]
        smx = fox_s(0)
        lnst = {}
        for h in range(8):
            bl = fox_t(h, smx)
            run_taps(6)
            nxt = fox_s(h + 1) if h < 7 else None
            run_later()
            fox_pv(h, bl, smx)
            run_taps(6)
            smx = nxt
            if h == 4:
                run_taps(200)
                cs = ColSum(4)
                for j in range(4):
                    cs.add(CO[:, j, :], conv_t[j])
                r_ = cs.finish(1.0 / 512, None, 8)
                bi, mps, mtok = spread(8, S, r_)
                xc = [tt(CO[:, j, :], CO[:, j, :], mps[:], ALU.subtract, mtok) for j in range(4)]
                give(bi, xc)
            if h == 5:
                cs = ColSum(4)
                for j in range(4):
                    k, tm, tf = tmp()
                    a = af(tm[:], CO[:, j, :], ACT.Square, xc[j], tf)
                    tfree[k] = [cs.add(tm, a)]
                r_ = cs.finish(1.0 / 512, "eps6", 16)
                bi, mps, mtok = spread(16, S, r_)
                xc = [tt(CO[:, j, :], CO[:, j, :], mps[:], ALU.mult, mtok) for j in range(4)]
                give(bi, xc)
        run_later()
        for j in range(4):
            a = af(CO[:, j, :], CO[:, j, :], ACT.Silu, xc[j], scale=par("cln_g", j), bias=par("cln_b", j))
            cat[j] = split(CO[:, j, :], HH[:, j, :], HL[:, j, :], a, fx["pv"])

        def y_evac(Y, ys, *w):
            toks = []

            def ev(n, ps, m):
                a = cp(Y[:, n, :], ps[:], m, *w)
                k, tm, tf = tmp()
                b = af(tm[:], ps[:], ACT.Square, m, tf)
                tpend.add(k)

                def add():
                    tfree[k] = [ys.add(tm, b)]
                    tpend.discard(k)

                later.append(add)
                toks.append([a])
                return [b]

            return ev, toks

        def post(Y, yt, ys, g, g2, *w):
            nonlocal xt
            r_ = ys.finish(1.0 / D, "eps6", 8)
            bi, rps, rtok = spread(8, S, r_)
            xn, hn = [], []
            st = ColSum(8)
            a = [None] * 8
            lo = [None] * 8

            def first(k):
                a[k] = stt(Y[:, k, :], Y[:, k, :], par(g, k), rps[:], ALU.mult, ALU.mult, rtok, yt[k])

            def second(k):
                b = pool.do(lambda e: e.tensor_tensor(X[:, k, :], X[:, k, :], Y[:, k, :], ALU.add), a[k], xt[k])
                xn.append([b])
                hi = HH[:, k, :]
                if g2 is None:
                    c = cp(hi, X[:, k, :], b, *w)
                else:
                    c = act.do(lambda e: e.activation(hi, X[:, k, :], ACT.Identity, scale=par(g2, k)), b, *w)
                    q = af(Y[:, k, :], X[:, k, :], ACT.Square, b)
                    later.append(lambda: st.add(Y[:, k, :], q))
                lo[k] = c

            def third(k):
                if g2 is None:
                    d = tt(HL[:, k, :], X[:, k, :], HH[:, k, :].bitcast(F), ALU.subtract, lo[k])
                else:
                    d = stt(HL[:, k, :], X[:, k, :], par(g2, k), HH[:, k, :].bitcast(F), ALU.mult, ALU.subtract, lo[k])
                hn.append([lo[k], d])

            for k in range(10):
                if k < 8:
                    first(k)
                    second(k)
                if k >= 2:
                    third(k - 2)
            give(bi, [a[7]])
            xt = xn
            return hn, st

        Y1 = sb("Y1", A + 101, [128, 8, 512])
        MX = sb("MX", A + 32, [128, 8, 256])
        HMH = sb("HMH", A + 40, [128, 8, 256], R)
        HML = sb("HML", A + 48, [128, 8, 256], R)
        KMH = sb("KMH", A + 56, [128, 4, 256], R)
        KML = sb("KML", A + 60, [128, 4, 256], R)
        VMH = sb("VMH", A + 64, [128, 2, 512], R)
        VML = sb("VML", A + 68, [128, 2, 512], R)
        QMH = sb("QMH", A + 72, [128, 4, 512], R)
        QML = sb("QML", A + 80, [128, 4, 512], R)
        PM = sb("PM", A + 88, [128, 4, 256])
        PMH = sb("PMH", A + 92, [128, 2, 512], R)
        PML = sb("PML", A + 96, [128, 2, 512], R)
        OMH = sb("OMH", A + 100, [128, 4, 512], R)
        OML = sb("OML", A + 108, [128, 4, 512], R)
        att_done = [pe.mark()]
        k_m = dma(sp, once("mem"), MX[:], t["memt"], att_done)
        ys = ColSum(8)
        ev, yt = y_evac(Y1, ys, att_done, xc)
        ms = ColSum(8, 256)
        hmt = []

        def mem_norm():
            for k in range(8):
                q, tm, tf = tmp()
                a = af(tm[:, 0:256], MX[:, k, :], ACT.Square, k_m, tf)
                tfree[q] = [ms.add(tm, a)]
            r_ = ms.finish(1.0 / D, "eps6", 24)
            mrs = spread(24, 256, r_, RS[:, 0:256])
            for k in range(8):
                q, tm, tf = tmp()
                a = stt(tm[:, 0:256], MX[:, k, :], par("g_memkv", k), RS[:, 0:256], ALU.mult, ALU.mult, mrs, tf)
                tfree[q] = split(tm[:, 0:256], HMH[:, k, :], HML[:, k, :], a, att_done)
                hmt.append(tfree[q])

        def ev_w_out(n, ps, m):
            r = ev(n, ps, m)
            if n == 3:
                later.append(mem_norm)
            return r

        gemm_t("w_out", 4, 8, 2, (HH, HL), cat, ev_w_out, korder=[4, 5, 6, 7, 0, 1, 2, 3])
        h_dead = [pe.mark()]
        ht, st = post(Y1, yt, ys, "g_mix_post", "g_mem_pre", h_dead)
        kmt = []

        def ev_km(n, ps, m):
            r = split(ps[:, 0:256], KMH[:, n, :], KML[:, n, :], m)
            kmt.append(r)
            return r

        hold_later, later[:] = later[:], []
        gemm_t("w_mk", 2, 8, 2, (HMH, HML), hmt, ev_km, N=256)
        later[:] = hold_later
        vb = [bank() for _ in range(2)]
        vmt = []
        for c in range(2):
            wh, wl, wt = w_get("w_mv")
            for b in range(2):
                for k in range(4):
                    kk = 4 * c + k
                    bs = slice(128 * b, 128 * b + 128)
                    mm3(vb[b][1][:], HMH[:, kk, bs], HML[:, kk, bs], wh[:, 512 * k:512 * k + 512],
                        wl[:, 512 * k:512 * k + 512], kk == 0, kk == 7, vb[b][2], wt, hmt)
                if c == 1:
                    free[vb[b][0]] = split(vb[b][1][:], VMH[:, b, :], VML[:, b, :], pe.mark())
                    vmt.append(free[vb[b][0]])
            w_release()
        run_later()
        rr = st.finish(1.0 / D, "eps6", 0)
        rs = spread(0, S, rr, RS[:])
        qmt = []
        MS = float(128.0 ** -0.5)
        mfx = {"p": [], "pv": []}

        def ev_scaled(dsts):
            def ev(n, ps, m):
                k, tm, tf = tmp()
                a = tt(tm[:], ps[:], RS[:], ALU.mult, m, rs, tf)
                r = split(tm[:], dsts[0][:, n, :], dsts[1][:, n, :], a)
                tfree[k] = r
                qmt.append(r)
                return [a]
            return ev

        def mem_s(h):
            out = []
            for i_ in range(4):
                bi, ps, fr = bank()
                qs = slice(128 * i_, 128 * i_ + 128)
                mm3(ps[:, 0:256], QMH[:, h, qs], QML[:, h, qs], KMH[:, h, :], KML[:, h, :], True, True, fr,
                    qmt[h], kmt[h])
                slot = 32 * (h % 2) + 160
                c, d = logits_softmax(i_, ps, 256, pe.mark(), MS, PM[:, i_, :], slot, mfx["p"])
                free[bi] = [c]
                out.append([ts(PM[:, i_, :], PM[:, i_, :], SM[:, slot + 8 + i_:slot + 9 + i_], None, ALU.mult, None,
                               c, d)])
            return out

        def mem_t(h, sm_):
            bl = []
            for j in range(2):
                bi, ps, fr = bank()
                for i_ in range(4):
                    o, src = ps[:, 128 * i_:128 * i_ + 128], PM[:, i_, 128 * j:128 * j + 128]
                    pe.do(lambda e, o=o, src=src: e.transpose(o, src, IDT[:]), fr, sm_[i_], inc=False)
                sp_ = split(ps[:], PMH[:, j, :], PML[:, j, :], pe.mark(), mfx["pv"])
                free[bi] = sp_
                bl.append(sp_)
            mfx["p"] = [pe.mark()]
            return bl

        omt = []

        def mem_pv(h, bl):
            bi, ps, fr = bank()
            hs = slice(128 * h, 128 * h + 128)
            for j in range(2):
                mm3(ps[:], VMH[:, j, hs], VML[:, j, hs], PMH[:, j, :], PML[:, j, :], j == 0, j == 1, fr, bl, vmt)
            mfx["pv"] = [pe.mark()]
            free[bi] = split(ps[:], OMH[:, h, :], OML[:, h, :], mfx["pv"], xt)
            omt.append(free[bi])

        ev = ev_scaled((QMH, QML))
        gemm_t("w_mq", 1, 8, 2, (HH, HL), ht, ev)
        smx = mem_s(0)
        gemm_t("w_mq", 1, 8, 2, (HH, HL), ht, ev, base=2, head=False)
        for h in range(4):
            bl = mem_t(h, smx)
            nxt = mem_s(h + 1) if h < 3 else None
            mem_pv(h, bl)
            smx = nxt
        h_dead = [pe.mark()]
        Y2 = sb("Y2", A + 32, [128, 8, 512])
        ys = ColSum(8)
        ev, yt = y_evac(Y2, ys, h_dead)
        gemm_t("w_mo", 2, 4, 4, (OMH, OML), omt, ev, lag=1)
        mo_dead = [pe.mark()]
        ht, st = post(Y2, yt, ys, "g_mem_post", "g_mlp_pre", h_dead)

        MID = sb("MID", A + 32, [128, 32, 512])
        MRH = [sb(f"MRH{i}", A + 96 + 2 * i, [128, 512], R) for i in range(5)]
        MRL = [sb(f"MRL{i}", A + 106 + 2 * i, [128, 512], R) for i in range(5)]
        mid = []
        mlp = {}

        def ev_up(n, ps, m):
            if n == 0:
                run_later()
                mlp["rr"] = st.finish(1.0 / D, "eps6", 0)
                mlp["rs"] = spread(0, S, mlp["rr"], RS[:])
                mlp["y"] = [pe.mark()]
            k, tm, tf = tmp()
            a = tt(tm[:], ps[:], RS[:], ALU.mult, m, mlp["rs"], tf)
            b = stt(MID[:, n, :], tm[:], 0.0, tm[:], ALU.max, ALU.mult, a, mlp["y"])
            tfree[k] = [b]
            mid.append([b])
            return [a]

        gemm_t("w_up", 16, 8, 2, (HH, HL), ht, ev_up)
        h_dead = [pe.mark()]

        def down(name, nchunk, src, toks, evac, lag=2, dead=None):
            bs = [bank() for _ in range(8)]
            used = [dead] * 5
            sps = []

            def prep(k):
                if k < 2 * nchunk:
                    sps.append(split(src[:, k, :], MRH[k % 5][:], MRL[k % 5][:], toks[k], used[k % 5]))

            def step(m_, k, kk, wh, wl, wt):
                col = kk * 1024 + 128 * m_
                mm3(bs[m_][1][:], wh[:, col:col + 128], wl[:, col:col + 128], MRH[k % 5][:], MRL[k % 5][:],
                    k == 0, k == 2 * nchunk - 1, bs[m_][2], wt, sps[k])

            for k in range(3):
                prep(k)
            for c in range(nchunk - 1):
                prep(2 * c + 3)
                wh, wl, wt = w_get(name)
                for kk in range(2):
                    k = 2 * c + kk
                    if kk:
                        prep(k + 3)
                    for m_ in range(8):
                        step(m_, k, kk, wh, wl, wt)
                    used[k % 5] = [pe.mark()]
                w_release()
            wh, wl, wt = w_get(name)
            for m_ in range(8):
                for kk in range(2):
                    step(m_, 2 * nchunk - 2 + kk, kk, wh, wl, wt)
                free[bs[m_][0]] = evac(m_, bs[m_][1], pe.mark())
                run_later(lag)
            w_release()
            run_later()

        Y3 = sb("Y3", A + 32, [128, 8, 512])
        ys = ColSum(8)
        mid_use = {}

        def ev_mlp(n, ps, m):
            if n == 0:
                mid_use["ev"], mid_use["yt"] = y_evac(Y3, ys, m)
            return mid_use["ev"](n, ps, m)

        down("w_down", 16, MID, mid, ev_mlp)
        ht, st = post(Y3, mid_use["yt"], ys, "g_mlp_post", None, h_dead)
        down_dead = [pe.mark()]

        dsum = {}

        def ev_deep(n, ps, m):
            a = stt(X[:, n, :], X[:, n, :], ALPHA, ps[:], ALU.mult, ALU.add, m, xt[n])
            xt[n] = [a]
            if n == 0:
                dsum["s"] = ColSum(8)
            later.append(lambda: dsum["s"].add(X[:, n, :], a))
            return [a]

        def deep_norm(g, b, do_split=True, *w):
            nonlocal xt
            r_ = dsum["s"].finish(1.0 / D, None, 8)
            bi, mps, mtok = spread(8, S, r_)
            cs = ColSum(8)
            xc = []
            for k in range(8):
                a = tt(X[:, k, :], X[:, k, :], mps[:], ALU.subtract, mtok)
                xc.append(a)
                q, tm, tf = tmp()
                s_ = af(tm[:], X[:, k, :], ACT.Square, a, tf)
                tfree[q] = [cs.add(tm, s_)]
            give(bi, [xc[7]])
            r_ = cs.finish(1.0 / D, "eps5", 16)
            bi, rps, rtok = spread(16, S, r_)
            xn, hn = [], []
            lo = [None] * 8
            last = None
            for k in range(10):
                if k < 8:
                    a = last = tt(X[:, k, :], X[:, k, :], rps[:], ALU.mult, rtok)
                    xn.append([af(X[:, k, :], X[:, k, :], ACT.Identity, a, scale=par(g, k), bias=par(b, k))])
                    if do_split:
                        lo[k] = cp(HH[:, k, :], X[:, k, :], xn[k], *w)
                if k >= 2 and do_split:
                    hn.append([lo[k - 2], tt(HL[:, k - 2, :], X[:, k - 2, :], HH[:, k - 2, :].bitcast(F),
                                             ALU.subtract, lo[k - 2])])
            give(bi, [last])
            xt = xn
            return hn

        def ffn(l, ht):
            cw = f"ffn_conv{l}"
            start = [pe.mark()]
            PADB = [sb(f"PAD{l}{i}", A + 76 + 2.25 * i, [128, 514]) for i in range(4)]
            zp = [pool.do(lambda e, q=q: e.memset(q[:, 0:1], 0.0), start) for q in PADB]
            zp += [pool.do(lambda e, q=q: e.memset(q[:, 513:514], 0.0), start) for q in PADB]
            pu = [None] * 4
            mid = []
            ab = {}

            def ev(n, ps, m):
                b = n % 4
                q = PADB[b]
                k, o, tf = tmp()
                j = n // 2 + (22 if n % 2 else 0)
                a = cp(q[:, 1:513], ps[:], m, pu[b], zp)
                c = ts(o[:], q[:, 0:512], par(cw, 3 * j), None, ALU.mult, None, a, tf)
                c = stt(o[:], q[:, 1:513], par(cw, 3 * j + 1), o[:], ALU.mult, ALU.add, c)
                c = stt(o[:], q[:, 2:514], par(cw, 3 * j + 2), o[:], ALU.mult, ALU.add, c)
                pu[b] = c
                if n % 2 == 0:
                    ab["k"], ab["o"], ab["c"] = k, o, c
                else:
                    s_ = af(o[:], o[:], ACT.Silu, c)
                    r = tt(MID[:, n // 2, :], ab["o"][:], o[:], ALU.mult, s_, ab["c"], start)
                    mid.append([r])
                    tfree[k] = tfree[ab["k"]] = [r]
                return [a]

            gemm_t(f"up2_{l}", 22, 8, 2, (HH, HL), ht, ev)
            down(f"down2_{l}", 11, MID, mid, ev_deep, dead=start)

        CQF = sb("CQF", A + 60, [128, 6, 512])
        CQH = sb("CQH", A + 32, [128, 3, 512], R)
        CQL = sb("CQL", A + 38, [128, 3, 512], R)
        CVH = sb("CVH", A + 44, [128, 2, 512], R)
        CVL = sb("CVL", A + 48, [128, 2, 512], R)
        KRH = sb("KRH", A + 52, [128, 512], R)
        KRL = sb("KRL", A + 54, [128, 512], R)
        CS = sb("CS", A + 56, [128, 512])
        SN = sb("SN", A + 58, [128, 512])
        POSI = sb("POSI", A + 88, [128, 512], I32)
        ANG = sb("ANG", A + 90, [128, 512])
        AN2 = sb("AN2", A + 92, [128, 512])
        k_pos = dma(sp, once("pos"), POSI[:], t["pos"], down_dead)
        a = dve.do(lambda e: e.tensor_copy(ANG[:], POSI[:]), k_pos, ht, xt)
        a = ts(ANG[:], ANG[:], par("inv"), None, ALU.mult, None, a)
        s_, rd = sin_of(SN[:], ANG[:], 128, a)
        a = af(AN2[:], ANG[:], ACT.Abs, rd)
        c_ = af(CS[:], AN2[:], ACT.Sin, a, scale=-1.0, bias=par("halfpi"))
        s_ = ts(SN[:], SN[:], par("sgn"), None, ALU.mult, None, s_)
        tab = [s_, c_]
        cqt = []

        def rope(psA, psB, mA, mB, hi, lo, *w):
            k1, t1, f1 = tmp()
            k2, t2, f2 = tmp()
            a = tt(t1[:], psA, CS[:], ALU.mult, mA, tab, f1)
            b = tt(t2[:], psB, SN[:], ALU.mult, mB, tab, f2)
            c = tt(t1[:], t1[:], t2[:], ALU.add, a, b)
            r = split(t1[:], hi, lo, c, *w)
            tfree[k1], tfree[k2] = r, [c]
            return a, b, r

        krs = {}
        cqs, cvs = ColSum(3), ColSum(2)

        def ev_in(n, ps, m):
            if n < 5:
                a = cp(CQF[:, n, :], ps[:], m, xt)
                k, tm, tf = tmp()
                b = af(tm[:], ps[:], ACT.Square, m, tf)
                tpend.add(k)

                def add():
                    tfree[k] = [(cqs if n < 3 else cvs).add(tm, b)]
                    tpend.discard(k)

                later.append(add)
                cqt.append([a])
                return [b]
            a = cp(KRS[:], ps[:], m, tab)
            krs["a"] = a
            return [a]

        KRS = sb("KRS", A + 94, [128, 512])

        def norm3(cs, gain, src, n, hi, lo, toks, slot):
            r_ = cs.finish(1.0 / (128 * n), "eps6", slot)
            bi, rps, rtok = spread(slot, S, r_)
            out = []
            for k in range(n):
                q, tm, tf = tmp()
                a = stt(tm[:], src[:, k, :], par(gain, k), rps[:], ALU.mult, ALU.mult, rtok, toks[k], tf)
                tfree[q] = split(tm[:], hi[:, k, :], lo[:, k, :], a)
                out.append(tfree[q])
            give(bi, [a])
            return out

        gemm_t("mla_in", 3, 8, 2, (HH, HL), ht, ev_in)
        cq = norm3(cqs, "g_q", CQF, 3, CQH, CQL, cqt, 8)
        cv = norm3(cvs, "g_kv", CQF[:, 3:5, :], 2, CVH, CVL, cqt[3:5], 16)

        def ev_inx(n, ps, m):
            a, b, krs["t"] = rope(KRS[:], ps[:], krs["a"], m, KRH[:], KRL[:])
            return [b]

        gemm_t("mla_inx", 1, 8, 1, (HH, HL), ht, ev_inx)
        x_dead = [pe.mark()]
        QNH = sb("QNH", A + 60, [128, 2, 512], R)
        QNL = sb("QNL", A + 64, [128, 2, 512], R)
        QRH = sb("QRH", A + 68, [128, 512], R)
        QRL = sb("QRL", A + 70, [128, 512], R)
        KNH = sb("KNH", A + 72, [128, 2, 512], R)
        KNL = sb("KNL", A + 76, [128, 2, 512], R)
        V2H = sb("V2H", A + 80, [128, 4, 256], R)
        V2L = sb("V2L", A + 84, [128, 4, 256], R)
        PA = sb("PA", A + 88, [128, 4, 512])
        PAH = sb("PAH", A + 96, [128, 4, 512], R)
        PAL = sb("PAL", A + 104, [128, 4, 512], R)
        QRS = sb("QRS", A + 112, [128, 512])
        MLS = float(192.0 ** -0.5)
        lfx = {"p": [krs["t"], krs["a"]], "pv": [], "pair": [cq, cv], "rope": []}
        omt = []

        def mla_s(h, pt):
            hh = h % 2
            pb = 64 * hh
            out = []
            for i_ in range(4):
                bi, ps, fr = bank()
                qs = slice(128 * i_, 128 * i_ + 128)
                mm3(ps[:], QNH[:, hh, qs], QNL[:, hh, qs], KNH[:, hh, :], KNL[:, hh, :], True, False, fr, pt)
                mm3(ps[:], QRH[pb:pb + 64, qs], QRL[pb:pb + 64, qs], KRH[pb:pb + 64, :], KRL[pb:pb + 64, :],
                    False, True, krs["t"])
                slot = 32 * hh + 160
                c, d = logits_softmax(i_, ps, 512, pe.mark(), MLS, PA[:, i_, :], slot, lfx["p"])
                free[bi] = [c]
                out.append([ts(PA[:, i_, :], PA[:, i_, :], SM[:, slot + 8 + i_:slot + 9 + i_], None, ALU.mult, None,
                               c, d)])
            return out

        def mla_t(h, sm_):
            bl = []
            for j in range(4):
                bi, ps, fr = bank()
                for i_ in range(4):
                    o, src = ps[:, 128 * i_:128 * i_ + 128], PA[:, i_, 128 * j:128 * j + 128]
                    pe.do(lambda e, o=o, src=src: e.transpose(o, src, IDT[:]), fr, sm_[i_], inc=False)
                sp_ = split(ps[:], PAH[:, j, :], PAL[:, j, :], pe.mark(), lfx["pv"])
                free[bi] = sp_
                bl.append(sp_)
            lfx["p"] = [pe.mark()]
            return bl

        def mla_pv(h, bl, pt):
            bi, ps, fr = bank()
            hs = slice(128 * (h % 2), 128 * (h % 2) + 128)
            for j in range(4):
                mm3(ps[:], V2H[:, j, hs], V2L[:, j, hs], PAH[:, j, :], PAL[:, j, :], j == 0, j == 3, fr, bl, pt)
            lfx["pv"] = [pe.mark()]
            free[bi] = split(ps[:], HH[:, h, :], HL[:, h, :], lfx["pv"], x_dead)
            omt.append(free[bi])

        for p in range(4):
            wh, wl, wt = w_get("uq")
            pw = lfx["pair"]
            pt = []
            rb = []
            for m_ in (0, 1, 2, 3):
                bi, ps, fr = bank()
                for k in range(3):
                    col = (k * 4 + m_) * 128
                    mm3(ps[:], wh[:, col:col + 128], wl[:, col:col + 128], CQH[:, k, :], CQL[:, k, :], k == 0, k == 2,
                        fr, wt, cq)
                m = pe.mark()
                if m_ < 2:
                    free[bi] = split(ps[:], QNH[:, m_, :], QNL[:, m_, :], m, pw)
                    pt.append(free[bi])
                elif m_ == 2:
                    cpa = cp(QRS[:], ps[:], m, lfx["rope"])
                    free[bi] = [cpa]
                else:
                    a, b, r = rope(QRS[:], ps[:], cpa, m, QRH[:], QRL[:], pw)
                    free[bi] = [b]
                    lfx["rope"] = r
                    pt.append(r)
            w_release()
            wh, wl, wt = w_get("ukv")
            for m_ in range(2):
                bi, ps, fr = bank()
                for k in range(2):
                    col = k * 512 + m_ * 128
                    mm3(ps[:], wh[:, col:col + 128], wl[:, col:col + 128], CVH[:, k, :], CVL[:, k, :], k == 0, k == 1,
                        fr, wt, cv)
                free[bi] = split(ps[:], KNH[:, m_, :], KNL[:, m_, :], pe.mark(), pw)
                pt.append(free[bi])
            vp = []
            for b in range(4):
                bi, ps, fr = bank()
                bs = slice(128 * b, 128 * b + 128)
                for k in range(2):
                    col = k * 512 + 256
                    mm3(ps[:, 0:256], CVH[:, k, bs], CVL[:, k, bs], wh[:, col:col + 256], wl[:, col:col + 256],
                        k == 0, k == 1, fr, wt, cv)
                free[bi] = split(ps[:, 0:256], V2H[:, b, :], V2L[:, b, :], pe.mark(), pw)
                vp.append(free[bi])
            w_release()
            smx = mla_s(2 * p, pt)
            for hh in range(2):
                h = 2 * p + hh
                bl = mla_t(h, smx)
                nxt = mla_s(h + 1, pt) if hh == 0 else None
                mla_pv(h, bl, vp)
                smx = nxt
            lfx["pair"] = [pe.mark()]
        gemm_t("mla_o", 4, 8, 2, (HH, HL), omt, ev_deep)
        ht = deep_norm("ln1_g0", "ln1_b0", True, [pe.mark()])
        ffn(0, ht)

        ht = deep_norm("ln2_g0", "ln2_b0", True, [pe.mark()])
        h_dead = [pe.mark()]
        XD = t["xd"]
        s_x = dma(sp, once("xs"), XD, X[:], xt)
        stores.append(s_x)
        VG = [sb(f"VG{i}", A + 32 + 16 * i, [128, 8, 512]) for i in range(3)]
        PADH = [sb(f"PADH{i}", A + 112 + 2.25 * i, [128, 514]) for i in range(2)]
        zp = [pool.do(lambda e, q=q: e.memset(q[:, 0:1], 0.0), h_dead) for q in PADH]
        zp += [pool.do(lambda e, q=q: e.memset(q[:, 513:514], 0.0), h_dead) for q in PADH]
        hyu = [None] * 2
        vg = [[None] * 8 for _ in range(3)]
        ZH = sb("ZH", A + 80, [128, 4, 1024], R)
        ZL = sb("ZL", A + 96, [128, 4, 1024], R)
        YF = sb("YF", A, [128, 8, 1024])
        KB = [sb(f"KB{i}", 8 * i, [128, 2048]) for i in range(2)]
        YH = [sb(f"YH{i}", A + 80 + 8 * i, [128, 1024], R) for i in range(4)]
        YL = [sb(f"YL{i}", A + 84 + 8 * i, [128, 1024], R) for i in range(4)]
        ch_k = [chan("c_k0"), chan("c_k1")]
        ch_kx = chan("c_kx")
        zst = {"t": [], "dead": [h_dead]}

        def z_turn(tb, c, toks):
            bi, ps, fr = bank()
            for j in range(4):
                dst = ps[:, 128 * j:128 * j + 128]
                src = VG[0][:, 4 * c + j, 128 * tb:128 * tb + 128]
                pe.do(lambda e, dst=dst, src=src: e.transpose(dst, src, IDT[:]), fr, toks[4 * c + j], inc=False)
            csl = slice(512 * c, 512 * c + 512)
            free[bi] = split(ps[:], ZH[:, tb, csl], ZL[:, tb, csl], pe.mark(), zst["dead"])
            zst["t"].append(free[bi])

        def ev_hy(n, ps, m):
            b = n % 2
            q = PADH[b]
            g, j = n // 8, n % 8
            o = VG[g][:, j, :]
            a = cp(q[:, 1:513], ps[:], m, hyu[b], zp)
            c = ts(o, q[:, 0:512], par("w_short", 3 * n), None, ALU.mult, None, a, h_dead)
            c = stt(o, q[:, 1:513], par("w_short", 3 * n + 1), o, ALU.mult, ALU.add, c)
            c = stt(o, q[:, 2:514], par("w_short", 3 * n + 2), o, ALU.mult, ALU.add, c)
            hyu[b] = c
            vg[g][j] = [c]
            if n >= 10 and n < 18:
                later.append(lambda: z_turn((n - 10) // 2, n % 2, vg[0]))
            return [a]

        gemm_t("hy_in", 12, 8, 2, (HH, HL), ht, ev_hy)
        x_dead = [pe.mark()]
        kbu = [[s_x], [s_x]]
        kx_done = []
        z_tok = vg[0]
        yf_free = [x_dead] * 8
        for o in range(2):
            zt = zst["t"]
            yft = [None] * 8
            pt_ = [None, None]
            for m_ in range(4):
                kl = dma(sp, ch_k[m_ % 2], KB[m_ % 2][:].rearrange("p (a c) -> p a c", a=2),
                         KD[o, 2 * m_:2 * m_ + 2].rearrange("a p c -> p a c"), kbu[m_ % 2], kd_done, s_x)
                wh, wl, wt = w_get("dft_z")
                bk = []
                for part in range(2):
                    for c in range(2):
                        bi, ps, fr = bank()
                        for kt in range(4):
                            col = kt * 256 + 128 * part
                            csl = slice(512 * c, 512 * c + 512)
                            mm3(ps[:], wh[:, col:col + 128], wl[:, col:col + 128], ZH[:, kt, csl], ZL[:, kt, csl],
                                kt == 0, kt == 3, fr, wt, zt)
                        bk.append((bi, ps, pe.mark()))
                w_release()
                ku = []
                for c in range(2):
                    csl = slice(512 * c, 512 * c + 512)
                    (br, pr, mr), (bi_, pi, mi) = bk[c], bk[2 + c]
                    kr = KB[m_ % 2][:, 512 * c:512 * c + 512]
                    ki = KB[m_ % 2][:, 1024 + 512 * c:1536 + 512 * c]
                    kr2, kr2t = kr, None
                    if m_ == 0:
                        kr2 = TMP[5][:]
                        kr2t = dma(sp, ch_kx, kr2, KD[o, 8, :, 512 * c:512 * c + 512], kd_done, dg_used[0], kx_done)
                    q1, q2, q3, q4 = tmp(), tmp(), tmp(), tmp()
                    a1 = tt(q1[1][:], pr[:], kr, ALU.mult, mr, kl, q1[2])
                    a2 = tt(q2[1][:], pi[:], ki, ALU.mult, mi, kl, q2[2])
                    b1 = tt(q3[1][:], pr[:], ki, ALU.mult, q3[2])
                    b2 = tt(q4[1][:], pi[:], kr2, ALU.mult, kr2t, q4[2])
                    yr, yi = YF[:, 2 * m_, csl], YF[:, 2 * m_ + 1, csl]
                    a3 = pool.do(lambda e, y=yr, q1=q1, q2=q2: e.tensor_tensor(y, q1[1][:], q2[1][:], ALU.subtract),
                                 a1, a2, yf_free[2 * m_])
                    b3 = pool.do(lambda e, y=yi, q3=q3, q4=q4: e.tensor_tensor(y, q3[1][:], q4[1][:], ALU.add),
                                 b1, b2, yf_free[2 * m_ + 1])
                    tfree[q1[0]] = tfree[q2[0]] = [a3]
                    tfree[q3[0]] = tfree[q4[0]] = [b3]
                    if m_ == 0:
                        kx_done = [b2]
                        dg_used[0] = b2
                    free[br], free[bi_] = [b1], [b2]
                    ku.append(b2)
                    yft[2 * m_] = (yft[2 * m_] or []) + [a3]
                    yft[2 * m_ + 1] = (yft[2 * m_ + 1] or []) + [b3]
                kbu[m_ % 2] = ku
            fwd_done = [pe.mark()]
            bs = [bank() for _ in range(8)]
            order = [0, 2, 4, 6, 1, 3, 5, 7]
            used = [fwd_done] * 4
            gate = VG[1 + o]
            res = []
            sps = []

            def prep(k):
                if k < 8:
                    f_ = order[k]
                    sps.append(split(YF[:, f_, :], YH[k % 4][:], YL[k % 4][:], yft[f_], used[k % 4]))
                    yf_free[f_] = sps[k]

            def istep(m_, k, kk, wh, wl, wt):
                cs_ = slice(128 * m_, 128 * m_ + 128)
                ws_ = slice(512 * kk, 512 * kk + 512)
                mm3(bs[m_][1][:], YH[k % 4][:, cs_], YL[k % 4][:, cs_], wh[:, ws_], wl[:, ws_],
                    k == 0, k == 7, bs[m_][2], wt, sps[k])

            for k in range(4):
                prep(k)
            wh, wl, wt = w_get("dft_i")
            for k in range(4):
                for m_ in range(8):
                    istep(m_, k, k, wh, wl, wt)
                used[k % 4] = [pe.mark()]
                prep(k + 4)
            w_release()
            wh, wl, wt = w_get("dft_i")
            for m_ in range(8):
                for k in range(4, 8):
                    istep(m_, k, k - 4, wh, wl, wt)
                a = stt(VG[0][:, m_, :], VG[0][:, m_, :], par("d_bias", 8 * o + m_), bs[m_][1][:],
                        ALU.mult, ALU.add, pe.mark(), z_tok[m_], zt)
                b = tt(VG[0][:, m_, :], VG[0][:, m_, :], gate[:, m_, :], ALU.mult, a, vg[1 + o][m_])
                free[bs[m_][0]] = [a]
                res.append([b])
            w_release()
            z_tok = res
            if o == 0:
                zst = {"t": [], "dead": [pe.mark()]}
                for c in range(2):
                    for tb in range(4):
                        z_turn(tb, c, z_tok)
        inv_done = [pe.mark()]
        k_x = dma(sp, once("xl"), X[:], XD, kbu)
        xt = [[k_x] for _ in range(8)]
        ht = [split(VG[0][:, k, :], HH[:, k, :], HL[:, k, :], z_tok[k], inv_done) for k in range(8)]
        gemm_t("hy_o", 4, 8, 2, (HH, HL), ht, ev_deep)
        ht = deep_norm("ln1_g1", "ln1_b1", True, [pe.mark()])
        ffn(1, ht)
        deep_norm("ln2_g1", "ln2_b1", False)
        for k in range(8):
            stores.append(dma(sp, once(f"out{k}"), t["out"][:, k, :], X[:, k, :], xt[k]))
        assert wst["get"] == len(CHUNKS)
        sp.ops.append([lambda e: None, tokens(stores), None])

        block = es.enter_context(nc.Block())

        @block.sync
        def _(e):
            sp.issue(e)

        @block.gpsimd
        def _(e):
            pool.issue(e)

        @block.scalar
        def _(e):
            act.issue(e)

        @block.vector
        def _(e):
            dve.issue(e)

        @block.tensor
        def _(e):
            pe.issue(e)


def layout(v):
    f32 = np.float32
    o = {}

    def cut(w, kt, mt):
        K, M = w.shape
        n = M // (128 * mt)
        return np.ascontiguousarray(w.reshape(kt, 128, n, mt * 128).transpose(2, 1, 0, 3).reshape(n, 128, -1))

    def rows(w, kk):
        K, N = w.shape
        return np.ascontiguousarray(w.reshape(K // (128 * kk), kk, 128, N).transpose(0, 2, 1, 3).reshape(-1, 128, kk * N))

    def pairs(a, b):
        K = a.shape[0]
        return np.stack([a.reshape(K, -1, 128), b.reshape(K, -1, 128)], 2).reshape(K, -1)

    w_in = v["w_in"][0]
    o["win_ag"] = cut(pairs(w_in[:, 512:1024], w_in[:, 0:512]), 8, 2)
    o["win_qk"] = cut(pairs(w_in[:, 1024:1536], w_in[:, 1536:2048]), 8, 2)
    o["win_v"] = rows(w_in[:, 2048:2560], 4)
    o["win_f"] = rows(w_in[:, 2560:2568], 8)
    o["w_out"] = cut(v["w_out"][0], 8, 2)
    o["w_mk"] = cut(v["w_mk"][0], 8, 2)
    o["w_mv"] = rows(v["w_mv"][0], 4)
    o["w_mq"] = cut(v["w_mq"][0], 8, 2)
    o["w_mo"] = cut(v["w_mo"][0], 4, 4)
    o["w_up"] = cut(v["w_up"][0], 8, 2)
    o["w_down"] = rows(v["w_down"][0], 2)
    mi = v["mla_w_in_2"][0]
    kr = mi[:, 640:704]
    sw = np.concatenate([kr[:, 32:64], kr[:, 0:32]], 1)
    o["mla_in"] = cut(np.concatenate([mi[:, 0:640], kr, kr], 1), 8, 2)
    o["mla_inx"] = cut(np.concatenate([sw, sw], 1), 8, 1)
    uq = v["mla_w_uq_2"][0].reshape(384, 8, 192)
    qn, q1, q2 = uq[:, :, 0:128], uq[:, :, 128:160], uq[:, :, 160:192]
    qr = np.concatenate([q1, q2], 2)
    qs = np.concatenate([q2, q1], 2)
    uqp = np.concatenate([qn.reshape(384, 4, 256), qr.reshape(384, 4, 128), qs.reshape(384, 4, 128)], 2)
    o["uq"] = cut(uqp.reshape(384, 2048), 3, 4)
    ukv = v["mla_w_ukv_2"][0].reshape(256, 4, 2, 256)
    ukp = np.concatenate([ukv[..., 0:128].reshape(256, 4, 256), ukv[..., 128:256].reshape(256, 4, 256)], 2)
    o["ukv"] = cut(ukp.reshape(256, 2048), 2, 4)
    o["mla_o"] = cut(v["mla_w_o_2"][0], 8, 2)
    o["hy_in"] = cut(v["hy_w_in_2"][0], 8, 2)
    o["hy_o"] = cut(v["hy_w_o_2"][0], 8, 2)
    for l in range(2):
        up = v["ffn_w_up_2"][l]
        o[f"up2_{l}"] = cut(pairs(up[:, 0:2816], up[:, 2816:5632]), 8, 2)
        o[f"down2_{l}"] = rows(v["ffn_w_down_2"][l], 2)
    tt_ = np.arange(512)
    ph = (np.outer(tt_, tt_) % 1024) * (2 * np.pi / 1024)
    cr, si = np.cos(ph), -np.sin(ph)
    alt = (-1.0) ** tt_
    sn = si.copy()
    sn[:, 0] = alt
    crx = cr[:, 0:128].copy()
    crx[:, 0] = alt
    o["dft_c"] = cut(cr.astype(f32), 4, 4)
    o["dft_s"] = cut(si.astype(f32), 4, 4)
    o["dft_kx"] = cut(crx.astype(f32), 4, 1)
    o["dft_z"] = cut(pairs(cr, sn).astype(f32), 4, 2)
    wgt = np.full((512, 1), 2.0 / 1024)
    wgt[0] = 1.0 / 1024
    ir, ii = cr.T * wgt, si.T * wgt
    ii[0] = alt / 1024
    o["dft_i"] = rows(np.concatenate([ir, ii], 0).astype(f32), 4)
    ln = np.linspace(0.0, 1.0, 512, dtype=f32)[:, None]
    w = (2.0 * np.pi * np.arange(512)[:, None] / 512).astype(f32)
    fr = np.linspace(1e-4, 15, 16, dtype=f32)[None]
    o["zfeat"] = np.ascontiguousarray(np.concatenate([ln, np.cos(fr * w), -np.sin(fr * w)], 1).T.astype(f32))
    dl = np.abs(np.linspace(np.log(0.3) / 1e-2, np.log(1.5) / 1e-2, 1024, dtype=f32))
    o["decay"] = np.ascontiguousarray(np.exp(-ln * dl).astype(f32).reshape(4, 128, 1024).transpose(1, 0, 2))
    o["fw_out"] = np.ascontiguousarray(v["hy_fw_out_2"][0])
    fs = np.zeros((64, 256), f32)
    fs[0:33, 0:64] = v["hy_fw1_2"][0]
    fs[:, 64:128] = v["hy_fw2_2"][0]
    fs[:, 128:192] = v["hy_fw3_2"][0]
    for i, n in enumerate(("hy_fb1_2", "hy_fb2_2", "hy_fb3_2", "hy_freq_2")):
        fs[:, 192 + i] = v[n][0]
    o["fsmall"] = fs

    def feat(x):
        return np.ascontiguousarray(x.T.reshape(8, 128, -1).transpose(1, 0, 2))

    o["xt"] = feat(v["x"][0])
    o["memt"] = feat(v["mem"][0])
    o["pos"] = np.ascontiguousarray(np.broadcast_to(v["positions_2"], (128, 512)))
    i_, j_ = np.arange(128)[:, None], np.arange(128)[None]
    o["consts"] = np.concatenate([np.eye(128), np.where(j_ <= i_, 0.0, -1e30), (i_ <= j_) * 1.0,
                                  np.ones((128, 384))], 1).astype(f32)
    p = np.zeros((128, NPC), f32)

    def put(name, x):
        c = x.reshape(-1, 128).T
        p[:, POFF[name]:POFF[name] + c.shape[1]] = c

    for n, k in (("g_mix_pre", "norm_mix_pre"), ("g_mix_post", "norm_mix_post"), ("g_mem_pre", "norm_mem_pre"),
                 ("g_mem_post", "norm_mem_post"), ("g_memkv", "norm_memkv"), ("g_mlp_pre", "norm_mlp_pre"),
                 ("g_mlp_post", "norm_mlp_post"), ("conv_b", "conv_b"), ("cln_g", "conv_ln_g"),
                 ("cln_b", "conv_ln_b"), ("g_q", "mla_g_q_2"), ("g_kv", "mla_g_kv_2"), ("d_bias", "hy_d_bias_2")):
        put(n, v[k])
    put("conv_w", np.ascontiguousarray(v["conv_w"][0].reshape(31, 4, 128).transpose(1, 0, 2)))
    put("w_short", np.ascontiguousarray(v["hy_w_short_2"][0].reshape(3, 24, 128).transpose(1, 0, 2)))
    for l in range(2):
        put(f"ffn_conv{l}", np.ascontiguousarray(v["ffn_w_conv_2"][l].reshape(3, 44, 128).transpose(1, 0, 2)))
        for n in ("ln1_g", "ln1_b", "ln2_g", "ln2_b"):
            put(f"{n}{l}", v[f"{n}_2"][l])
    p[:, POFF["b_forget"]:POFF["b_forget"] + 8] = v["b_forget"]
    inv = (1.0 / (np.float32(10000.0) ** (np.arange(0, 64, 2, dtype=f32) / np.float32(64)))).astype(f32)
    p[:, POFF["inv"]] = np.tile(inv, 4)
    p[:, POFF["sgn"]] = np.where(np.arange(128) % 64 < 32, -1.0, 1.0)
    p[:, POFF["one"]] = 1.0
    p[:, POFF["eps6"]] = 1e-6
    p[:, POFF["eps5"]] = 1e-5
    p[:, POFF["halfpi"]] = HALF_PI
    o["par"] = p
    return o


def kernel(**inputs):
    import concourse.bacc as _bacc
    from concourse.bass_utils import run_bass_kernel_spmd as _run

    arrays = layout({k: np.asarray(a) for k, a in inputs.items()})
    nc = _bacc.Bacc("TRN2", target_bir_lowering=False, num_devices=1)
    t = {}
    for name, a in arrays.items():
        t[name] = nc.dram_tensor(f"in_{name}", a.shape, mybir.dt.from_np(a.dtype), kind="ExternalInput").ap()
    t["out"] = nc.dram_tensor("out_0", (128, 8, 512), F, kind="ExternalOutput").ap()
    t["kd"] = nc.dram_tensor("kd", (2, 9, 128, 1024), F, kind="Internal").ap()
    t["xd"] = nc.dram_tensor("xd", (128, 8, 512), F, kind="Internal").ap()
    build(nc, t)
    r = _run(nc, [{f"in_{n}": a for n, a in arrays.items()}], core_ids=[0])
    got = np.asarray(r.results[0]["out_0"])
    return np.ascontiguousarray(got.transpose(1, 0, 2).reshape(1024, 512).T)[None]
```

```python
from contextlib import ExitStack

import numpy as np

import concourse.bass as bass
from concourse import mybir

F = mybir.dt.float32
R = mybir.dt.float32r
I32 = mybir.dt.int32
ALU = mybir.AluOpType
ACT = mybir.ActivationFunctionType
AX = mybir.AxisListType.X

S = 512
D = 1024
ALPHA = float(np.float32((2.0 * 2) ** 0.25))
MAGIC = 12582912.0
TWO_PI = 6.283185307179586
C1 = 6.28125
C2 = 0.0019350051879882812
C3 = TWO_PI - C1 - C2
PI_IN = 3.1415925
HALF_PI = 1.5707963267948966


def tokens(waits):
    out = []
    for w in waits:
        if isinstance(w, list) or (isinstance(w, tuple) and not isinstance(w[-1], int)):
            out += tokens(w)
        elif w is not None:
            out.append(w)
    return out


class Engine:

    def __init__(self, sem):
        self.sem, self.count, self.ops = sem, 0, []

    def do(self, make, *waits, inc=True):
        self.ops.append([make, tokens(waits), False])
        return self.mark() if inc else None

    def mark(self):
        if not self.ops[-1][2]:
            self.ops[-1][2] = True
            self.count += 1
        return (self.sem, self.count)

    def issue(self, eng):
        seen = {}

        for make, waits, inc in self.ops:
            for sem, value in waits:
                if seen.get(id(sem), 0) < value:
                    eng.wait_ge(sem, value)
                    seen[id(sem)] = value
            ins = make(eng)
            if inc is True:
                ins.then_inc(self.sem, 1)


class Channel:

    def __init__(self, sem):
        self.sem, self.count = sem, 0


PCOLS = [("g_mix_pre", 8), ("g_mix_post", 8), ("g_mem_pre", 8), ("g_mem_post", 8), ("g_memkv", 8),
         ("g_mlp_pre", 8), ("g_mlp_post", 8), ("conv_w", 124), ("conv_b", 4), ("cln_g", 4), ("cln_b", 4),
         ("g_q", 3), ("g_kv", 2), ("w_short", 72), ("d_bias", 16), ("ffn_conv0", 132), ("ffn_conv1", 132),
         ("ln1_g0", 8), ("ln1_b0", 8), ("ln2_g0", 8), ("ln2_b0", 8),
         ("ln1_g1", 8), ("ln1_b1", 8), ("ln2_g1", 8), ("ln2_b1", 8), ("b_forget", 8),
         ("inv", 1), ("sgn", 1), ("one", 1), ("eps6", 1), ("eps5", 1), ("halfpi", 1)]
POFF, _at = {}, 0
for _n, _w in PCOLS:
    POFF[_n] = _at
    _at += _w
NPC = _at

CHUNKS = [
    ("dft_c", 0, 2048), ("dft_kx", 0, 512), ("dft_s", 0, 2048),
    ("dft_c", 0, 2048), ("dft_kx", 0, 512), ("dft_s", 0, 2048),
    ("win_f", 0, 64), *[("win_ag", i, 2048) for i in range(4)], *[("win_v", i, 2048) for i in range(2)],
    *[("win_qk", i, 2048) for i in range(4)], *[("w_mk", i, 2048) for i in range(2)],
    *[("w_out", i, 2048) for i in range(4)],
    *[("w_mv", i, 2048) for i in range(2)],
    *[("w_mq", i, 2048) for i in range(2)], *[("w_mo", i, 2048) for i in range(2)],
    *[("w_up", i, 2048) for i in range(16)], *[("w_down", i, 2048) for i in range(16)],
    *[("mla_in", i, 2048) for i in range(3)], ("mla_inx", 0, 1024),
]
for _p in range(4):
    CHUNKS += [("uq", _p, 1536), ("ukv", _p, 1024)]
CHUNKS += [("mla_o", i, 2048) for i in range(4)]
CHUNKS += [("up2_0", i, 2048) for i in range(22)] + [("down2_0", i, 2048) for i in range(11)]
CHUNKS += [("hy_in", i, 2048) for i in range(12)]
for _o in range(2):
    CHUNKS += [("dft_z", 0, 2048), ("dft_i", 0, 2048)]
CHUNKS += [("hy_o", i, 2048) for i in range(4)]
CHUNKS += [("up2_1", i, 2048) for i in range(22)] + [("down2_1", i, 2048) for i in range(11)]


def build(nc, t):
    es = ExitStack()
    BASE = 16512

    def sb(name, kb, shape, dt=F):
        return nc.alloc_sbuf_tensor_at(name, shape, dt, offset=BASE + int(kb * 1024))

    def sem(name):
        return es.enter_context(nc.semaphore(name))

    def chan(name):
        return Channel(sem(name))

    with es:
        psum = [es.enter_context(nc.psum_tensor(f"ps{i}", [128, 512], F)) for i in range(8)]
        pe, act, dve, pool, sp = (Engine(sem(n)) for n in ("s_pe", "s_act", "s_dve", "s_pool", "s_sp"))

        def dma(q, ch, dst, src, *waits):
            ch.count += 16
            sm = ch.sem
            q.ops.append([lambda e: e.dma_start(dst, src).then_inc(sm, 16), tokens(waits), None])
            return (ch.sem, ch.count)

        X = sb("X", 0, [128, 8, 512])
        W32 = [sb(f"W32_{i}", 16 + 8 * i, [128, 2048]) for i in range(2)]
        WH = [sb(f"WH{i}", 40 + 8 * i, [128, 2048], R) for i in range(2)]
        WL = [sb(f"WL{i}", 56 + 8 * i, [128, 2048], R) for i in range(2)]
        PAR = sb("PAR", 72, [128, NPC])
        IDT = sb("IDT", 75, [128, 128])
        ONE = sb("ONE", 75.5, [128, 128])
        IDR = sb("IDR", 76, [128, 128], R)
        MKR = sb("MKR", 76.5, [128, 128], R)
        SM = sb("SM", 77, [128, 256])
        TMP = [sb(f"TMP{i}", 78 + 2 * i, [128, 512]) for i in range(6)]
        A = 90

        ch_w = [chan(f"c_w{i}") for i in range(2)]
        ch_s = [chan(f"c_s{i}") for i in range(8)]
        ch_m = {}

        def once(name):
            ch_m[name] = chan("c_" + name)
            return ch_m[name]

        stores = []

        free = [[] for _ in range(8)]
        turn = [0]

        held = set()

        def bank(hold=False):
            while turn[0] % 8 in held:
                turn[0] += 1
            i = turn[0] % 8
            turn[0] += 1
            if hold:
                held.add(i)
            return i, psum[i], free[i]

        def give(i, toks):
            free[i] = toks
            held.discard(i)

        later = []

        def run_later(keep=0):
            while len(later) > keep:
                later.pop(0)()

        tfree = [[] for _ in range(4)]
        tturn = [0]
        tpend = set()

        def tmp():
            if len(tpend) == 4:
                run_later()
            while tturn[0] % 4 in tpend:
                tturn[0] += 1
            k = tturn[0] % 4
            tturn[0] += 1
            return k, TMP[k], tfree[k]

        taps = []

        def run_taps(n):
            for _ in range(min(n, len(taps))):
                taps.pop(0)()

        wst = {"dma": 0, "split": 0, "get": 0}
        w_split = []
        w_used = []

        def w_dma():
            n = wst["dma"]
            if n >= len(CHUNKS):
                return
            name, i, cols = CHUNKS[n]
            s = n % 2
            wst["dma"] += 1
            w_split.append([dma(sp, ch_w[s], W32[s][:, 0:cols], t[name][i], w_split[n - 2] if n >= 2 else None)])

        def w_do_split():
            n = wst["split"]
            if n >= len(CHUNKS):
                return
            name, i, cols = CHUNKS[n]
            s = r = n % 2
            landed = w_split[n][0]
            used = w_used[n - 2] if n >= 2 else None
            src, hi, lo = W32[s][:, 0:cols], WH[r][:, 0:cols], WL[r][:, 0:cols]
            a = act.do(lambda e: e.activation(hi, src, ACT.Copy), landed, used)
            if n > 0 and CHUNKS[n - 1][2] < 1000 or (name, i) == ("hy_o", 1):
                h = cols // 2
                l1, s1, h1 = WL[r][:, 0:h], W32[s][:, 0:h], WH[r][:, 0:h]
                l2, s2, h2 = WL[r][:, h:cols], W32[s][:, h:cols], WH[r][:, h:cols]
                b = [pool.do(lambda e: e.tensor_tensor(l1, s1, h1.bitcast(F), ALU.subtract), landed, used, a),
                     tt(l2, s2, h2.bitcast(F), ALU.subtract, landed, used, a)]
            else:
                b = pool.do(lambda e: e.tensor_tensor(lo, src, hi.bitcast(F), ALU.subtract), landed, used, a)
            w_split[n] = [a, b]
            wst["split"] += 1
            w_dma()

        def w_get(name):
            n = wst["get"]
            assert CHUNKS[n][0] == name, (CHUNKS[n], name)
            if wst["split"] <= n:
                w_do_split()
            if wst["split"] <= n + 1:
                w_do_split()
            wst["get"] += 1
            r = n % 2
            return WH[r], WL[r], w_split[n]

        def w_ahead():
            if wst["split"] <= wst["get"] + 1:
                w_do_split()

        def w_release():
            w_used.append(pe.mark())

        def mm(out, l, r, start, stop, *waits):
            pe.do(lambda e: e.matmul(out, l, r, start=start, stop=stop), *waits, inc=False)

        def mm3(out, lh, ll, rh, rl, first, last, *waits):
            mm(out, ll, rh, first, False, *waits)
            mm(out, lh, rl, False, False)
            mm(out, lh, rh, False, last)

        def cp(out, src, *w, scale=1.0):
            return act.do(lambda e: e.activation(out, src, ACT.Copy, scale=scale), *w)

        def tt(out, a, b, op, *w):
            return dve.do(lambda e: e.tensor_tensor(out, a, b, op), *w)

        def ts(out, a, s1, s2, o1, o2, *w):
            if s2 is None:
                return dve.do(lambda e: e.tensor_scalar(out, a, s1, None, o1), *w)
            return dve.do(lambda e: e.tensor_scalar(out, a, s1, s2, o1, o2), *w)

        def stt(out, a, s, b, o1, o2, *w):
            return dve.do(lambda e: e.scalar_tensor_tensor(out=out, in0=a, scalar=s, in1=b, op0=o1, op1=o2), *w)

        def af(out, src, fn, *w, scale=1.0, bias=0.0):
            return act.do(lambda e: e.activation(out, src, fn, scale=scale, bias=bias), *w)

        def split(src, hi, lo, *w, scale=None):
            a = cp(hi, src, *w, scale=1.0 if scale is None else scale)
            if scale is None:
                b = tt(lo, src, hi.bitcast(F), ALU.subtract, *w, a)
            else:
                b = stt(lo, src, scale, hi.bitcast(F), ALU.mult, ALU.subtract, *w, a)
            return [a, b]

        def par(name, i=0, p=slice(0, 128)):
            c = POFF[name] + i
            return PAR[p, c:c + 1]

        k_par = dma(sp, once("par"), PAR[:], t["par"])
        k_id = dma(sp, once("idt"), IDT[:], t["consts"][:, 0:128])
        k_mk = dma(sp, once("mk"), TMP[0][:, 0:128], t["consts"][:, 128:256])
        k_one = dve.do(lambda e: e.memset(ONE[:], 1.0))
        c_idr = cp(IDR[:], IDT[:], k_id)
        c_mkr = cp(MKR[:], TMP[0][:, 0:128], k_mk)
        consts = [k_par, k_id, k_one, c_idr, c_mkr]
        for e in (pe, act, dve, pool):
            e.ops.append([lambda g: None, tokens(consts), None])

        FW = sb("FW", A, [64, 4096])
        WPH = sb("WPH", A + 16, [64, 2048], R)
        WPL = sb("WPL", A + 24, [64, 2048], R)
        HPH = sb("HPH", A + 32, [128, 2, 4, 1024], R)
        HPL = sb("HPL", A + 64, [128, 2, 4, 1024], R)
        DEC = sb("DEC", A + 96, [128, 4, 1024])
        H3H = sb("H3H", A + 112, [64, 512], R)
        H3L = sb("H3L", A + 114, [64, 512], R)
        ZF = TMP[1]
        k_zf = dma(sp, once("zf"), ZF[0:33, :], t["zfeat"])
        k_f1 = dma(sp, once("f1"), SM[0:64, :], t["fsmall"])
        k_fw = dma(sp, once("fw"), FW[:], t["fw_out"])
        w_dma()
        k_dec = dma(sp, once("dec"), DEC[:], t["decay"])
        w_dma()

        def sin_of(dst, arg, P, *w):
            kq = TMP[4][0:P, :]
            a = ts(kq, arg, 1.0 / TWO_PI, MAGIC, ALU.mult, ALU.add, *w)
            a = ts(kq, kq, MAGIC, None, ALU.subtract, None, a)
            for c in (C1, C2, C3):
                a = stt(arg, kq, -c, arg, ALU.mult, ALU.add, a)
            a = ts(arg, arg, PI_IN, -PI_IN, ALU.min, ALU.max, a)
            return af(dst, arg, ACT.Sin, a), a

        KD = t["kd"]
        stage = [None] * 8
        sturn = [0]
        wp = [[], []]
        hp_used = [[], []]
        hpt = [[], []]

        def make_w(sgn, o):
            make_w_half(sgn, o, 0)
            make_w_half(sgn, o, 1)

        def make_w_half(sgn, o, c):
            c0 = 2048 * o
            f_ = FW[:, c0 + 512 * c:c0 + 512 * c + 512]
            b_ = FW[:, c0 + 1024 + 512 * c:c0 + 1024 + 512 * c + 512]
            q = 1024 * sgn + 512 * c
            k, tm, tf = tmp()
            a = tt(tm[0:64, :], f_, b_, ALU.subtract if sgn else ALU.add, k_fw, tf)
            x = split(tm[0:64, :], WPH[:, q:q + 512], WPL[:, q:q + 512], a, hpt[sgn])
            tfree[k] = [x]
            wp[sgn] = [x] if c == 0 else wp[sgn] + [x]

        tfree[0], tfree[1], tfree[2], tfree[3] = [c_mkr], [], [], []
        tpend.add(1)
        hin, hw, kin = ZF[0:33, :], [k_zf], 1
        for layer in range(3):
            i, ps, fr = bank()
            lhs = SM[0:33, 0:64] if layer == 0 else SM[0:64, 64 * layer:64 * layer + 64]
            mm(ps[0:64, :], lhs, hin, True, True, fr, k_f1, *hw)
            m = pe.mark()
            tfree[kin] = [m]
            tpend.discard(kin)
            kin, arg, tf = tmp()
            tpend.add(kin)
            arg = arg[0:64, :]
            a = ts(arg, ps[0:64, :], SM[0:64, 192 + layer:193 + layer], SM[0:64, 195:196], ALU.add, ALU.mult, m, tf)
            free[i] = [a]
            s, _ = sin_of(arg, arg, 64, a)
            hin, hw = arg, [s]
            if layer == 1:
                w_do_split()
            make_w_half(*[(0, 0, 0), (0, 0, 1), (1, 0, 0)][layer])
        make_w_half(1, 0, 1)
        h3 = split(hin, H3H[:], H3L[:], *hw)
        tfree[kin] = [h3]
        tpend.discard(kin)
        unsplit = []

        def flush():
            while unsplit:
                unsplit.pop(0)()

        def make_h(sgn, tb, lag=False):
            for c in range(2):
                i, ps, fr = bank()
                q = 1024 * sgn + 512 * c
                tsl = slice(128 * tb, 128 * tb + 128)
                csl = slice(512 * c, 512 * c + 512)
                mm3(ps[:], H3H[:, tsl], H3L[:, tsl], WPH[:, q:q + 512], WPL[:, q:q + 512], True, True,
                    fr, h3, wp[sgn])
                k, tm, tf = tmp()
                a = tt(tm[:], ps[:], DEC[:, tb, csl], ALU.mult, pe.mark(), k_dec, tf)
                free[i] = [a]
                hi, lo = HPH[:, sgn, tb, csl], HPL[:, sgn, tb, csl]
                x1 = cp(hi, tm[:], a, hp_used[sgn])

                def rest(tm=tm, hi=hi, lo=lo, x1=x1, k=k, c=c):
                    if lag and c == 0:
                        x2 = pool.do(lambda e: e.tensor_tensor(lo, tm[:], hi.bitcast(F), ALU.subtract), x1,
                                     hp_used[sgn])
                    else:
                        x2 = tt(lo, tm[:], hi.bitcast(F), ALU.subtract, x1, hp_used[sgn])
                    tfree[k] = [x1, x2]
                    hpt[sgn].append([x1, x2])

                flush()
                unsplit.append(rest)
                if not lag:
                    flush()

        STG = [X[:, k, :] for k in range(8)]
        ch_g = ch_s
        dec_dead = None

        def spectrum(o, part, nm, wh, wl, wt, row0, between):
            for m_ in range(nm):
                for c in range(2):
                    i, ps, fr = bank()
                    csl = slice(512 * c, 512 * c + 512)
                    for kt in range(4):
                        col = kt * 128 * nm + 128 * m_
                        mm3(ps[:], wh[:, col:col + 128], wl[:, col:col + 128], HPH[:, part, kt, csl],
                            HPL[:, part, kt, csl], kt == 0, kt == 3, fr, wt, hpt[part])
                    k = sturn[0] % 8
                    sturn[0] += 1
                    a = cp(STG[k][:], ps[:], pe.mark(), stage[k], dec_dead)
                    free[i] = [a]
                    stage[k] = dma(sp, ch_g[k], KD[o, row0 + 2 * m_, :, csl], STG[k][:], a)
                    run_later(1)
                if between is not None:
                    between(m_)

        def gemm_t(name, nchunk, KT, MT, acts, atoks, evac, N=512, korder=None, base=0, lag=0, head=True):
            at = acts if callable(acts) else lambda k: (acts[0][:, k, 0:N], acts[1][:, k, 0:N])
            ko = korder or list(range(KT))

            def step(ps, fr, m_, k, wh, wl, wt):
                col = (k * MT + m_) * 128
                mm3(ps[:, 0:N], wh[:, col:col + 128], wl[:, col:col + 128], *at(k),
                    k == ko[0], k == ko[-1], fr, wt, atoks[k])

            for c in range(nchunk):
                wh, wl, wt = w_get(name)
                if c == 0 and head:
                    bs = [bank(hold=True) for _ in range(MT)]
                    for k in ko:
                        for m_ in range(MT):
                            step(bs[m_][1], bs[m_][2], m_, k, wh, wl, wt)
                            if k == ko[-1]:
                                give(bs[m_][0], evac(base + m_, bs[m_][1], pe.mark()))
                        if k != ko[-1] and later:
                            later.pop(0)()
                else:
                    for m_ in range(MT):
                        i, ps, fr = bank()
                        for k in ko:
                            step(ps, fr, m_, k, wh, wl, wt)
                        free[i] = evac(base + c * MT + m_, ps, pe.mark())
                        run_later(lag)
                w_release()
            run_later()

        dg_used = [None]

        class ColSum:

            def __init__(self, n, N=S):
                self.n, self.nb, self.k = n, N // 128, 0
                self.bank = None

            def add(self, ap, *w):
                if self.bank is None:
                    self.bank = bank(hold=True)
                i, ps, fr = self.bank
                last = self.k == self.n - 1
                for b in range(self.nb):
                    st, l, o = self.k == 0 and b == 0, ap[:, 128 * b:128 * b + 128], ps[:, b:b + 1]
                    pe.do(lambda e, o=o, l=l, st=st: e.matmul(o, l, ONE[:, 0:1], start=st, stop=last,
                                                              skip_group_check=True), fr, *w, inc=False)
                self.k += 1
                return pe.mark()

            def finish(self, scale, eps, slot):
                i, ps, _ = self.bank
                m = pe.mark()
                v, r = SM[:, slot:slot + self.nb], SM[:, slot + 4:slot + 4 + self.nb]
                if eps is None:
                    a = a2 = ts(r, ps[:, 0:self.nb], scale, None, ALU.mult, None, m)
                else:
                    a = af(v, ps[:, 0:self.nb], ACT.Sqrt, m, scale=scale, bias=par(eps))
                    a2 = dve.do(lambda e: e.reciprocal(r, v), a)
                give(i, [a])
                return a2

        def diag(dg, slot, N, *w):
            return [ts(dg[:, 128 * b:128 * b + 128], IDT[:], SM[:, slot + 4 + b:slot + 5 + b], None,
                       ALU.mult, None, *w) for b in range(N // 128)]

        def spread(slot, N, tok, out=None, d=None):
            dg = TMP[5]
            d = d or diag(dg, slot, N, tok, dg_used[0])
            i, ps, fr = bank(hold=True)
            mm(ps[:, 0:N], ONE[:], dg[:, 0:N], True, True, fr, *d)
            m = dg_used[0] = pe.mark()
            if out is None:
                return i, ps, m
            o = cp(out, ps[:, 0:N], m, d)
            give(i, [o])
            return o

        RS = TMP[4]
        HH = sb("HH", A, [128, 8, 512], R)
        HL = sb("HL", A + 16, [128, 8, 512], R)

        def gain_split(src, g, hi, lo, *w):
            a = act.do(lambda e: e.activation(hi, src, ACT.Identity, scale=g), *w)
            b = stt(lo, src, g, hi.bitcast(F), ALU.mult, ALU.subtract, *w, a)
            return [a, b]

        for tb in range(4):
            make_h(0, tb, True)
        flush()
        xt, ht = [], []
        xs = ColSum(8)

        def x_in(m_):
            for k in (2 * m_, 2 * m_ + 1):
                kx = xld[k]
                xt.append([kx])
                ht.append(gain_split(X[:, k, :], par("g_mix_pre", k), HH[:, k, :], HL[:, k, :], kx, fw_dead))
                q, tm, tf = tmp()
                a = af(tm[:], X[:, k, :], ACT.Square, kx, tf)
                tpend.add(q)

                def add(tm=tm, a=a, q=q):
                    tfree[q] = [xs.add(tm, a)]
                    tpend.discard(q)

                later.append(add)

        for o in range(2):
            wh, wl, wt = w_get("dft_c")
            if o == 0:
                spectrum(o, 0, 4, wh, wl, wt, 0, lambda m_: make_h(1, m_))
            else:
                make_w(1, 1)
                hpt[1] = []
                spectrum(o, 0, 4, wh, wl, wt, 0, lambda m_: make_h(1, m_))
            w_release()
            wh, wl, wt = w_get("dft_kx")
            spectrum(o, 0, 1, wh, wl, wt, 8, None)
            w_release()
            hp_used[0] = [pe.mark()]
            wh, wl, wt = w_get("dft_s")
            if o == 0:
                make_w(0, 1)
                hpt[0] = []
            if o == 1:
                fw_dead = [pe.mark()]
                xld = [dma(sp, ch_s[k], X[:, k, :], t["xt"][:, k, :], stage[k]) for k in range(8)]
                kd_done = list(stage)
                stage = [None] * 8
                STG = [sb(f"STG{k}", A + 96 + 2 * k, [128, 512]) for k in range(8)]
                ch_g = [chan(f"c_g{k}") for k in range(8)]
                dec_dead = list(hpt)
            spectrum(o, 1, 4, wh, wl, wt, 1, (lambda m_: make_h(0, m_)) if o == 0 else x_in)
            w_release()
            hp_used[1] = [pe.mark()]
        run_later()
        kd_done += stage
        stores += kd_done
        hp_used = [pe.mark(), stage]

        rr = xs.finish(1.0 / D, "eps6", 0)
        rs = spread(0, S, rr, RS[:])

        QH = sb("QH", A + 32, [128, 4, 512], R)
        QL = sb("QL", A + 40, [128, 4, 512], R)
        KH = sb("KH", A + 48, [128, 4, 512], R)
        KL = sb("KL", A + 56, [128, 4, 512], R)
        VH = sb("VH", A + 64, [128, 4, 512], R)
        VL = sb("VL", A + 72, [128, 4, 512], R)
        U = sb("U", A + 80, [128, 4, 542])
        CO = sb("CO", A + 89, [128, 4, 512])
        PP = sb("PP", 32, [128, 1280])
        ATP = sb("ATP", 37, [128, 4, 128])
        POFS = [0, 128, 384, 768]
        TOFS = [0, 384, 640, 768]
        QA = sb("QA", A + 109, [128, 2, 512], R)
        KA = sb("KA", A + 113, [128, 2, 512], R)
        z_u = dve.do(lambda e: e.memset(U[:, :, 0:30], 0.0), hp_used)
        conv_t = [None] * 4
        sg = {}

        def tap(j, w_):
            if w_ == 0:
                conv_t[j] = ts(CO[:, j, :], U[:, j, 0:512], par("conv_w", 31 * j), par("conv_b", j),
                               ALU.mult, ALU.add, z_u, conv_t[j])
            else:
                conv_t[j] = stt(CO[:, j, :], U[:, j, w_:w_ + 512], par("conv_w", 31 * j + w_), CO[:, j, :],
                                ALU.mult, ALU.add, conv_t[j])

        def ev_ag(n, ps, m):
            j = n // 2
            if n % 2 == 0:
                k, tm, tf = tmp()
                a = tt(tm[:], ps[:], RS[:], ALU.mult, m, rs, tf)
                b = af(tm[:], tm[:], ACT.Sigmoid, a)
                c = pool.do(lambda e: e.tensor_tensor(tm[:], tm[:], RS[:], ALU.mult), b, rs)
                sg["k"], sg["tm"], sg["c"] = k, tm, c
                run_taps(6)
                return [a]
            a = tt(U[:, j, 30:542], ps[:], sg["tm"][:], ALU.mult, m, sg["c"], hp_used)
            tfree[sg["k"]] = [a]
            conv_t[j] = a
            for w_ in range(31):
                taps.append(lambda w_=w_: tap(j, w_))
            run_taps(6)
            return [a]

        wh, wl, wt = w_get("win_f")
        i, ps, fr = bank()
        for b in range(4):
            for k in range(8):
                bs = slice(128 * b, 128 * b + 128)
                mm3(ps[:, 8 * b:8 * b + 8], HH[:, k, bs], HL[:, k, bs], wh[:, 8 * k:8 * k + 8], wl[:, 8 * k:8 * k + 8],
                    k == 0, k == 7, fr, wt, ht)
        w_release()
        m = pe.mark()
        z, e1, e2, lf = (SM[:, 32 * q:32 * q + 32] for q in range(1, 5))
        bf = PAR[:, POFF["b_forget"]:POFF["b_forget"] + 8]
        zt = [stt(SM[:, 32 + 8 * b:40 + 8 * b], ps[:, 8 * b:8 * b + 8], SM[:, 4 + b:5 + b], bf, ALU.mult, ALU.add,
                  m, rr) for b in range(4)]
        free[i] = zt
        a = af(e1, z, ACT.Abs, *zt)
        a = af(e1, e1, ACT.Exp, a, scale=-1.0)
        a = af(e1, e1, ACT.Ln, a, bias=par("one"))
        b_ = ts(e2, z, 0.0, None, ALU.min, None, *zt)
        lft = tt(lf, e2, e1, ALU.subtract, a, b_)
        gemm_t("win_ag", 2, 8, 2, (HH, HL), ht, ev_ag)
        TRI = TMP[5]
        k_tri = dma(sp, once("tri"), TRI[:], t["consts"][:, 256:768], dg_used[0])
        i, ps, fr = bank()
        for k in range(4):
            mm(ps[0:8, 128 * k:512], SM[:, 128 + 8 * k:136 + 8 * k], TRI[:, 0:512 - 128 * k], k == 0, k == 3,
               fr, lft, k_tri)
        m = pe.mark()
        dg_used[0] = m
        CH = sb("CH", 32, [8, 512], R)
        CL = sb("CL", 34, [8, 512], R)
        NH = sb("NH", 36, [8, 512], R)
        NL = sb("NL", 38, [8, 512], R)
        c_ = split(ps[0:8, :], CH[:], CL[:], m, hp_used)
        free[i] = c_
        n1 = cp(NH[:], CH[:].bitcast(F), *c_, scale=-1.0)
        n2 = cp(NL[:], CL[:].bitcast(F), *c_, scale=-1.0)
        o1 = pool.do(lambda e: e.memset(QA[:].bitcast(F), 1.0), hp_used)
        o2 = pool.do(lambda e: e.memset(KA[:].bitcast(F), 1.0), hp_used)
        augt = []
        for q, (dst, src, row) in enumerate([(QA, CH, 0), (QA, CL, 1), (KA, NH, 2), (KA, NL, 3)]):
            for g in range(2):
                augt.append(dma(sp, once(f"aug{q}{g}"), dst[row:row + 97:32, g, :].bitcast(F),
                                src[4 * g:4 * g + 4, :].bitcast(F), *c_, n1, n2, o1, o2))
        gemm_t("win_ag", 2, 8, 2, (HH, HL), ht, ev_ag, base=4, head=False)
        vb = [bank() for _ in range(4)]
        vt = []
        for c in range(2):
            wh, wl, wt = w_get("win_v")
            for b in range(4):
                for k in range(4):
                    kk = 4 * c + k
                    bs = slice(128 * b, 128 * b + 128)
                    mm3(vb[b][1][:], HH[:, kk, bs], HL[:, kk, bs], wh[:, 512 * k:512 * k + 512],
                        wl[:, 512 * k:512 * k + 512], kk == 0, kk == 7, vb[b][2], wt, ht)
                if c == 1:
                    free[vb[b][0]] = gain_split(vb[b][1][:], SM[:, 4 + b:5 + b], VH[:, b, :], VL[:, b, :], pe.mark(),
                                                hp_used, rr)
                    vt.append(free[vb[b][0]])
                run_taps(4 - 2 * c)
            w_release()
        qkt = []

        def ev_qk(n, ps, m):
            j = n // 2
            k, tm, tf = tmp()
            a = stt(tm[:], ps[:], 1.0 if n % 2 else 0.125, RS[:], ALU.mult, ALU.mult, m, rs, tf)
            hi, lo = (KH, KL) if n % 2 else (QH, QL)
            r = split(tm[:], hi[:, j, :], lo[:, j, :], a, hp_used)
            tfree[k] = r
            qkt.append(r)
            if n == 2:
                run_taps(3)
            return [a]

        qk = {"n": 0}

        def qk_tile():
            n = qk["n"]
            qk["n"] += 1
            if n >= 8:
                return
            if n % 2 == 0:
                qk["w"] = w_get("win_qk")
            wh, wl, wt = qk["w"]
            i, ps, fr = bank()
            for k in range(8):
                col = (2 * k + n % 2) * 128
                mm3(ps[:], wh[:, col:col + 128], wl[:, col:col + 128], HH[:, k, :], HL[:, k, :], k == 0, k == 7,
                    fr, wt, ht[k])
            free[i] = ev_qk(n, ps, pe.mark())
            if n % 2 == 1:
                w_release()

        PTH = sb("PTH", A + 97, [128, 1280], R)
        PTL = sb("PTL", A + 102, [128, 1280], R)

        def logits_softmax(i_, ps, nk, m, scale, Pt, slot, pfree):
            mx = SM[:, slot + i_:slot + i_ + 1]
            sm_ = SM[:, slot + 4 + i_:slot + 5 + i_]
            rc = SM[:, slot + 8 + i_:slot + 9 + i_]
            a = dve.do(lambda e: e.reduce_max(mx, ps[:, 0:nk], AX), m, pfree)
            b = ts(mx, mx, -scale, None, ALU.mult, None, a)
            c = act.do(lambda e: e.activation(Pt, ps[:, 0:nk], ACT.Exp, bias=mx, scale=scale, accum_out=sm_), b, pfree)
            d = dve.do(lambda e: e.reciprocal(rc, sm_), c)
            return c, d

        fx = {"p": [], "pv": []}
        cat = [None] * 8
        h_dead = []
        turned = []

        def fox_s(h):
            pb, j = 64 * (h % 2), h // 2
            ab, g = 32 * (h % 4), h // 4
            out = []
            for i_ in range(4):
                nk = 128 * (i_ + 1)
                bi, ps, fr = bank()
                qs = slice(128 * i_, 128 * i_ + 128)
                mm3(ps[:, 0:nk], QH[pb:pb + 64, j, qs], QL[pb:pb + 64, j, qs], KH[pb:pb + 64, j, 0:nk],
                    KL[pb:pb + 64, j, 0:nk], True, False, fr, qkt[2 * j], qkt[2 * j + 1])
                mm(ps[:, 0:nk], QA[ab:ab + 4, g, qs], KA[ab:ab + 4, g, 0:nk], False, False, augt)
                mm(ps[:, nk - 128:nk], IDR[:], MKR[:], False, True)
                c, d = logits_softmax(i_, ps, nk, pe.mark(), 1.0, PP[:, POFS[i_]:POFS[i_] + nk], 32 * (h % 2) + 160, fx["p"] + augt)
                free[bi] = [c]
                out.append((c, d))
            return out

        atd = [None]

        def fox_t(h, sm_):
            bl = []
            for j in range(4):
                bi, ps, fr = bank()
                for i_ in range(j, 4):
                    o = ps[:, 128 * i_:128 * i_ + 128]
                    src = PP[:, POFS[i_] + 128 * j:POFS[i_] + 128 * j + 128]
                    pe.do(lambda e, o=o, src=src: e.transpose(o, src, IDT[:]), fr, sm_[i_][0], inc=False)
                m = pe.mark()
                q = slice(TOFS[j] + 128 * j, TOFS[j] + 512)
                sp_ = split(ps[:, 128 * j:512], PTH[:, q], PTL[:, q], m, fx["pv"], hp_used)
                free[bi] = sp_
                bl.append(sp_)
            fx["p"] = [pe.mark()]
            return bl

        def fox_pv(h, bl, sm_):
            bi, ps, fr = bank()
            hs = slice(64 * h, 64 * h + 64)
            for i_ in range(4):
                for j in range(i_ + 1):
                    q = slice(TOFS[j] + 128 * i_, TOFS[j] + 128 * i_ + 128)
                    mm3(ps[:, 64 * i_:64 * i_ + 64], PTH[:, q], PTL[:, q], VH[:, j, hs], VL[:, j, hs],
                        j == 0, j == i_, fr, bl, vt)
            m = pe.mark()
            fx["pv"] = [m]
            slot = 32 * (h % 2) + 160 + 8
            o = []
            for i_ in range(4):
                dst = ATP[:, i_, 64 * (h % 2):64 * (h % 2) + 64]
                o.append(ts(dst, ps[:, 64 * i_:64 * i_ + 64], SM[:, slot + i_:slot + i_ + 1], None, ALU.mult, None,
                            m, sm_[i_][1], atd[0], augt))
            free[bi] = o
            if h % 2 == 0:
                fx["o"] = o
                return
            oo = fx["o"] + o

            def turn_pair():
                bi, ps, fr = bank()
                for i_ in range(4):
                    dst, src = ps[:, 128 * i_:128 * i_ + 128], ATP[:, i_, 0:128]
                    pe.do(lambda e, dst=dst, src=src: e.transpose(dst, src, IDT[:]), fr, oo, inc=False)
                atd[0] = pe.mark()
                j = h // 2
                sp_ = split(ps[:], QH[:, j, :], QL[:, j, :], atd[0])
                free[bi] = sp_
                cat[4 + j] = sp_

            later.append(turn_pair)

        MX = sb("MX", A + 24, [128, 8, 256])
        HMT = [sb(f"HM{i}", A + 48 + 8 * i, [128, 4, 256], R) for i in range(2)]
        HMH = [HMT[k // 4][:, k % 4, :] for k in range(8)]
        HML = sb("HML", A + 80, [128, 8, 256], R)
        KMH = sb("KMH", A + 52, [128, 4, 256], R)
        KML = sb("KML", A + 60, [128, 4, 256], R)
        VMH = sb("VMH", A + 64, [128, 2, 512], R)
        VML = sb("VML", A + 68, [128, 2, 512], R)
        QMH = sb("QMH", A + 32, [128, 4, 512], R)
        QML = sb("QML", A + 40, [128, 4, 512], R)
        PM = sb("PM", A + 88, [128, 4, 256])
        PMH = sb("PMH", A + 92, [128, 2, 512], R)
        PML = sb("PML", A + 96, [128, 2, 512], R)
        OMH = sb("OMH", A + 100, [128, 4, 512], R)
        OML = sb("OML", A + 108, [128, 4, 512], R)
        CO2 = sb("CO2", A + 16, [128, 4, 512])
        MSQ = sb("MSQ", A + 8, [128, 8, 256])
        ms = ColSum(1, 256)
        hmt = []
        kmt = []

        def mem_norm():
            k_dead = [pe.mark()]
            for k in range(8):
                q, tm, tf = tmp()
                a = stt(tm[:, 0:256], MX[:, k, :], par("g_memkv", k), RS[:, 0:256], ALU.mult, ALU.mult, mrs, tf)
                x1 = cp(HMH[k], tm[:, 0:256], a, conv_t, k_dead)
                x2 = pool.do(lambda e, k=k, tm=tm: e.tensor_tensor(HML[:, k, :], tm[:, 0:256], HMH[k].bitcast(F),
                                                                   ALU.subtract), x1, conv_t)
                tfree[q] = [x1, x2]
                hmt.append(tfree[q])

        def mem_k(c):
            wh, wl, wt = w_get("w_mk")
            for m_ in range(2):
                i, ps, fr = bank()
                for k in range(8):
                    col = (2 * k + m_) * 128
                    mm3(ps[:, 0:256], wh[:, col:col + 128], wl[:, col:col + 128], HMH[k], HML[:, k, :],
                        k == 0, k == 7, fr, wt, hmt[k])
                n = 2 * c + m_
                free[i] = split(ps[:, 0:256], KMH[:, n, :], KML[:, n, :], pe.mark())
                kmt.append(free[i])
            w_release()

        qk_tile()
        qk_tile()
        smx = fox_s(0)
        qk_tile()
        for h in range(8):
            bl = fox_t(h, smx)
            if h == 0:
                qk_tile()
            nxt = fox_s(h + 1) if h < 7 else None
            run_taps(10)
            run_later()
            if h == 5:
                cs = ColSum(4)
                for j in range(4):
                    cs.add(CO[:, j, :], conv_t[j])
                cd = diag(TMP[5], 8, S, cs.finish(1.0 / 512, None, 8), dg_used[0])
                ms.add(MSQ[:, 0, :], msum)
            if h == 6:
                cs = ColSum(4)
                for j in range(4):
                    cs.add(CO2[:, j, :], csq[j])
                c_ = cs.finish(1.0 / 512, "eps6", 16)
                cd = diag(TMP[5], 16, S, c_, dg_used[0])
                mi, ps, fr = bank(hold=True)
                mm(ps[:, 0:256], ONE[:], mdt[:, 0:256], True, True, fr, md)
                mm_ = pe.mark()
                tfree[mdk] = [mm_]
                tpend.discard(mdk)
                mrs = cp(RS[:, 0:256], ps[:, 0:256], mm_)
                give(mi, [mrs])
            if h == 7:
                for j in range(4):
                    a = af(CO[:, j, :], CO[:, j, :], ACT.Silu, xc[j], scale=par("cln_g", j), bias=par("cln_b", j))
                    cat[j] = split(CO[:, j, :], HH[:, j, :], HL[:, j, :], a, h_dead)
                mem_k(0)
            fox_pv(h, bl, smx)
            qk_tile()
            smx = nxt
            if h == 3:
                h_dead.append(pe.mark())
                k_m = dma(sp, once("mem"), MX[:], t["memt"], h_dead)
            if h == 4:
                msum = af(MSQ[:], MX[:], ACT.Square, k_m, h_dead)
                for q in (4, 2, 1):
                    msum = pool.do(lambda e, q=q: e.tensor_tensor(MSQ[:, 0:q, :], MSQ[:, 0:q, :], MSQ[:, q:2 * q, :],
                                                                  ALU.add), msum)
                run_taps(200)
            if h == 5:
                bi, mps, mtok = spread(8, S, None, d=cd)
                xc = [tt(CO[:, j, :], CO[:, j, :], mps[:], ALU.subtract, mtok) for j in range(4)]
                give(bi, xc)
                csq = []
                for j in range(4):
                    csq.append(af(CO2[:, j, :], CO[:, j, :], ACT.Square, xc[j], h_dead))
                m_ = ms.finish(1.0 / D, "eps6", 24)
                mdk, mdt, tf = tmp()
                tpend.add(mdk)
                md = diag(mdt, 24, 256, m_, tf)
                w_ahead()
            if h == 6:
                bi, mps, mtok = spread(16, S, None, d=cd)
                xc = [tt(CO[:, j, :], CO[:, j, :], mps[:], ALU.mult, mtok) for j in range(4)]
                give(bi, xc)
                mem_norm()
        mem_k(1)
        run_later()

        def cat_tile(k):
            return (HH[:, k, :], HL[:, k, :]) if k < 4 else (QH[:, k - 4, :], QL[:, k - 4, :])


        def y_evac(Y, ys, *w):
            toks = []

            def ev(n, ps, m):
                a = cp(Y[:, n, :], ps[:], m, *w)
                k, tm, tf = tmp()
                b = af(tm[:], ps[:], ACT.Square, m, tf)
                tpend.add(k)

                def add():
                    tfree[k] = [ys.add(tm, b)]
                    tpend.discard(k)

                later.append(add)
                toks.append([a])
                return [b]

            return ev, toks

        def post(Y, yt, ys, g, g2, *w):
            nonlocal xt
            r_ = ys.finish(1.0 / D, "eps6", 8)
            w_ahead()
            bi, rps, rtok = spread(8, S, r_)
            xn, hn = [], []
            st = ColSum(8)
            a = [None] * 8
            lo = [None] * 8

            def first(k):
                a[k] = stt(Y[:, k, :], Y[:, k, :], par(g, k), rps[:], ALU.mult, ALU.mult, rtok, yt[k])

            def second(k):
                if k < 2:
                    b = tt(X[:, k, :], X[:, k, :], Y[:, k, :], ALU.add, a[k], xt[k])
                else:
                    b = pool.do(lambda e: e.tensor_tensor(X[:, k, :], X[:, k, :], Y[:, k, :], ALU.add), a[k], xt[k])
                xn.append([b])
                hi = HH[:, k, :]
                if g2 is None:
                    c = cp(hi, X[:, k, :], b, *w)
                else:
                    c = act.do(lambda e: e.activation(hi, X[:, k, :], ACT.Identity, scale=par(g2, k)), b, *w)
                    q = af(Y[:, k, :], X[:, k, :], ACT.Square, b)
                    later.append(lambda: st.add(Y[:, k, :], q))
                lo[k] = c

            def third(k):
                if g2 is None:
                    d = tt(HL[:, k, :], X[:, k, :], HH[:, k, :].bitcast(F), ALU.subtract, lo[k])
                else:
                    d = stt(HL[:, k, :], X[:, k, :], par(g2, k), HH[:, k, :].bitcast(F), ALU.mult, ALU.subtract, lo[k])
                hn.append([lo[k], d])

            for k in range(10):
                if k < 8:
                    first(k)
                    second(k)
                if k >= 2:
                    third(k - 2)
            give(bi, [a[7]])
            xt = xn
            return hn, st

        Y1 = sb("Y1", A + 101, [128, 8, 512])
        att_done = [pe.mark()]
        ys = ColSum(8)
        ev, yt = y_evac(Y1, ys, att_done, xc)
        gemm_t("w_out", 4, 8, 2, cat_tile, cat, ev, lag=1)
        h_dead = [pe.mark()]
        ht, st = post(Y1, yt, ys, "g_mix_post", "g_mem_pre", h_dead)
        vb = [bank() for _ in range(2)]
        vmt = []
        for c in range(2):
            wh, wl, wt = w_get("w_mv")
            for b in range(2):
                for k in range(4):
                    kk = 4 * c + k
                    bs = slice(128 * b, 128 * b + 128)
                    mm3(vb[b][1][:], HMH[kk][:, bs], HML[:, kk, bs], wh[:, 512 * k:512 * k + 512],
                        wl[:, 512 * k:512 * k + 512], kk == 0, kk == 7, vb[b][2], wt, hmt)
                if c == 1:
                    free[vb[b][0]] = split(vb[b][1][:], VMH[:, b, :], VML[:, b, :], pe.mark(), att_done)
                    vmt.append(free[vb[b][0]])
            w_release()
        run_later()
        rr = st.finish(1.0 / D, "eps6", 0)
        rs = spread(0, S, rr, RS[:])
        qmt = []
        MS = float(128.0 ** -0.5)
        mfx = {"p": [], "pv": []}

        def ev_scaled(dsts):
            def ev(n, ps, m):
                k, tm, tf = tmp()
                a = tt(tm[:], ps[:], RS[:], ALU.mult, m, rs, tf)
                r = split(tm[:], dsts[0][:, n, :], dsts[1][:, n, :], a)
                tfree[k] = r
                qmt.append(r)
                return [a]
            return ev

        def mem_s(h):
            out = []
            for i_ in range(4):
                bi, ps, fr = bank()
                qs = slice(128 * i_, 128 * i_ + 128)
                mm3(ps[:, 0:256], QMH[:, h, qs], QML[:, h, qs], KMH[:, h, :], KML[:, h, :], True, True, fr,
                    qmt[h], kmt[h])
                slot = 32 * (h % 2) + 160
                c, d = logits_softmax(i_, ps, 256, pe.mark(), MS, PM[:, i_, :], slot, mfx["p"])
                free[bi] = [c]
                out.append([ts(PM[:, i_, :], PM[:, i_, :], SM[:, slot + 8 + i_:slot + 9 + i_], None, ALU.mult, None,
                               c, d)])
            return out

        def mem_t(h, sm_):
            bl = []
            for j in range(2):
                bi, ps, fr = bank()
                for i_ in range(4):
                    o, src = ps[:, 128 * i_:128 * i_ + 128], PM[:, i_, 128 * j:128 * j + 128]
                    pe.do(lambda e, o=o, src=src: e.transpose(o, src, IDT[:]), fr, sm_[i_], inc=False)
                sp_ = split(ps[:], PMH[:, j, :], PML[:, j, :], pe.mark(), mfx["pv"])
                free[bi] = sp_
                bl.append(sp_)
            mfx["p"] = [pe.mark()]
            return bl

        omt = []

        def mem_pv(h, bl):
            bi, ps, fr = bank()
            hs = slice(128 * h, 128 * h + 128)
            for j in range(2):
                mm3(ps[:], VMH[:, j, hs], VML[:, j, hs], PMH[:, j, :], PML[:, j, :], j == 0, j == 1, fr, bl, vmt)
            mfx["pv"] = [pe.mark()]
            free[bi] = split(ps[:], OMH[:, h, :], OML[:, h, :], mfx["pv"], xt)
            omt.append(free[bi])

        ev = ev_scaled((QMH, QML))
        mq = {}

        def mem_q(n):
            if n % 2 == 0:
                mq["w"] = w_get("w_mq")
            wh, wl, wt = mq["w"]
            i, ps, fr = bank()
            for k in range(8):
                col = (2 * k + n % 2) * 128
                mm3(ps[:], wh[:, col:col + 128], wl[:, col:col + 128], HH[:, k, :], HL[:, k, :], k == 0, k == 7,
                    fr, wt, ht[k])
            free[i] = ev(n, ps, pe.mark())
            if n % 2 == 1:
                w_release()

        mem_q(0)
        mem_q(1)
        smx = mem_s(0)
        mem_q(2)
        for h in range(4):
            bl = mem_t(h, smx)
            smx = mem_s(h + 1) if h < 3 else None
            if h == 0:
                mem_q(3)
            mem_pv(h, bl)
        h_dead = [pe.mark()]
        Y2 = sb("Y2", A + 32, [128, 8, 512])
        ys = ColSum(8)
        ev, yt = y_evac(Y2, ys, h_dead)
        gemm_t("w_mo", 2, 4, 4, (OMH, OML), omt, ev, lag=1)
        mo_dead = [pe.mark()]
        ht, st = post(Y2, yt, ys, "g_mem_post", "g_mlp_pre", h_dead)

        MID = sb("MID", A + 32, [128, 32, 512])
        MRH = [sb(f"MRH{i}", A + 96 + 2 * i, [128, 512], R) for i in range(5)]
        MRL = [sb(f"MRL{i}", A + 106 + 2 * i, [128, 512], R) for i in range(5)]
        mid = []
        mlp = {}

        def ev_up(n, ps, m):
            if n == 0:
                run_later()
                mlp["rr"] = st.finish(1.0 / D, "eps6", 0)
                mlp["rs"] = spread(0, S, mlp["rr"], RS[:])
                mlp["y"] = [pe.mark()]
            k, tm, tf = tmp()
            a = tt(tm[:], ps[:], RS[:], ALU.mult, m, mlp["rs"], tf)
            b = stt(MID[:, n, :], tm[:], 0.0, tm[:], ALU.max, ALU.mult, a, mlp["y"])
            tfree[k] = [b]
            mid.append([b])
            if n == 27:
                dpr.update(down_prep(32, MID, mid, mlp["y"]))
            if n >= 27 and n < 30:
                dpr["prep"](n - 27)
            return [a]


        def down_prep(n, src, toks, dead):
            d = {"used": [dead] * 5, "sps": []}

            def prep(k):
                if k < n:
                    d["sps"].append(split(src[:, k, :], MRH[k % 5][:], MRL[k % 5][:], toks[k], d["used"][k % 5]))

            d["prep"] = prep
            return d

        def down(name, nchunk, d, evac, lag=2):
            bs = [bank() for _ in range(8)]
            used, sps, prep = d["used"], d["sps"], d["prep"]

            def step(m_, k, kk, wh, wl, wt):
                col = kk * 1024 + 128 * m_
                mm3(bs[m_][1][:], wh[:, col:col + 128], wl[:, col:col + 128], MRH[k % 5][:], MRL[k % 5][:],
                    k == 0, k == 2 * nchunk - 1, bs[m_][2], wt, sps[k])

            for c in range(nchunk - 1):
                prep(2 * c + 3)
                wh, wl, wt = w_get(name)
                for kk in range(2):
                    k = 2 * c + kk
                    if kk:
                        prep(k + 3)
                    for m_ in range(8):
                        step(m_, k, kk, wh, wl, wt)
                    used[k % 5] = [pe.mark()]
                w_release()
            wh, wl, wt = w_get(name)
            for m_ in range(8):
                for kk in range(2):
                    step(m_, 2 * nchunk - 2 + kk, kk, wh, wl, wt)
                free[bs[m_][0]] = evac(m_, bs[m_][1], pe.mark())
                run_later(lag)
            w_release()
            run_later()

        dpr = {}
        gemm_t("w_up", 16, 8, 2, (HH, HL), ht, ev_up)
        h_dead = [pe.mark()]
        Y3 = sb("Y3", A + 32, [128, 8, 512])
        ys = ColSum(8)
        mid_use = {}

        def ev_mlp(n, ps, m):
            if n == 0:
                mid_use["ev"], mid_use["yt"] = y_evac(Y3, ys, m)
            return mid_use["ev"](n, ps, m)

        down("w_down", 16, dpr, ev_mlp)
        ht, st = post(Y3, mid_use["yt"], ys, "g_mlp_post", None, h_dead)
        down_dead = [pe.mark()]

        dn = {}

        def center(k):
            a = tt(X[:, k, :], X[:, k, :], dn["c"][0], ALU.subtract, dn["c"][1], xt[k])
            xt[k] = [a]
            q, tm, tf = tmp()
            s_ = af(tm[:], X[:, k, :], ACT.Square, a, tf)
            tpend.add(q)

            def add():
                dn["s"].add(X[:, k, :], a)
                tfree[q] = [dn["q"].add(tm, s_)]
                tpend.discard(q)

            later.append(add)

        def ev_deep(n, ps, m):
            a = stt(X[:, n, :], X[:, n, :], ALPHA, ps[:], ALU.mult, ALU.add, m, xt[n])
            xt[n] = [a]
            if n == 1:
                c = ColSum(1)
                c.add(X[:, 0, :], xt[0])
                r_ = c.finish(1.0 / 128, None, 8)
                dn["d"] = diag(TMP[5], 8, S, r_, dg_used[0])
            if n == 2:
                bi, cps, ctok = spread(8, S, None, d=dn["d"])
                dn["c"], dn["bank"] = (cps[:], ctok), bi
            if n == 3:
                dn["s"], dn["q"] = ColSum(8), ColSum(8)
            for k in {3: (0,), 4: (1, 2), 5: (3, 4), 6: (5, 6), 7: (7,)}.get(n, ()):
                center(k)
            return [a]

        def deep_norm(g, b, do_split=True, *w):
            nonlocal xt
            give(dn["bank"], [xt[7]])
            i1, p1, _ = dn["s"].bank
            i2, p2, _ = dn["q"].bank
            m = pe.mark()
            mu, rs_, va, sq = SM[:, 12:16], SM[:, 20:24], SM[:, 24:28], SM[:, 28:32]
            a1 = ts(mu, p1[:, 0:4], 1.0 / D, None, ALU.mult, None, m)
            give(i1, [a1])
            a2 = tt(sq, mu, mu, ALU.mult, a1)
            a2 = stt(va, p2[:, 0:4], 1.0 / D, sq, ALU.mult, ALU.subtract, a2, m)
            give(i2, [a2])
            a3 = af(va, va, ACT.Sqrt, a2, bias=par("eps5"))
            w_ahead()
            bj, mps, mtok = spread(8, S, a1)
            a3 = dve.do(lambda e: e.reciprocal(rs_, va), a3)
            q, tm, tf = tmp()
            d = diag(tm, 16, S, a3, tf)
            bi, rps, fr = bank(hold=True)
            mm(rps[:], ONE[:], tm[:], True, True, fr, d)
            rtok = pe.mark()
            tfree[q] = [rtok]
            xn, hn = [], []
            lo = [None] * 8
            last = None
            for k in range(10):
                if k < 8:
                    a = tt(X[:, k, :], X[:, k, :], mps[:], ALU.subtract, mtok)
                    a = last = tt(X[:, k, :], X[:, k, :], rps[:], ALU.mult, rtok, a)
                    xn.append([af(X[:, k, :], X[:, k, :], ACT.Identity, a, scale=par(g, k), bias=par(b, k))])
                    if do_split:
                        lo[k] = cp(HH[:, k, :], X[:, k, :], xn[k], *w)
                if k >= 1 and k < 9 and do_split:
                    j = k - 1
                    src, hi, lw = X[:, j, :], HH[:, j, :].bitcast(F), HL[:, j, :]
                    if j % 2:
                        z = tt(lw, src, hi, ALU.subtract, lo[j])
                    else:
                        z = pool.do(lambda e, lw=lw, src=src, hi=hi: e.tensor_tensor(lw, src, hi, ALU.subtract), lo[j])
                    hn.append([lo[j], z])
            give(bi, [last])
            give(bj, [last])
            xt = xn
            return hn

        def ffn(l, ht):
            cw = f"ffn_conv{l}"
            start = [pe.mark()]
            PADB = [sb(f"PAD{l}{i}", A + 76 + 2.25 * i, [128, 514]) for i in range(4)]
            zp = [pool.do(lambda e, q=q: e.memset(q[:, 0:1], 0.0), start) for q in PADB]
            zp += [pool.do(lambda e, q=q: e.memset(q[:, 513:514], 0.0), start) for q in PADB]
            pu = [None] * 4
            mid = []
            dp = down_prep(22, MID, mid, start)
            ab = {}

            def ev(n, ps, m):
                b = n % 4
                q = PADB[b]
                k, o, tf = tmp()
                j = n // 2 + (22 if n % 2 else 0)
                a = cp(q[:, 1:513], ps[:], m, pu[b], zp)
                c = ts(o[:], q[:, 0:512], par(cw, 3 * j), None, ALU.mult, None, a, tf)
                c = stt(o[:], q[:, 1:513], par(cw, 3 * j + 1), o[:], ALU.mult, ALU.add, c)
                c = stt(o[:], q[:, 2:514], par(cw, 3 * j + 2), o[:], ALU.mult, ALU.add, c)
                pu[b] = c
                if n % 2 == 0:
                    ab["k"], ab["o"], ab["c"] = k, o, c
                else:
                    s_ = af(o[:], o[:], ACT.Silu, c)
                    r = tt(MID[:, n // 2, :], ab["o"][:], o[:], ALU.mult, s_, ab["c"], start)
                    mid.append([r])
                    tfree[k] = tfree[ab["k"]] = [r]
                    if n in (35, 37, 39):
                        dp["prep"]((n - 35) // 2)
                return [a]

            gemm_t(f"up2_{l}", 22, 8, 2, (HH, HL), ht, ev)
            down(f"down2_{l}", 11, dp, ev_deep)

        CQF = sb("CQF", A + 60, [128, 6, 512])
        CQH = sb("CQH", A + 32, [128, 3, 512], R)
        CQL = sb("CQL", A + 38, [128, 3, 512], R)
        CVH = sb("CVH", A + 44, [128, 2, 512], R)
        CVL = sb("CVL", A + 48, [128, 2, 512], R)
        KRH = sb("KRH", A + 52, [128, 512], R)
        KRL = sb("KRL", A + 54, [128, 512], R)
        CS = sb("CS", A + 56, [128, 512])
        SN = sb("SN", A + 58, [128, 512])
        POSI = sb("POSI", A + 88, [128, 512], I32)
        ANG = sb("ANG", A + 90, [128, 512])
        AN2 = sb("AN2", A + 92, [128, 512])
        k_pos = dma(sp, once("pos"), POSI[:], t["pos"], down_dead)
        a = dve.do(lambda e: e.tensor_copy(ANG[:], POSI[:]), k_pos, ht, xt)
        a = ts(ANG[:], ANG[:], par("inv"), None, ALU.mult, None, a)
        s_, rd = sin_of(SN[:], ANG[:], 128, a)
        a = af(AN2[:], ANG[:], ACT.Abs, rd)
        c_ = af(CS[:], AN2[:], ACT.Sin, a, scale=-1.0, bias=par("halfpi"))
        s_ = ts(SN[:], SN[:], par("sgn"), None, ALU.mult, None, s_)
        tab = [s_, c_]
        cqt = []

        def rope(psA, psB, mA, mB, hi, lo, *w):
            k1, t1, f1 = tmp()
            k2, t2, f2 = tmp()
            a = tt(t1[:], psA, CS[:], ALU.mult, mA, tab, f1)
            b = tt(t2[:], psB, SN[:], ALU.mult, mB, tab, f2)
            c = tt(t1[:], t1[:], t2[:], ALU.add, a, b)
            r = split(t1[:], hi, lo, c, *w)
            tfree[k1], tfree[k2] = r, [c]
            return a, b, r

        krs = {}
        cqs, cvs = ColSum(3), ColSum(2)

        def norm3(gain, src, n, hi, lo, toks, sp_):
            bi, rps, rtok = sp_
            out = []
            for k in range(n):
                q, tm, tf = tmp()
                a = stt(tm[:], src[:, k, :], par(gain, k), rps[:], ALU.mult, ALU.mult, rtok, toks[k], tf)
                tfree[q] = split(tm[:], hi[:, k, :], lo[:, k, :], a)
                out.append(tfree[q])
            give(bi, [a])
            return out

        nq = {}

        def ev_in(n, ps, m):
            if n == 4:
                run_later()
                nq["d"] = diag(TMP[5], 8, S, cqs.finish(1.0 / 384, "eps6", 8), dg_used[0])
            if n == 5:
                nq["s"] = spread(8, S, None, d=nq["d"])
            if n < 5:
                a = cp(CQF[:, n, :], ps[:], m, xt)
                k, tm, tf = tmp()
                b = af(tm[:], ps[:], ACT.Square, m, tf)
                tpend.add(k)

                def add():
                    tfree[k] = [(cqs if n < 3 else cvs).add(tm, b)]
                    tpend.discard(k)

                later.append(add)
                cqt.append([a])
                return [b]
            a = cp(KRS[:], ps[:], m, tab)
            krs["a"] = a
            nq["q"] = norm3("g_q", CQF, 3, CQH, CQL, cqt, nq["s"])
            return [a]

        KRS = sb("KRS", A + 94, [128, 512])

        gemm_t("mla_in", 3, 8, 2, (HH, HL), ht, ev_in, lag=1)
        dv = diag(TMP[5], 16, S, cvs.finish(1.0 / 256, "eps6", 16), dg_used[0])
        cq = nq["q"]

        def ev_inx(n, ps, m):
            a, b, krs["t"] = rope(KRS[:], ps[:], krs["a"], m, KRH[:], KRL[:])
            return [b]

        gemm_t("mla_inx", 1, 8, 1, (HH, HL), ht, ev_inx)
        cv = norm3("g_kv", CQF[:, 3:5, :], 2, CVH, CVL, cqt[3:5], spread(16, S, None, d=dv))
        x_dead = [pe.mark()]
        QNH = sb("QNH", A + 60, [128, 2, 512], R)
        QNL = sb("QNL", A + 64, [128, 2, 512], R)
        QRH = sb("QRH", A + 68, [128, 512], R)
        QRL = sb("QRL", A + 70, [128, 512], R)
        KNH = sb("KNH", A + 72, [128, 2, 512], R)
        KNL = sb("KNL", A + 76, [128, 2, 512], R)
        V2H = sb("V2H", A + 80, [128, 4, 256], R)
        V2L = sb("V2L", A + 84, [128, 4, 256], R)
        PA = sb("PA", A + 88, [128, 4, 512])
        PAH = sb("PAH", A + 96, [128, 4, 512], R)
        PAL = sb("PAL", A + 104, [128, 4, 512], R)
        QRS = sb("QRS", A + 112, [128, 512])
        MLS = float(192.0 ** -0.5)
        lfx = {"p": [krs["t"], krs["a"]], "pv": [], "s": [cq, cv], "rope": []}
        omt = []

        def mla_s(h, pt):
            hh = h % 2
            pb = 64 * hh
            out = []
            for i_ in range(4):
                bi, ps, fr = bank()
                qs = slice(128 * i_, 128 * i_ + 128)
                mm3(ps[:], QNH[:, hh, qs], QNL[:, hh, qs], KNH[:, hh, :], KNL[:, hh, :], True, False, fr, pt)
                mm3(ps[:], QRH[pb:pb + 64, qs], QRL[pb:pb + 64, qs], KRH[pb:pb + 64, :], KRL[pb:pb + 64, :],
                    False, True, krs["t"])
                slot = 32 * hh + 160
                c, d = logits_softmax(i_, ps, 512, pe.mark(), MLS, PA[:, i_, :], slot, lfx["p"])
                free[bi] = [c]
                out.append([ts(PA[:, i_, :], PA[:, i_, :], SM[:, slot + 8 + i_:slot + 9 + i_], None, ALU.mult, None,
                               c, d)])
            return out

        def mla_t(h, sm_):
            bl = []
            for j in range(4):
                bi, ps, fr = bank()
                for i_ in range(4):
                    o, src = ps[:, 128 * i_:128 * i_ + 128], PA[:, i_, 128 * j:128 * j + 128]
                    pe.do(lambda e, o=o, src=src: e.transpose(o, src, IDT[:]), fr, sm_[i_], inc=False)
                sp_ = split(ps[:], PAH[:, j, :], PAL[:, j, :], pe.mark(), lfx["pv"])
                free[bi] = sp_
                bl.append(sp_)
            lfx["p"] = [pe.mark()]
            return bl

        def mla_pv(h, bl, pt):
            bi, ps, fr = bank()
            hs = slice(128 * (h % 2), 128 * (h % 2) + 128)
            for j in range(4):
                mm3(ps[:], V2H[:, j, hs], V2L[:, j, hs], PAH[:, j, :], PAL[:, j, :], j == 0, j == 3, fr, bl, pt)
            lfx["pv"] = [pe.mark()]
            free[bi] = split(ps[:], HH[:, h, :], HL[:, h, :], lfx["pv"], x_dead)
            omt.append(free[bi])

        pr = {}

        def mla_uq(p):
            wh, wl, wt = w_get("uq")
            pr["pt"] = pt = []
            for m_ in (0, 1, 2, 3):
                bi, ps, fr = bank()
                for k in range(3):
                    col = (k * 4 + m_) * 128
                    mm3(ps[:], wh[:, col:col + 128], wl[:, col:col + 128], CQH[:, k, :], CQL[:, k, :], k == 0, k == 2,
                        fr, wt, cq)
                m = pe.mark()
                if m_ < 2:
                    free[bi] = split(ps[:], QNH[:, m_, :], QNL[:, m_, :], m, lfx["s"])
                    pt.append(free[bi])
                elif m_ == 2:
                    cpa = cp(QRS[:], ps[:], m, lfx["rope"])
                    free[bi] = [cpa]
                else:
                    a, b, r = rope(QRS[:], ps[:], cpa, m, QRH[:], QRL[:], lfx["s"])
                    free[bi] = [b]
                    lfx["rope"] = r
                    pt.append(r)
            w_release()

        def mla_k():
            wh, wl, wt = pr["w"] = w_get("ukv")
            for m_ in range(2):
                bi, ps, fr = bank()
                for k in range(2):
                    col = k * 512 + m_ * 128
                    mm3(ps[:], wh[:, col:col + 128], wl[:, col:col + 128], CVH[:, k, :], CVL[:, k, :], k == 0, k == 1,
                        fr, wt, cv)
                free[bi] = split(ps[:], KNH[:, m_, :], KNL[:, m_, :], pe.mark(), lfx["s"])
                pr["pt"].append(free[bi])

        def mla_v():
            wh, wl, wt = pr["w"]
            pr["vp"] = []
            for b in range(4):
                bi, ps, fr = bank()
                bs = slice(128 * b, 128 * b + 128)
                for k in range(2):
                    col = k * 512 + 256
                    mm3(ps[:, 0:256], CVH[:, k, bs], CVL[:, k, bs], wh[:, col:col + 256], wl[:, col:col + 256],
                        k == 0, k == 1, fr, wt, cv)
                free[bi] = split(ps[:, 0:256], V2H[:, b, :], V2L[:, b, :], pe.mark(), lfx["pv"], cq, cv)
                pr["vp"].append(free[bi])
            w_release()

        mla_uq(0)
        mla_k()
        smx = mla_s(0, pr["pt"])
        mla_v()
        for p in range(4):
            bl = mla_t(2 * p, smx)
            smx = mla_s(2 * p + 1, pr["pt"])
            lfx["s"] = [pe.mark()]
            mla_pv(2 * p, bl, pr["vp"])
            if p < 3:
                mla_uq(p + 1)
                mla_k()
            bl = mla_t(2 * p + 1, smx)
            if p < 3:
                smx = mla_s(2 * p + 2, pr["pt"])
            mla_pv(2 * p + 1, bl, pr["vp"])
            if p < 3:
                mla_v()
        gemm_t("mla_o", 4, 8, 2, (HH, HL), omt, ev_deep, lag=1)
        ht = deep_norm("ln1_g0", "ln1_b0", True, [pe.mark()])
        ffn(0, ht)

        ht = deep_norm("ln2_g0", "ln2_b0", True, [pe.mark()])
        h_dead = [pe.mark()]
        XD = t["xd"]
        s_x = dma(sp, once("xs"), XD, X[:], xt)
        stores.append(s_x)
        VG = [sb(f"VG{i}", A + 32 + 16 * i, [128, 8, 512]) for i in range(3)]
        PADH = [sb(f"PADH{i}", A + 112 + 2.25 * i, [128, 514]) for i in range(2)]
        zp = [pool.do(lambda e, q=q: e.memset(q[:, 0:1], 0.0), h_dead) for q in PADH]
        zp += [pool.do(lambda e, q=q: e.memset(q[:, 513:514], 0.0), h_dead) for q in PADH]
        hyu = [None] * 2
        vg = [[None] * 8 for _ in range(3)]
        AT = [A + 80, A]
        ZHS = [sb(f"ZH{o}", AT[o], [128, 4, 1024], R) for o in range(2)]
        ZLS = [sb(f"ZL{o}", AT[o] + 16, [128, 4, 1024], R) for o in range(2)]
        YFS = [sb(f"YF{o}", AT[1 - o], [128, 8, 1024]) for o in range(2)]
        KB = [sb(f"KB{i}", 8 * i, [128, 2048]) for i in range(2)]
        YHS = [[sb(f"YH{o}{i}", AT[o] + 8 * i if i else 32, [128, 1024], R) for i in range(4)] for o in range(2)]
        YLS = [[sb(f"YL{o}{i}", AT[o] + 8 * i + 4 if i else 36, [128, 1024], R) for i in range(4)] for o in range(2)]
        ch_k = [chan("c_k0"), chan("c_k1")]
        ch_kx = chan("c_kx")
        zst = {"t": [], "dead": [h_dead]}
        zfold = [[None] * 8 for _ in range(2)]

        def z_turn(o, j, toks):
            k, tm, tf = tmp()
            a, b = VG[0][:, j, 0:256], VG[0][:, j, 256:512]
            x = pool.do(lambda e: e.tensor_tensor(tm[:, 0:256], a, b, ALU.add), toks[j], tf)
            y = pool.do(lambda e: e.tensor_tensor(tm[:, 256:512], a, b, ALU.subtract), toks[j], tf)
            zfold[o][j] = [x, y]
            tpend.add(k)

            def turn_z():
                bi, ps, fr = bank()
                for tb in range(4):
                    dst, src = ps[:, 128 * tb:128 * tb + 128], tm[:, 128 * tb:128 * tb + 128]
                    pe.do(lambda e, dst=dst, src=src: e.transpose(dst, src, IDT[:]), fr, x, y, inc=False)
                m = pe.mark()
                tfree[k] = [m]
                tpend.discard(k)
                cs_ = slice(128 * j, 128 * j + 128)
                p3 = ps[:].rearrange("p (a c) -> p a c", a=4)
                free[bi] = split(p3, ZHS[o][:, :, cs_], ZLS[o][:, :, cs_], m, zst["dead"])
                zst["t"].append(free[bi])

            later.append(turn_z)

        def ev_hy(n, ps, m):
            b = n % 2
            q = PADH[b]
            g, j = n // 8, n % 8
            o = VG[g][:, j, :]
            kt_, y, tf = tmp()
            a = cp(q[:, 1:513], ps[:], m, hyu[b], zp)
            c = ts(y[:], q[:, 0:512], par("w_short", 3 * n), None, ALU.mult, None, a, tf)
            c = stt(y[:], q[:, 1:513], par("w_short", 3 * n + 1), y[:], ALU.mult, ALU.add, c)
            w2 = par("w_short", 3 * n + 2)
            c1 = stt(o[:, 0:256], q[:, 2:258], w2, y[:, 0:256], ALU.mult, ALU.add, c, h_dead)
            c2 = stt(o[:, 511:255:-1], q[:, 258:514], w2, y[:, 256:512], ALU.mult, ALU.add, c, h_dead)
            hyu[b] = c2
            tfree[kt_] = [c2]
            vg[g][j] = [c1, c2]
            if n >= 10 and n < 18:
                z_turn(0, n - 10, vg[0])
            return [a]

        gemm_t("hy_in", 12, 8, 2, (HH, HL), ht, ev_hy, lag=1)
        x_dead = [pe.mark()]
        kbu = [[s_x], [s_x]]
        kx_done = [hyu[0], hyu[1]]
        KX = sb("KX", A + 112, [128, 1024])
        z_tok = vg[0]
        yf_free = [x_dead] * 8
        inv_used = [x_dead]
        HYH = sb("HYH", A + 80, [128, 8, 512], R)
        HYL = sb("HYL", A + 96, [128, 8, 512], R)
        ht = []

        def hy_split(k):
            v1, v2 = VG[0][:, k, 0:256], VG[0][:, k, 511:255:-1]
            h1, h2 = HYH[:, k, 0:256], HYH[:, k, 256:512]
            l1, l2 = HYL[:, k, 0:256], HYL[:, k, 256:512]
            a1 = cp(h1, v1, res[k], sps)
            a2 = cp(h2, v2, res[k], sps)
            b1 = tt(l1, v1, h1.bitcast(F), ALU.subtract, a1, a2)
            b2 = tt(l2, v2, h2.bitcast(F), ALU.subtract, a2)
            ht.append([a1, a2, b1, b2])

        for o in range(2):
            zt = zst["t"]
            ZH, ZL, YF, YH, YL = ZHS[o], ZLS[o], YFS[o], YHS[o], YLS[o]
            yft = [None] * 8
            kxl = dma(sp, ch_kx, KX[:], KD[o, 8], kd_done, kx_done)
            wh, wl, wt = w_get("dft_z")
            used = [inv_used[0]] + [None] * 3
            sps = []

            def prep(k):
                if k < 8:
                    sps.append(split(YF[:, k, :], YH[k % 4][:], YL[k % 4][:], yft[k], used[k % 4]))

            for m_ in range(4):
                kl = dma(sp, ch_k[m_ % 2], KB[m_ % 2][:].rearrange("p (a c) -> p a c", a=2),
                         KD[o, 2 * m_:2 * m_ + 2].rearrange("a p c -> p a c"), kbu[m_ % 2], kd_done, s_x)
                bk = []
                for part in range(2):
                    for c in range(2):
                        bi, ps, fr = bank()
                        odd = 2 * (part ^ (m_ // 2))
                        for kt in range(2):
                            col = kt * 1024 + 256 * m_ + 128 * part
                            csl = slice(512 * c, 512 * c + 512)
                            mm3(ps[:], wh[:, col:col + 128], wl[:, col:col + 128], ZH[:, odd + kt, csl],
                                ZL[:, odd + kt, csl], kt == 0, kt == 1, fr, wt, zt)
                        bk.append((bi, ps, pe.mark()))
                ku = []
                for c in range(2):
                    csl = slice(512 * c, 512 * c + 512)
                    (br, pr, mr), (bi_, pi, mi) = bk[c], bk[2 + c]
                    kr = KB[m_ % 2][:, 512 * c:512 * c + 512]
                    ki = KB[m_ % 2][:, 1024 + 512 * c:1536 + 512 * c]
                    kr2, kr2t = kr, None
                    if m_ == 0:
                        kr2, kr2t = KX[:, csl], kxl
                    q1, q2, q3, q4 = tmp(), tmp(), tmp(), tmp()
                    a1 = tt(q1[1][:], pr[:], kr, ALU.mult, mr, kl, q1[2])
                    a2 = tt(q2[1][:], pi[:], ki, ALU.mult, mi, kl, q2[2])
                    b1 = tt(q3[1][:], pr[:], ki, ALU.mult, q3[2])
                    b2 = tt(q4[1][:], pi[:], kr2, ALU.mult, kr2t, q4[2])
                    yr, yi = YF[:, 2 * m_, csl], YF[:, 2 * m_ + 1, csl]
                    a3 = pool.do(lambda e, y=yr, q1=q1, q2=q2: e.tensor_tensor(y, q1[1][:], q2[1][:], ALU.subtract),
                                 a1, a2, yf_free[2 * m_])
                    b3 = pool.do(lambda e, y=yi, q3=q3, q4=q4: e.tensor_tensor(y, q3[1][:], q4[1][:], ALU.add),
                                 b1, b2, yf_free[2 * m_ + 1])
                    tfree[q1[0]] = tfree[q2[0]] = [a3]
                    tfree[q3[0]] = tfree[q4[0]] = [b3]
                    if m_ == 0:
                        kx_done.append(b2)
                    free[br], free[bi_] = [b1], [b2]
                    ku.append(b2)
                    yft[2 * m_] = (yft[2 * m_] or []) + [a3]
                    yft[2 * m_ + 1] = (yft[2 * m_ + 1] or []) + [b3]
                kbu[m_ % 2] = ku
                if m_ == 1:
                    prep(0)
            w_release()
            fwd_done = [pe.mark()]
            bs = [bank() for _ in range(8)]
            for q in range(1, 4):
                used[q] = fwd_done
            gate = VG[1 + o]
            res = []
            def istep(m_, k, wh, wl, wt):
                f_ = k
                part, mf = f_ % 2, f_ // 2
                half = part ^ (mf // 2)
                cs_ = slice(128 * m_, 128 * m_ + 128)
                col = 256 * (4 * part + mf)
                ps = bs[m_][1][:, 256 * half:256 * half + 256]
                l, h, w1, w2 = YL[k % 4][:, cs_], YH[k % 4][:, cs_], wh[:, col:col + 256], wl[:, col:col + 256]
                for x, y, st, sp_ in ((l, w1, k == 0, False), (h, w2, False, False), (h, w1, False, k == 7)):
                    pe.do(lambda e, ps=ps, x=x, y=y, st=st, sp_=sp_: e.matmul(ps, x, y, start=st, stop=sp_,
                                                                              skip_group_check=True),
                          bs[m_][2], wt, sps[k], inc=False)

            for k in range(1, 4):
                prep(k)
            wh, wl, wt = w_get("dft_i")
            for k in range(4):
                for m_ in range(8):
                    istep(m_, k, wh, wl, wt)
                used[k % 4] = [pe.mark()]
                prep(k + 4)
            if o == 0:
                zst = {"t": [], "dead": list(sps)}
            for m_ in range(8):
                for k in range(4, 8):
                    istep(m_, k, wh, wl, wt)
                ps, db, m = bs[m_][1], par("d_bias", 8 * o + m_), pe.mark()
                v1, v2 = VG[0][:, m_, 0:256], VG[0][:, m_, 256:512]
                a1 = stt(v1, v1, db, ps[:, 0:256], ALU.mult, ALU.add, m, z_tok[m_], zfold[o][m_])
                a2 = stt(v2, v2, db, ps[:, 0:256], ALU.mult, ALU.add, m, z_tok[m_], zfold[o][m_])
                a1 = tt(v1, v1, ps[:, 256:512], ALU.add, a1)
                a2 = tt(v2, v2, ps[:, 256:512], ALU.subtract, a2)
                vm, gm = VG[0][:, m_, :], gate[:, m_, :]
                if m_ % 2:
                    b = pool.do(lambda e, vm=vm, gm=gm: e.tensor_tensor(vm, vm, gm, ALU.mult), a1, a2, vg[1 + o][m_])
                else:
                    b = tt(vm, vm, gm, ALU.mult, a1, a2, vg[1 + o][m_])
                free[bs[m_][0]] = [a2]
                res.append([b])
                if o == 0:
                    z_turn(1, m_, res)
                    run_later(2)
                elif m_ >= 2:
                    hy_split(m_ - 2)
            w_release()
            run_later()
            z_tok = res
            yf_free = [[pe.mark()]] * 8
            inv_used = [[pe.mark()]]
        inv_done = [pe.mark()]
        k_x = dma(sp, once("xl"), X[:], XD, kbu)
        xt = [[k_x] for _ in range(8)]
        hy_split(6)
        hy_split(7)
        gemm_t("hy_o", 4, 8, 2, (HYH, HYL), ht, ev_deep, lag=1)
        ht = deep_norm("ln1_g1", "ln1_b1", True, [pe.mark()])
        ffn(1, ht)
        deep_norm("ln2_g1", "ln2_b1", False)
        for k in range(8):
            stores.append(dma(sp, once(f"out{k}"), t["out"][:, k, :], X[:, k, :], xt[k]))
        assert wst["get"] == len(CHUNKS)
        sp.ops.append([lambda e: None, tokens(stores), None])

        block = es.enter_context(nc.Block())

        @block.sync
        def _(e):
            sp.issue(e)

        @block.gpsimd
        def _(e):
            pool.issue(e)

        @block.scalar
        def _(e):
            act.issue(e)

        @block.vector
        def _(e):
            dve.issue(e)

        @block.tensor
        def _(e):
            pe.issue(e)


def layout(v):
    f32 = np.float32
    o = {}

    def cut(w, kt, mt):
        K, M = w.shape
        n = M // (128 * mt)
        return np.ascontiguousarray(w.reshape(kt, 128, n, mt * 128).transpose(2, 1, 0, 3).reshape(n, 128, -1))

    def rows(w, kk):
        K, N = w.shape
        return np.ascontiguousarray(w.reshape(K // (128 * kk), kk, 128, N).transpose(0, 2, 1, 3).reshape(-1, 128, kk * N))

    def pairs(a, b):
        K = a.shape[0]
        return np.stack([a.reshape(K, -1, 128), b.reshape(K, -1, 128)], 2).reshape(K, -1)

    w_in = v["w_in"][0]
    o["win_ag"] = cut(pairs(w_in[:, 512:1024], w_in[:, 0:512]), 8, 2)
    o["win_qk"] = cut(pairs(w_in[:, 1024:1536], w_in[:, 1536:2048]), 8, 2)
    o["win_v"] = rows(w_in[:, 2048:2560], 4)
    o["win_f"] = rows(w_in[:, 2560:2568], 8)
    o["w_out"] = cut(v["w_out"][0], 8, 2)
    o["w_mk"] = cut(v["w_mk"][0], 8, 2)
    o["w_mv"] = rows(v["w_mv"][0], 4)
    o["w_mq"] = cut(v["w_mq"][0], 8, 2)
    o["w_mo"] = cut(v["w_mo"][0], 4, 4)
    o["w_up"] = cut(v["w_up"][0], 8, 2)
    o["w_down"] = rows(v["w_down"][0], 2)
    mi = v["mla_w_in_2"][0]
    kr = mi[:, 640:704]
    sw = np.concatenate([kr[:, 32:64], kr[:, 0:32]], 1)
    o["mla_in"] = cut(np.concatenate([mi[:, 0:640], kr, kr], 1), 8, 2)
    o["mla_inx"] = cut(np.concatenate([sw, sw], 1), 8, 1)
    uq = v["mla_w_uq_2"][0].reshape(384, 8, 192)
    qn, q1, q2 = uq[:, :, 0:128], uq[:, :, 128:160], uq[:, :, 160:192]
    qr = np.concatenate([q1, q2], 2)
    qs = np.concatenate([q2, q1], 2)
    uqp = np.concatenate([qn.reshape(384, 4, 256), qr.reshape(384, 4, 128), qs.reshape(384, 4, 128)], 2)
    o["uq"] = cut(uqp.reshape(384, 2048), 3, 4)
    ukv = v["mla_w_ukv_2"][0].reshape(256, 4, 2, 256)
    ukp = np.concatenate([ukv[..., 0:128].reshape(256, 4, 256), ukv[..., 128:256].reshape(256, 4, 256)], 2)
    o["ukv"] = cut(ukp.reshape(256, 2048), 2, 4)
    o["mla_o"] = cut(v["mla_w_o_2"][0], 8, 2)
    o["hy_in"] = cut(v["hy_w_in_2"][0], 8, 2)
    o["hy_o"] = cut(v["hy_w_o_2"][0], 8, 2)
    for l in range(2):
        up = v["ffn_w_up_2"][l]
        o[f"up2_{l}"] = cut(pairs(up[:, 0:2816], up[:, 2816:5632]), 8, 2)
        o[f"down2_{l}"] = rows(v["ffn_w_down_2"][l], 2)
    tt_ = np.arange(512)
    fq = np.concatenate([np.arange(0, 512, 2), np.arange(1, 512, 2)])
    ph = (np.outer(tt_, fq) % 1024) * (2 * np.pi / 1024)
    cr, si = np.cos(ph), -np.sin(ph)
    alt = (-1.0) ** tt_
    crx = cr[:, 0:128].copy()
    crx[:, 0] = alt
    o["dft_c"] = cut(cr.astype(f32), 4, 4)
    o["dft_s"] = cut(si.astype(f32), 4, 4)
    o["dft_kx"] = cut(crx.astype(f32), 4, 1)
    ph = (np.outer(2 * tt_[0:256] + 1, fq) % 2048) * (2 * np.pi / 2048)
    cr, si = np.cos(ph), -np.sin(ph)
    si[:, 0] = alt[0:256]
    o["dft_z"] = cut(pairs(cr, si).astype(f32), 2, 8)
    wgt = np.full((512, 1), 2.0 / 1024)
    wgt[0] = 1.0 / 1024
    o["dft_i"] = rows(np.concatenate([cr.T * wgt, si.T * wgt], 0).astype(f32), 8)
    ln = np.linspace(0.0, 1.0, 512, dtype=f32)[:, None]
    w = (2.0 * np.pi * np.arange(512)[:, None] / 512).astype(f32)
    fr = np.linspace(1e-4, 15, 16, dtype=f32)[None]
    o["zfeat"] = np.ascontiguousarray(np.concatenate([ln, np.cos(fr * w), -np.sin(fr * w)], 1).T.astype(f32))
    dl = np.abs(np.linspace(np.log(0.3) / 1e-2, np.log(1.5) / 1e-2, 1024, dtype=f32))
    o["decay"] = np.ascontiguousarray(np.exp(-ln * dl).astype(f32).reshape(4, 128, 1024).transpose(1, 0, 2))
    o["fw_out"] = np.ascontiguousarray(v["hy_fw_out_2"][0])
    fs = np.zeros((64, 256), f32)
    fs[0:33, 0:64] = v["hy_fw1_2"][0]
    fs[:, 64:128] = v["hy_fw2_2"][0]
    fs[:, 128:192] = v["hy_fw3_2"][0]
    for i, n in enumerate(("hy_fb1_2", "hy_fb2_2", "hy_fb3_2", "hy_freq_2")):
        fs[:, 192 + i] = v[n][0]
    o["fsmall"] = fs

    def feat(x):
        return np.ascontiguousarray(x.T.reshape(8, 128, -1).transpose(1, 0, 2))

    o["xt"] = feat(v["x"][0])
    o["memt"] = feat(v["mem"][0])
    o["pos"] = np.ascontiguousarray(np.broadcast_to(v["positions_2"], (128, 512)))
    i_, j_ = np.arange(128)[:, None], np.arange(128)[None]
    o["consts"] = np.concatenate([np.eye(128), np.where(j_ <= i_, 0.0, -1e30), (i_ <= j_) * 1.0,
                                  np.ones((128, 384))], 1).astype(f32)
    p = np.zeros((128, NPC), f32)

    def put(name, x):
        c = x.reshape(-1, 128).T
        p[:, POFF[name]:POFF[name] + c.shape[1]] = c

    for n, k in (("g_mix_pre", "norm_mix_pre"), ("g_mix_post", "norm_mix_post"), ("g_mem_pre", "norm_mem_pre"),
                 ("g_mem_post", "norm_mem_post"), ("g_memkv", "norm_memkv"), ("g_mlp_pre", "norm_mlp_pre"),
                 ("g_mlp_post", "norm_mlp_post"), ("conv_b", "conv_b"), ("cln_g", "conv_ln_g"),
                 ("cln_b", "conv_ln_b"), ("g_q", "mla_g_q_2"), ("g_kv", "mla_g_kv_2"), ("d_bias", "hy_d_bias_2")):
        put(n, v[k])
    put("conv_w", np.ascontiguousarray(v["conv_w"][0].reshape(31, 4, 128).transpose(1, 0, 2)))
    put("w_short", np.ascontiguousarray(v["hy_w_short_2"][0].reshape(3, 24, 128).transpose(1, 0, 2)))
    for l in range(2):
        put(f"ffn_conv{l}", np.ascontiguousarray(v["ffn_w_conv_2"][l].reshape(3, 44, 128).transpose(1, 0, 2)))
        for n in ("ln1_g", "ln1_b", "ln2_g", "ln2_b"):
            put(f"{n}{l}", v[f"{n}_2"][l])
    p[:, POFF["b_forget"]:POFF["b_forget"] + 8] = v["b_forget"]
    inv = (1.0 / (np.float32(10000.0) ** (np.arange(0, 64, 2, dtype=f32) / np.float32(64)))).astype(f32)
    p[:, POFF["inv"]] = np.tile(inv, 4)
    p[:, POFF["sgn"]] = np.where(np.arange(128) % 64 < 32, -1.0, 1.0)
    p[:, POFF["one"]] = 1.0
    p[:, POFF["eps6"]] = 1e-6
    p[:, POFF["eps5"]] = 1e-5
    p[:, POFF["halfpi"]] = HALF_PI
    o["par"] = p
    return o


def kernel(**inputs):
    import concourse.bacc as _bacc
    from concourse.bass_utils import run_bass_kernel_spmd as _run

    arrays = layout({k: np.asarray(a) for k, a in inputs.items()})
    nc = _bacc.Bacc("TRN2", target_bir_lowering=False, num_devices=1)
    t = {}
    for name, a in arrays.items():
        t[name] = nc.dram_tensor(f"in_{name}", a.shape, mybir.dt.from_np(a.dtype), kind="ExternalInput").ap()
    t["out"] = nc.dram_tensor("out_0", (128, 8, 512), F, kind="ExternalOutput").ap()
    t["kd"] = nc.dram_tensor("kd", (2, 9, 128, 1024), F, kind="Internal").ap()
    t["xd"] = nc.dram_tensor("xd", (128, 8, 512), F, kind="Internal").ap()
    build(nc, t)
    r = _run(nc, [{f"in_{n}": a for n, a in arrays.items()}], core_ids=[0])
    got = np.asarray(r.results[0]["out_0"])
    return np.ascontiguousarray(got.transpose(1, 0, 2).reshape(1024, 512).T)[None]
```
